# Optimizing a Trainium2 kernel written in Bass

```python
import jax, jax.numpy as jnp
from jax import lax
import numpy as np

D_MODEL = 1024
BATCH = 1
SEQ = 1024
DEPTH = 2

GRID_W = 64
CTX_LEN = 256
EPS = 1e-6
NEG_INF = -1e30
HEAD_DIM = 64
N_Q_HEADS = 8
N_KV_HEADS = 2
Q_PER_KV = N_Q_HEADS // N_KV_HEADS
ATTN_WIDTH = N_Q_HEADS * HEAD_DIM
KV_WIDTH = N_KV_HEADS * HEAD_DIM
WINDOW = 128
BLOCK = 128
ROPE_BASE = 10000.0
CONV_B_WIDTH = D_MODEL // 2
CONV_B_GROUPS = 8
CONV_B_K = 3
CONV_B_LEFT = 1
EVEN_SPLITS = (ATTN_WIDTH, ATTN_WIDTH + KV_WIDTH, ATTN_WIDTH + 2 * KV_WIDTH,
               ATTN_WIDTH + 2 * KV_WIDTH + CONV_B_WIDTH, ATTN_WIDTH + 2 * KV_WIDTH + 2 * CONV_B_WIDTH)
EVEN_IN = ATTN_WIDTH + 2 * KV_WIDTH + 3 * CONV_B_WIDTH
EVEN_OUT = ATTN_WIDTH + CONV_B_WIDTH
LRU_WIDTH = D_MODEL
LRU_HEADS = 8
LRU_BLOCK = LRU_WIDTH // LRU_HEADS
LRU_C = 8.0
LRU_CONV_K = 4
LRU_CONV_LEFT = 2
N_EXPERTS = 16
CAPACITY_FACTOR = 2
EXPERT_FF = 1408
N_EVEN = (DEPTH + 1) // 2
N_ODD = DEPTH // 2

kernel_name = "hybrid_swa_shortconv_rglru_ecmoe_dit"

def rmsnorm(x, g):
    xf = x.astype(jnp.float32)
    y = xf * lax.rsqrt(jnp.mean(xf * xf, axis=-1, keepdims=True) + EPS)
    return (y * g.astype(jnp.float32)).astype(x.dtype)

def modulate(h, shift, scale):
    return h * (1.0 + scale) + shift

def axial_rope(x, rows, cols):
    dh = x.shape[-1]
    half = dh // 2
    nf = half // 2
    inv = ROPE_BASE ** (-jnp.arange(nf, dtype=jnp.float32) / nf)
    out = []
    for part, pos in ((x[..., :half], rows), (x[..., half:], cols)):
        ang = pos.astype(jnp.float32)[:, None] * inv[None, :]
        cos = jnp.cos(ang)[None, :, None, :]
        sin = jnp.sin(ang)[None, :, None, :]
        p1 = part[..., :nf].astype(jnp.float32)
        p2 = part[..., nf:].astype(jnp.float32)
        out += [p1 * cos - p2 * sin, p2 * cos + p1 * sin]
    return jnp.concatenate(out, axis=-1).astype(x.dtype)

def dwconv(u, w, bias, left):
    k_w = w.shape[0]
    n = u.shape[1]
    up = jnp.pad(u, ((0, 0), (left, k_w - 1 - left), (0, 0)))
    return sum(w[k] * up[:, k:k + n] for k in range(k_w)) + bias

def sink_logits(sink, shape):
    return jnp.broadcast_to(sink.astype(jnp.float32).reshape(1, N_KV_HEADS, Q_PER_KV, *([1] * (len(shape) - 3))), shape)

def windowed_gqa_with_context(q, k, v, kc, vc, sink):
    b, n, hk, g, dh = q.shape
    nb = n // BLOCK
    scale = dh ** -0.5
    qb = q.reshape(b, nb, BLOCK, hk, g, dh)
    pad = ((0, 0), (BLOCK, BLOCK), (0, 0), (0, 0))
    kp = jnp.pad(k, pad).reshape(b, nb + 2, BLOCK, hk, dh)
    vp = jnp.pad(v, pad).reshape(b, nb + 2, BLOCK, hk, dh)
    kb = jnp.concatenate([kp[:, :-2], kp[:, 1:-1], kp[:, 2:]], axis=2)
    vb = jnp.concatenate([vp[:, :-2], vp[:, 1:-1], vp[:, 2:]], axis=2)
    s_loc = jnp.einsum('bnqkgd,bnjkd->bkgnqj', qb, kb).astype(jnp.float32) * scale
    qpos = jnp.arange(nb)[:, None] * BLOCK + jnp.arange(BLOCK)[None, :]
    kpos = jnp.arange(nb)[:, None] * BLOCK - BLOCK + jnp.arange(3 * BLOCK)[None, :]
    diff = kpos[:, None, :] - qpos[:, :, None]
    valid = (jnp.abs(diff) <= WINDOW) & (kpos[:, None, :] >= 0) & (kpos[:, None, :] < n)
    s_loc = jnp.where(valid, s_loc, NEG_INF)
    s_ctx = jnp.einsum('bnqkgd,bjkd->bkgnqj', qb, kc).astype(jnp.float32) * scale
    s_snk = sink_logits(sink, s_loc.shape[:-1] + (1,))
    p = jax.nn.softmax(jnp.concatenate([s_loc, s_ctx, s_snk], axis=-1), axis=-1)
    n_loc = 3 * BLOCK
    n_ctx = kc.shape[1]
    p_loc = p[..., :n_loc].astype(v.dtype)
    p_ctx = p[..., n_loc:n_loc + n_ctx].astype(v.dtype)
    o = (jnp.einsum('bkgnqj,bnjkd->bnqkgd', p_loc, vb)
         + jnp.einsum('bkgnqj,bjkd->bnqkgd', p_ctx, vc))
    return o.reshape(b, n, hk * g * dh)

def context_attention(qc, kc, vc, sink):
    b, L, hk, g, dh = qc.shape
    s = jnp.einsum('bqkgd,bjkd->bkgqj', qc, kc).astype(jnp.float32) * dh ** -0.5
    s_snk = sink_logits(sink, s.shape[:-1] + (1,))
    p = jax.nn.softmax(jnp.concatenate([s, s_snk], axis=-1), axis=-1)
    o = jnp.einsum('bkgqj,bjkd->bqkgd', p[..., :L].astype(vc.dtype), vc)
    return o.reshape(b, L, hk * g * dh)

def gated_short_conv(gb, gc, u, w, bias):
    return gb * dwconv(gc * u, w, bias, CONV_B_LEFT)

def even_mixer(hl, hc, rows, cols, w_in, w_out, sink, conv_w, conv_b, need_ctx_out):
    def project(h):
        b, n = h.shape[:2]
        q, k, v, gb, gc, u = jnp.split(h @ w_in, EVEN_SPLITS, axis=-1)
        return (q.reshape(b, n, N_Q_HEADS, HEAD_DIM), k.reshape(b, n, N_KV_HEADS, HEAD_DIM),
                v.reshape(b, n, N_KV_HEADS, HEAD_DIM), gb, gc, u)
    b, n = hl.shape[:2]
    ql, kl, vl, bl, cl, ul = project(hl)
    qc, kc, vc, bc, cc, uc = project(hc)
    ql = axial_rope(ql, rows, cols).reshape(b, n, N_KV_HEADS, Q_PER_KV, HEAD_DIM)
    kl = axial_rope(kl, rows, cols)
    att_l = windowed_gqa_with_context(ql, kl, vl, kc, vc, sink)
    conv_l = gated_short_conv(bl, cl, ul, conv_w, conv_b)
    yl = jnp.concatenate([att_l, conv_l], axis=-1) @ w_out
    if not need_ctx_out:
        return yl, None
    L = hc.shape[1]
    att_c = context_attention(qc.reshape(b, L, N_KV_HEADS, Q_PER_KV, HEAD_DIM), kc, vc, sink)
    conv_c = gated_short_conv(bc, cc, uc, conv_w, conv_b)
    yc = jnp.concatenate([att_c, conv_c], axis=-1) @ w_out
    return yl, yc

def rglru_coeffs(u, wa, ba, wx, bx, lam):
    b, n, w = u.shape
    ub = u.reshape(b, n, LRU_HEADS, LRU_BLOCK)
    r = jax.nn.sigmoid(jnp.einsum('bnhi,hij->bnhj', ub, wa.astype(jnp.float32)).reshape(b, n, w) + ba.astype(jnp.float32))
    i = jax.nn.sigmoid(jnp.einsum('bnhi,hij->bnhj', ub, wx.astype(jnp.float32)).reshape(b, n, w) + bx.astype(jnp.float32))
    log_a = -LRU_C * r * jax.nn.softplus(-lam.astype(jnp.float32))
    a = jnp.exp(log_a)
    mult = jnp.sqrt(-jnp.expm1(2.0 * log_a))
    return a, mult * (i * u)

def linear_scan(a, b, reverse):
    def combine(e1, e2):
        a1, b1 = e1
        a2, b2 = e2
        return a1 * a2, a2 * b1 + b2
    return lax.associative_scan(combine, (a, b), reverse=reverse, axis=1)[1]

def odd_mixer(hl, hc, w_in, w_out, conv_w, conv_b, wa, ba, wx, bx, lam, need_ctx_out):
    gl, ul = jnp.split(hl @ w_in, 2, axis=-1)
    gc, uc = jnp.split(hc @ w_in, 2, axis=-1)
    ul = dwconv(ul, conv_w, conv_b, LRU_CONV_LEFT).astype(jnp.float32)
    uc = dwconv(uc, conv_w, conv_b, LRU_CONV_LEFT).astype(jnp.float32)
    hs_l, hs_c = [], []
    for d, reverse in ((0, False), (1, True)):
        a_c, b_c = rglru_coeffs(uc, wa[d], ba[d], wx[d], bx[d], lam[d])
        h_c = linear_scan(a_c, b_c, reverse)
        end = 0 if reverse else -1
        h0 = h_c[:, 0] if reverse else h_c[:, -1]
        a_l, b_l = rglru_coeffs(ul, wa[d], ba[d], wx[d], bx[d], lam[d])
        b_l = b_l.at[:, -1 if reverse else 0].add(a_l[:, -1 if reverse else 0] * h0)
        hs_l.append(linear_scan(a_l, b_l, reverse))
        hs_c.append(h_c)
    yl = (jax.nn.gelu(gl) * (hs_l[0] + hs_l[1]).astype(gl.dtype)) @ w_out
    if not need_ctx_out:
        return yl, None
    yc = (jax.nn.gelu(gc) * (hs_c[0] + hs_c[1]).astype(gc.dtype)) @ w_out
    return yl, yc

def expert_choice_ffn(h, router_w, w_gate, w_up, w_down):
    b, n, d = h.shape
    cap = max(1, CAPACITY_FACTOR * n // N_EXPERTS)
    aff = jax.nn.softmax((h @ router_w).astype(jnp.float32), axis=-1)
    g, idx = lax.top_k(jnp.swapaxes(aff, 1, 2), cap)
    flat = (jnp.arange(b)[:, None, None] * n + idx).reshape(-1)
    hf = h.reshape(b * n, d)
    xe = hf[flat].reshape(b, N_EXPERTS, cap, d)
    a = jnp.einsum('becd,edf->becf', xe, w_gate)
    u = jnp.einsum('becd,edf->becf', xe, w_up)
    y = jnp.einsum('becf,efd->becd', jax.nn.silu(a) * u, w_down)
    y = y * g[..., None].astype(y.dtype)
    out = jnp.zeros((b * n, d), y.dtype).at[flat].add(y.reshape(-1, d))
    return out.reshape(b, n, d)

def setup_inputs(seed: int = 0) -> dict:
    key = jax.random.key(seed)
    ks = jax.random.split(key, 32)
    f32 = jnp.float32
    D = D_MODEL

    def nrm(k, shape, s):
        return jax.random.normal(k, shape, f32) * s

    u = jax.random.uniform(ks[22], (N_ODD, 2, LRU_WIDTH), f32, 0.9, 0.999)
    s = u ** (1.0 / LRU_C)
    lam = jnp.log(s) - jnp.log1p(-s)
    return {
        "x": nrm(ks[0], (BATCH, SEQ, D), 1.0),
        "c": nrm(ks[1], (BATCH, D), 1.0),
        "ctx": nrm(ks[2], (BATCH, CTX_LEN, D), 1.0),
        "c_ctx": nrm(ks[3], (D,), 1.0),
        "ada_w": nrm(ks[4], (DEPTH, D, 6 * D), 0.02),
        "ada_b": nrm(ks[5], (DEPTH, 6 * D), 0.01),
        "norm_mix_g": 1.0 + nrm(ks[6], (DEPTH, D), 0.02),
        "norm_ffn_g": 1.0 + nrm(ks[7], (DEPTH, D), 0.02),
        "ev_w_in": nrm(ks[8], (N_EVEN, D, EVEN_IN), D ** -0.5),
        "ev_w_out": nrm(ks[9], (N_EVEN, EVEN_OUT, D), EVEN_OUT ** -0.5),
        "ev_sink": nrm(ks[10], (N_EVEN, N_Q_HEADS), 0.5),
        "ev_conv_w": nrm(ks[11], (N_EVEN, CONV_B_K, CONV_B_WIDTH), CONV_B_K ** -0.5),
        "ev_conv_b": nrm(ks[12], (N_EVEN, CONV_B_WIDTH), 0.01),
        "od_w_in": nrm(ks[13], (N_ODD, D, 2 * LRU_WIDTH), D ** -0.5),
        "od_w_out": nrm(ks[14], (N_ODD, LRU_WIDTH, D), LRU_WIDTH ** -0.5),
        "od_conv_w": nrm(ks[15], (N_ODD, LRU_CONV_K, LRU_WIDTH), LRU_CONV_K ** -0.5),
        "od_conv_b": nrm(ks[16], (N_ODD, LRU_WIDTH), 0.01),
        "od_wa": nrm(ks[17], (N_ODD, 2, LRU_HEADS, LRU_BLOCK, LRU_BLOCK), LRU_BLOCK ** -0.5),
        "od_ba": nrm(ks[18], (N_ODD, 2, LRU_WIDTH), 0.01),
        "od_wx": nrm(ks[19], (N_ODD, 2, LRU_HEADS, LRU_BLOCK, LRU_BLOCK), LRU_BLOCK ** -0.5),
        "od_bx": nrm(ks[20], (N_ODD, 2, LRU_WIDTH), 0.01),
        "od_lambda": lam,
        "router_w": nrm(ks[23], (DEPTH, D, N_EXPERTS), D ** -0.5),
        "w_gate": nrm(ks[24], (DEPTH, N_EXPERTS, D, EXPERT_FF), D ** -0.5),
        "w_up": nrm(ks[25], (DEPTH, N_EXPERTS, D, EXPERT_FF), D ** -0.5),
        "w_down": nrm(ks[26], (DEPTH, N_EXPERTS, EXPERT_FF, D), EXPERT_FF ** -0.5),
        "final_g": 1.0 + nrm(ks[27], (D,), 0.02),
    }

def reference(x, c, ctx, c_ctx, ada_w, ada_b, norm_mix_g, norm_ffn_g, ev_w_in, ev_w_out, ev_sink,
              ev_conv_w, ev_conv_b, od_w_in, od_w_out, od_conv_w, od_conv_b, od_wa, od_ba, od_wx, od_bx,
              od_lambda, router_w, w_gate, w_up, w_down, final_g):
    n = x.shape[1]
    n_rows = n // GRID_W
    rows = jnp.broadcast_to(jnp.arange(n_rows)[:, None], (n_rows, GRID_W)).reshape(-1)
    cols = jnp.broadcast_to(jnp.arange(GRID_W)[None, :], (n_rows, GRID_W)).reshape(-1)
    s_lat = jax.nn.silu(c)
    s_ctx = jax.nn.silu(c_ctx)[None, :]
    xl, xc = x, ctx
    for l in range(DEPTH):
        last = l == DEPTH - 1
        m_l = [m[:, None, :] for m in jnp.split(s_lat @ ada_w[l] + ada_b[l], 6, axis=-1)]
        m_c = [m[:, None, :] for m in jnp.split(s_ctx @ ada_w[l] + ada_b[l], 6, axis=-1)]
        hl = modulate(rmsnorm(xl, norm_mix_g[l]), m_l[0], m_l[1])
        hc = modulate(rmsnorm(xc, norm_mix_g[l]), m_c[0], m_c[1])
        j = l // 2
        if l % 2 == 0:
            yl, yc = even_mixer(hl, hc, rows, cols, ev_w_in[j], ev_w_out[j], ev_sink[j],
                                ev_conv_w[j], ev_conv_b[j], not last)
        else:
            yl, yc = odd_mixer(hl, hc, od_w_in[j], od_w_out[j], od_conv_w[j], od_conv_b[j],
                               od_wa[j], od_ba[j], od_wx[j], od_bx[j], od_lambda[j], not last)
        xl = xl + m_l[2] * yl
        if not last:
            xc = xc + m_c[2] * yc
        hl = modulate(rmsnorm(xl, norm_ffn_g[l]), m_l[3], m_l[4])
        xl = xl + m_l[5] * expert_choice_ffn(hl, router_w[l], w_gate[l], w_up[l], w_down[l])
        if not last:
            hc = modulate(rmsnorm(xc, norm_ffn_g[l]), m_c[3], m_c[4])
            xc = xc + m_c[5] * expert_choice_ffn(hc, router_w[l], w_gate[l], w_up[l], w_down[l])
    return rmsnorm(xl, final_g)


_drawn_inputs = setup_inputs


def setup_inputs(seed=0):
    import zlib

    import numpy as np

    out = dict(_drawn_inputs(seed))
    spreads = {}
    factors = {'norm_ffn_g': 5.539,
     'ev_sink': 8.0,
     'ev_conv_b': 8.0,
     'od_conv_b': 2.739,
     'od_ba': 64.0,
     'od_bx': 50.196,
     'final_g': 10.11}
    for name, (base, spread) in spreads.items():
        noise = np.random.default_rng([zlib.crc32(name.encode()), seed]).standard_normal(out[name].shape)
        drawn = base * np.exp(spread * noise) if base else spread * noise
        out[name] = __import__('jax').numpy.asarray(drawn.astype(out[name].dtype))
    for name, factor in factors.items():
        out[name] = (out[name] * factor).astype(out[name].dtype)
    return out
```

```python
from contextlib import ExitStack, contextmanager

import numpy as np

import concourse.bass as bass
from concourse import mybir

F32 = mybir.dt.float32
U32 = mybir.dt.uint32
ALU = mybir.AluOpType
ACT = mybir.ActivationFunctionType
AX_X = mybir.AxisListType.X

P = 128
D = 1024
K = D // P
SEQ = 1024
CTX = 256
TOK = SEQ + CTX
LT = SEQ // P
NT = TOK // P
EPS = 1e-6
DH = 64
NKV = 2
QPK = 4
GRID_W = 64
NE = 16
FF = 1408
FJ = FF // P
CAP = 2 * SEQ // NE
CAPC = 2 * CTX // NE
NEG = -1e30
CB = D // 2 // P
BANK = 512
CHUNKS = [(0, 512), (512, 512), (SEQ, CTX)]

C_COND, C_GMIX, C_GFFN = 0, 16, 32
C_EVW, C_EVB, C_ODW, C_ODB = 48, 60, 64, 96
C_BA, C_BX, C_LAM, C_ALL = 104, 120, 136, 152


class Memory:

    def __init__(self, nc, ctx):
        sb = lambda name, shape, dt=F32: ctx.enter_context(nc.sbuf_tensor(name, shape, dt))
        self.ring = sb("ring", [P, 18 * D])
        self.big = sb("big", [P, 28 * D])
        self.cols = sb("cols", [P, C_ALL])
        self.ident = sb("ident_sb", [P, P])
        self.rope = sb("rope_sb", [P, 2, SEQ])
        self.mask = sb("mask_sb", [P, 5 * P])
        self.mod = sb("mod", [P, 2, 6, K, 2])
        self.comb = sb("comb", [P, 2, 2, K, 2])
        self.sink = sb("sink_sb", [P, 8])
        self.idx = sb("idx", [P, NE + 1], U32)
        self.idxc = sb("idxc", [P, NE + 1], U32)
        self.gate = sb("gate", [P, NE])
        self.gatec = sb("gatec", [P, NE])
        self.ps = ctx.enter_context(nc.psum_tensor("ps", [P, 8, BANK], F32))
        self.A = self.big[:, 0:10 * D]
        self.B = self.big[:, 10 * D:20 * D]
        self.C = self.big[:, 20 * D:28 * D]


@contextmanager
def stage_of(nc):
    with ExitStack() as ctx:
        ctx.taken = []
        ctx.callback(nc.all_engine_barrier)
        ctx.callback(lambda: nc.clear_and_free_semaphores(ctx.taken))
        yield ctx


def semaphore(nc, ctx, name):
    ctx.taken.append(nc.alloc_semaphore(name))
    return ctx.taken[-1]


def semaphores(nc, ctx, names):
    return [semaphore(nc, ctx, n) for n in names.split()]


def ada_stage(nc, m, d):
    UNITS, SLOTS = 24, 4
    with stage_of(nc) as ctx:
        cols_in, bias_in, silu_done, mm_done, row_done, turned, stored0, stored1, col_done = semaphores(
            nc, ctx, "a_cols a_bias a_silu a_mm a_row a_turn a_st0 a_st1 a_col")
        stored = [stored0, stored1]
        unit_in = [semaphore(nc, ctx, f"a_unit{i}") for i in range(SLOTS)]
        comb_step = semaphores(nc, ctx, "a_comb")[0]
        consts_in = semaphores(nc, ctx, "a_consts")[0]
        w = m.ring[:, 0:SLOTS * 4 * D].rearrange("p (s k n) -> p s k n", s=SLOTS, k=K)
        bias = m.A[0:2, 0:10 * D]
        bias2 = m.B[0:2, 0:2 * D]
        row = m.C[0:2, 0:2 * BANK].rearrange("p (b n) -> p b n", b=2)
        cond = m.C[:, 4 * BANK:4 * BANK + 2 * K]
        modc = m.mod[:, :, :, :, :].rearrange("p l j k s -> p (l j k) s")
        block = ctx.enter_context(nc.Block())

        @block.sync
        def _(sp):
            sp.dma_start(m.cols[:, :], d["cols"]).then_inc(cols_in, 16)
            flat = d["ada_b"].rearrange("(o l) n -> o (l n)", o=1)
            sp.dma_start(bias, flat[:, 0:10 * D].to_broadcast((2, 10 * D))).then_inc(bias_in, 16)
            sp.dma_start(bias2, flat[:, 10 * D:12 * D].to_broadcast((2, 2 * D))).then_inc(bias_in, 16)
            with sp.Fori(0, UNITS // SLOTS) as i:
                for s in range(SLOTS):
                    sp.wait_ge(mm_done, i * SLOTS + s + 1)
                    sp.dma_start(w[:, s, :, :], d["ada_w"][i * SLOTS + s]).then_inc(unit_in[s], 16)

        @block.scalar
        def _(act):
            act.dma_start(m.ident[:, :], d["ident"]).then_inc(consts_in, 16)
            act.dma_start(m.rope[:, :, :], d["rope"]).then_inc(consts_in, 16)
            act.dma_start(m.mask[:, :], d["mask"]).then_inc(consts_in, 16)
            act.dma_start(m.sink[:, :], d["ev_sink"].to_broadcast((P, 8))).then_inc(consts_in, 16)
            act.wait_ge(cols_in, 16)
            act.activation(cond, m.cols[:, C_COND:C_COND + 2 * K], ACT.Silu).then_inc(silu_done, 1)
            with act.Fori(0, UNITS // 2) as i:
                for b in range(2):
                    act.wait_ge(row_done, 2 * i + b + 1)
                    act.dma_start(d["mrow"][:, bass.ds((2 * i + b) * BANK, BANK)], row[:, b, :]).then_inc(stored[b], 16)
            for b in range(2):
                act.wait_ge(stored[b], 16 * UNITS // 2)
            act.wait_ge(consts_in, 64)

        @block.tensor
        def _(pe):
            pe.wait_ge(silu_done, 1)
            pe.wait_ge(consts_in, 64)
            pe.nop().then_inc(mm_done, SLOTS)

            def product(i, u):
                n = i * SLOTS + u
                pe.wait_ge(unit_in[u], 16 * i + 16)
                for k in range(K):
                    mm = pe.matmul(m.ps[0:2, u % 2, :], cond[:, 2 * k:2 * k + 2], w[:, u, k, :],
                                   start=(k == 0), stop=(k == K - 1))
                mm.then_inc(mm_done, 1)

            def turn(n, b):
                pe.wait_ge(row_done, n + 1)
                for q in range(4):
                    mm = pe.matmul(m.ps[:, 2 + b, 2 * q:2 * q + 2], row[:, b, q * P:(q + 1) * P],
                                   m.ident[0:2, 0:2], start=True, stop=True)
                mm.then_inc(turned, 1)

            with pe.Fori(0, UNITS // SLOTS) as i:
                for u in range(SLOTS):
                    product(i, u)
                    turn(i * SLOTS + u, u % 2)

        @block.vector
        def _(dve):
            dve.wait_ge(bias_in, 32)

            def unit(n, b, bias_ap, first):
                dve.wait_ge(mm_done, n + 1 + SLOTS)
                if not first:
                    dve.wait_ge(stored[b], (n - b) * 8)
                    dve.wait_ge(turned, n - 1)
                dve.tensor_tensor(row[:, b, :], m.ps[0:2, b, :], bias_ap, ALU.add).then_inc(row_done, 1)
                dve.wait_ge(turned, n + 1)
                dve.tensor_copy(modc[:, bass.ds(n * 4, 4), :],
                                m.ps[:, 2 + b, 0:8].rearrange("p (q s) -> p q s", s=2)).then_inc(col_done, 1)

            for b in range(2):
                unit(b, b, bias[:, b * BANK:(b + 1) * BANK], True)
            with dve.Fori(1, 10) as i:
                for b in range(2):
                    unit(2 * i + b, b, bias[:, bass.ds(i * D + b * BANK, BANK)], False)
            for n in range(20, 24):
                unit(n, n % 2, bias2[:, (n - 20) * BANK:(n - 19) * BANK], False)
            dve.wait_ge(col_done, UNITS)
            step = 0
            for l in range(2):
                for part, gain in ((1, C_GMIX), (4, C_GFFN)):
                    g = m.cols[:, gain + K * l:gain + K * (l + 1)]
                    for s in range(2):
                        out = m.comb[:, l, part // 4, :, s]
                        dve.scalar_tensor_tensor(out, m.mod[:, l, part, :, s], 1.0, g, ALU.add, ALU.mult).then_inc(
                            comb_step, 1)


def norm_stage(nc, m, name, layer, sources, hT):
    with stage_of(nc) as ctx:
        sq, ms_done, sd_done, rs_done, xn_done, turned, ev_act, ev_dve = semaphores(
            nc, ctx, " ".join(f"{name}_{x}" for x in "sq ms sd rs xn turn eva evd".split()))
        x_in = [semaphore(nc, ctx, f"{name}_x{b}") for b in range(2)]
        xt = m.B[:, 0:2 * D].rearrange("p (b n) -> p b n", b=2)
        xn = m.B[:, 2 * D:4 * D].rearrange("p (b n) -> p b n", b=2)
        junk = m.B[:, 4 * D:5 * D]
        st = m.B[:, 5 * D:5 * D + 8]
        block = ctx.enter_context(nc.Block())

        def tiles(engine, body):
            base = 0
            for src, first, n, s in sources:
                if n > 2:
                    with engine.Fori(0, n // 2) as i:
                        for b in range(2):
                            body(i * 2 + b + base, i, src, first + (i * 2 + b) * P, s, b)
                else:
                    for b in range(2):
                        body(base + b, base // 2, src, first + b * P, s, b)
                base += n

        @block.sync
        def _(sp):
            def load(t, half, src, row, s, b):
                sp.wait_ge(xn_done, t + 1)
                sp.dma_start(xt[:, b, :], src[bass.ds(row, P), :]).then_inc(x_in[b], 16)
            tiles(sp, load)

        @block.scalar
        def _(act):
            act.nop().then_inc(ev_act, 2)

            def tile(t, half, src, row, s, b):
                act.wait_ge(x_in[b], 16 * half + 16)
                act.activation(junk, xt[:, b, :], ACT.Square, accum_out=st[:, b:b + 1]).then_inc(sq, 1)
                act.wait_ge(ms_done, t + 1)
                act.activation(st[:, 4 + b:5 + b], st[:, 2 + b:3 + b], ACT.Sqrt).then_inc(sd_done, 1)
                act.wait_ge(turned, t + 3)
                for k in range(4):
                    last = act.activation(hT[:, k, bass.ds(t * P, P)], m.ps[:, 2 * b, k * P:(k + 1) * P],
                                          ACT.Identity, bias=m.mod[:, layer, 0, k, s:s + 1],
                                          scale=m.comb[:, layer, 0, k, s:s + 1])
                last.then_inc(ev_act, 1)
            tiles(act, tile)

        @block.vector
        def _(dve):
            dve.nop().then_inc(xn_done, 2)
            dve.nop().then_inc(ev_dve, 2)

            def tile(t, half, src, row, s, b):
                dve.wait_ge(sq, t + 1)
                dve.tensor_scalar(st[:, 2 + b:3 + b], st[:, b:b + 1], 1.0 / D, EPS, ALU.mult, ALU.add).then_inc(ms_done, 1)
                dve.wait_ge(sd_done, t + 1)
                dve.reciprocal(st[:, 6 + b:7 + b], st[:, 4 + b:5 + b]).then_inc(rs_done, 1)
                dve.wait_ge(rs_done, t + 1)
                dve.wait_ge(turned, t + 1)
                dve.tensor_scalar(xn[:, b, :], xt[:, b, :], st[:, 6 + b:7 + b], None, ALU.mult).then_inc(xn_done, 1)
                dve.wait_ge(turned, t + 3)
                for k in range(4, 8):
                    last = dve.tensor_scalar(hT[:, k, bass.ds(t * P, P)], m.ps[:, 2 * b + 1, (k - 4) * P:(k - 3) * P],
                                             m.comb[:, layer, 0, k, s:s + 1], m.mod[:, layer, 0, k, s:s + 1],
                                             ALU.mult, ALU.add)
                last.then_inc(ev_dve, 1)
            tiles(dve, tile)

        @block.tensor
        def _(pe):
            pe.nop().then_inc(turned, 2)

            def tile(t, half, src, row, s, b):
                pe.wait_ge(xn_done, t + 3)
                pe.wait_ge(ev_act, t + 1)
                pe.wait_ge(ev_dve, t + 1)
                for k in range(K):
                    mm = pe.transpose(m.ps[:, 2 * b + k // 4, (k % 4) * P:(k % 4 + 1) * P],
                                      xn[:, b, k * P:(k + 1) * P], m.ident[:, :])
                mm.then_inc(turned, 1)
            tiles(pe, tile)


class Banks:

    def __init__(self, nc, ctx, name, plan, n, first=0):
        self.n, self.first = n, first
        self.at = {key: i for i, key in enumerate(plan)}
        assert len(self.at) == len(plan)
        self.free = [semaphore(nc, ctx, f"{name}_bank{b}") for b in range(n)]
        self.done = semaphore(nc, ctx, f"{name}_mm")

    def bank(self, key):
        return self.first + self.at[key] % self.n

    def sem(self, key):
        return self.free[self.at[key] % self.n]

    def uses(self, key):
        return self.at[key] // self.n

    def number(self, key):
        return self.at[key] + 1


def even_in_stage(nc, m, d):
    hT = m.A.rearrange("p (k t) -> p k t", k=K)
    cat = m.B.rearrange("p (k t) -> p k t", k=K)
    q = m.C[:, 0:4 * TOK].rearrange("p (j t) -> p j t", j=4)
    kk = m.C[:, 4 * TOK:5 * TOK]
    v = m.C[:, 5 * TOK:6 * TOK].rearrange("p (t c) -> p t c", t=NT)
    tmp = m.C[:, 6 * TOK:6 * TOK + BANK]
    gcb = m.B[:, 0:TOK]
    WP = TOK + 4
    prod = m.B[:, TOK:TOK + WP]
    acc = m.B[:, TOK + WP:TOK + WP + TOK + 2]
    at = 2 * TOK + WP + 2
    qraw = m.B[:, at:at + 2 * BANK].rearrange("p (b n) -> p b n", b=2)
    w = m.ring[:, :].rearrange("p (s k n) -> p s k n", s=18, k=K)
    slot = lambda kind, c: {"qk": c, "v": 5, "gc": 6 + 3 * c, "u": 7 + 3 * c, "gb": 8 + 3 * c}[kind]
    place = lambda c0: c0 + 1 if c0 < SEQ else c0 + 3
    after = lambda c0: c0 if c0 < SEQ else c0 + 2

    plan = []
    for j in range(5):
        plan += [("qk", j, 0), ("qk", j, 1), ("rot", j, 0), ("qk", j, 2), ("rot", j, 1)]
    plan += [("v", t, 0) for t in range(NT)]
    for c in range(CB):
        plan += [(kind, c, ch) for kind in ("gc", "u", "gb") for ch in range(3)]

    with stage_of(nc) as ctx:
        banks = Banks(nc, ctx, "ei", plan, 6)
        w_in = [semaphore(nc, ctx, f"ei_w{g}") for g in range(6)]
        rot_in, qraw_ready, roped, gc_ready, prod_done, chain = semaphores(
            nc, ctx, "ei_rot ei_qraw ei_roped ei_gc ei_prod ei_chain")
        block = ctx.enter_context(nc.Block())

        @block.sync
        def _(sp):
            for g in range(6):
                sp.dma_start(m.ring[:, 3 * D * g:3 * D * (g + 1)], d["ev_in"][g]).then_inc(w_in[g], 16)
            sp.dma_start(m.B[:, 4900:4900 + P], d["rot"]).then_inc(rot_in, 16)

        rot = m.B[:, 4900:4900 + P]

        @block.tensor
        def _(pe):
            seen = set()
            for key in plan:
                kind, c, ch = key
                if banks.uses(key):
                    pe.wait_ge(banks.sem(key), banks.uses(key))
                bank = m.ps[:, banks.bank(key), :]
                if kind == "rot":
                    if not seen & {"rot"}:
                        pe.wait_ge(rot_in, 16)
                        seen.add("rot")
                    pe.wait_ge(qraw_ready, 2 * c + ch + 1)
                    pe.matmul(bank, rot, qraw[:, ch, :], start=True, stop=True).then_inc(banks.done, 1)
                    continue
                g = slot(kind, c) // 3
                if g not in seen:
                    pe.wait_ge(w_in[g], 16)
                    seen.add(g)
                for k in range(K):
                    if kind == "v":
                        mm = pe.matmul(bank[:, 0:P], hT[:, k, c * P:(c + 1) * P], w[:, 5, k, :],
                                       start=(k == 0), stop=(k == K - 1))
                    else:
                        t0, n = CHUNKS[ch]
                        mm = pe.matmul(bank[:, 0:n], w[:, slot(kind, c), k, :], hT[:, k, t0:t0 + n],
                                       start=(k == 0), stop=(k == K - 1))
                mm.then_inc(banks.done, 1)

        @block.scalar
        def _(act):
            for key in plan:
                kind, c, ch = key
                if kind not in ("qk", "v", "gc"):
                    continue
                t0, n = CHUNKS[ch]
                src = m.ps[:, banks.bank(key), 0:n]
                act.wait_ge(banks.done, banks.number(key))
                if kind == "v":
                    act.copy(v[:, c, :], src[:, 0:P]).then_inc(banks.sem(key), 1)
                elif kind == "gc":
                    if c and ch == 0:
                        act.wait_ge(prod_done, 3 * c)
                    act.copy(gcb[:, t0:t0 + n], src).then_inc(banks.sem(key), 1)
                    if ch == 2:
                        act.wait_ge(banks.sem(key), banks.uses(key) + 1)
                        act.nop().then_inc(gc_ready, 1)
                elif ch == 2:
                    dst = q[:, c, t0:t0 + n] if c < 4 else kk[:, t0:t0 + n]
                    act.copy(dst, src).then_inc(banks.sem(key), 1)
                else:
                    if c:
                        act.wait_ge(roped, 2 * (c - 1) + ch + 1)
                    act.copy(qraw[:, ch, :], src).then_inc(banks.sem(key), 1)
                    act.wait_ge(banks.sem(key), banks.uses(key) + 1)
                    act.nop().then_inc(qraw_ready, 1)

        @block.vector
        def _(dve):
            links = 0

            def link(ins):
                nonlocal links
                links += 1
                ins.then_inc(chain, 1)
                dve.wait_ge(chain, links)

            link(dve.memset(prod, 0.0))
            for key in plan:
                kind, c, ch = key
                if kind not in ("rot", "u", "gb"):
                    continue
                t0, n = CHUNKS[ch]
                src = m.ps[:, banks.bank(key), 0:n]
                dve.wait_ge(banks.done, banks.number(key))
                if kind == "rot":
                    dst = q[:, c, t0:t0 + n] if c < 4 else kk[:, t0:t0 + n]
                    link(dve.tensor_tensor(qraw[:, ch, :], qraw[:, ch, :], m.rope[:, 0, t0:t0 + n], ALU.mult))
                    dve.tensor_tensor(tmp, src, m.rope[:, 1, t0:t0 + n], ALU.mult).then_inc(banks.sem(key), 1)
                    dve.wait_ge(banks.sem(key), banks.uses(key) + 1)
                    dve.tensor_tensor(dst, qraw[:, ch, :], tmp, ALU.add).then_inc(roped, 1)
                    dve.wait_ge(roped, 2 * c + ch + 1)
                elif kind == "u":
                    dve.wait_ge(gc_ready, c + 1)
                    dve.tensor_tensor(prod[:, place(t0):place(t0) + n], src, gcb[:, t0:t0 + n], ALU.mult).then_inc(
                        banks.sem(key), 1)
                    dve.wait_ge(banks.sem(key), banks.uses(key) + 1)
                    dve.nop().then_inc(prod_done, 1)
                    if ch == 2:
                        tap = lambda k: m.cols[:, C_EVW + 4 * k + c:C_EVW + 4 * k + c + 1]
                        link(dve.tensor_scalar(acc, prod[:, 0:TOK + 2], tap(0), m.cols[:, C_EVB + c:C_EVB + c + 1],
                                               ALU.mult, ALU.add))
                        for k in (1, 2):
                            link(dve.scalar_tensor_tensor(acc, prod[:, k:k + TOK + 2], tap(k), acc, ALU.mult, ALU.add))
                else:
                    dve.tensor_tensor(cat[:, 4 + c, t0:t0 + n], src, acc[:, after(t0):after(t0) + n],
                                      ALU.mult).then_inc(banks.sem(key), 1)


def attention_stage(nc, m):
    cat = m.B.rearrange("p (k t) -> p k t", k=K)
    q = m.C[:, 0:4 * TOK].rearrange("p (j t) -> p j t", j=4)
    kk = m.C[:, 4 * TOK:5 * TOK]
    v = m.C[:, 5 * TOK:6 * TOK].rearrange("p (t c) -> p t c", t=NT)
    W = 5 * P
    s = m.A[:, 0:2 * QPK * W].rearrange("p (b j n) -> p b j n", b=2, j=QPK)
    pt = m.ring[:, 0:2 * 5 * BANK].rearrange("p (b c n) -> p b c n", b=2, c=5)
    small = m.ring[:, 6 * D:6 * D + 128].rearrange("p (b x j) -> p b x j", b=2, j=4)
    steps = [(n, kv) for n in range(NT) for kv in range(NKV)]

    def span(n):
        if n >= LT:
            return P, 3 * P
        return (P if n == 0 else 0), (4 * P if n == LT - 1 else 5 * P)

    def key_tile(n, c):
        return {0: n - 1, 1: LT, 2: LT + 1, 3: n, 4: n + 1}[c]

    with stage_of(nc) as ctx:
        sc_done, pt_done, o_done = semaphores(nc, ctx, "at_sc at_pt at_o")
        sc_free = semaphores(nc, ctx, "at_scf0 at_scf1")
        pt_free = semaphores(nc, ctx, "at_ptf0 at_ptf1")
        pt_act, pt_dve, bias_ready, exp_done, normed, o_out, chain = semaphores(
            nc, ctx, "at_pta at_ptd at_bias at_exp at_norm at_out at_chain")
        block = ctx.enter_context(nc.Block())
        pieces = [(g, c) for g, (n, kv) in enumerate(steps) for c in range(span(n)[0] // P, span(n)[1] // P)]
        piece_at = {x: i for i, x in enumerate(pieces)}
        by_act = [sum(1 for i in range(j) if i % 2 == 0) for j in range(len(pieces) + 1)]
        last_piece = [max(piece_at[x] for x in pieces if x[0] == g) for g in range(len(steps))]

        @block.tensor
        def _(pe):
            def scores(g):
                n, kv = steps[g]
                a, b = span(n)
                rows = slice(DH * kv, DH * kv + DH)
                for j in range(QPK):
                    i = QPK * g + j
                    if i >= 2:
                        pe.wait_ge(sc_free[i % 2], i // 2)
                    ps = m.ps[:, 2 * (i % 2):2 * (i % 2) + 2, :].rearrange("p b n -> p (b n)")
                    lhs = q[rows, j, n * P:(n + 1) * P]
                    if a == 0:
                        pe.matmul(ps[:, 3 * P:4 * P], lhs, kk[rows, (n - 1) * P:n * P], start=True, stop=True)
                    mm = pe.matmul(ps[:, 4 * P:6 * P], lhs, kk[rows, SEQ:TOK], start=True, stop=True)
                    if b > 3 * P:
                        mm = pe.matmul(ps[:, 6 * P:3 * P + b], lhs, kk[rows, n * P:n * P + b - 3 * P],
                                       start=True, stop=True)
                    mm.then_inc(sc_done, 1)

            def context_product(g):
                n, kv = steps[g]
                pe.wait_ge(normed, g + 1)
                for c in range(span(n)[0] // P, span(n)[1] // P):
                    i = piece_at[g, c]
                    if i >= 2:
                        pe.wait_ge(pt_free[i % 2], i // 2)
                    for j in range(QPK):
                        mm = pe.transpose(m.ps[:, 4 + i % 2, j * P:(j + 1) * P],
                                          s[:, g % 2, j, c * P:(c + 1) * P], m.ident[:, :])
                    mm.then_inc(pt_done, 1)
                if g >= 2:
                    pe.wait_ge(o_out, g - 1)
                rows = slice(DH * kv, DH * kv + DH)
                chunks = range(span(n)[0] // P, span(n)[1] // P)
                for c in chunks:
                    i = piece_at[g, c]
                    pe.wait_ge(pt_free[i % 2], i // 2 + 1)
                    mm = pe.matmul(m.ps[rows, 6 + g % 2, :], v[:, key_tile(n, c), rows], pt[:, g % 2, c, :],
                                   start=(c == chunks[0]), stop=(c == chunks[-1]))
                mm.then_inc(o_done, 1)

            scores(0)
            for g in range(len(steps)):
                if g + 1 < len(steps):
                    scores(g + 1)
                context_product(g)

        def copy_out(engine, g, parity):
            for c in range(span(steps[g][0])[0] // P, span(steps[g][0])[1] // P):
                i = piece_at[g, c]
                if i % 2 == parity:
                    engine.wait_ge(pt_done, i + 1)
                    if g >= 2:
                        engine.wait_ge(o_done, g - 1)
                    copy = engine.copy if parity == 0 else engine.tensor_copy
                    copy(pt[:, g % 2, c, :], m.ps[:, 4 + parity, :]).then_inc(pt_free[parity], 1)

        @block.scalar
        def _(act):
            def exps(g):
                a, b = span(steps[g][0])
                act.wait_ge(bias_ready, g + 1)
                for j in range(QPK):
                    row = s[:, g % 2, j, a:b]
                    act.activation(row, row, ACT.Exp, bias=small[:, g % 2, 1, j:j + 1],
                                   accum_out=small[:, g % 2, 3, j:j + 1])
                act.activation(small[:, g % 2, 4, :], small[:, g % 2, 2, :], ACT.Exp).then_inc(exp_done, 1)

            exps(0)
            for g, (n, kv) in enumerate(steps):
                if g + 1 < len(steps):
                    exps(g + 1)
                copy_out(act, g, 0)
                act.wait_ge(o_done, g + 1)
                rows = slice(DH * kv, DH * kv + DH)
                act.copy(cat[rows, 0:QPK, n * P:(n + 1) * P],
                         m.ps[rows, 6 + g % 2, :].rearrange("p (j t) -> p j t", j=QPK)).then_inc(o_out, 1)

        @block.vector
        def _(dve):
            links = 0

            def link(ins):
                nonlocal links
                links += 1
                ins.then_inc(chain, 1)
                dve.wait_ge(chain, links)

            def maxima(g):
                n, kv = steps[g]
                a, b = span(n)
                if g >= 2:
                    dve.wait_ge(pt_done, last_piece[g - 2] + 1)
                x = small[:, g % 2]
                for j in range(QPK):
                    i = QPK * g + j
                    dve.wait_ge(sc_done, i + 1)
                    ps = m.ps[:, 2 * (i % 2):2 * (i % 2) + 2, :].rearrange("p b n -> p (b n)")
                    dve.tensor_tensor_reduce(s[:, g % 2, j, a:b], ps[:, 3 * P + a:3 * P + b], m.mask[:, a:b],
                                             DH ** -0.5, -3.0e38, ALU.add, ALU.max,
                                             x[:, 0, j:j + 1]).then_inc(sc_free[i % 2], 1)
                for i in (QPK * g + 2, QPK * g + 3):
                    dve.wait_ge(sc_free[i % 2], i // 2 + 1)
                link(dve.tensor_tensor(x[:, 5, :], x[:, 0, :], m.sink[:, 4 * kv:4 * kv + 4], ALU.max))
                link(dve.tensor_scalar(x[:, 1, :], x[:, 5, :], -1.0, None, ALU.mult))
                dve.tensor_tensor(x[:, 2, :], m.sink[:, 4 * kv:4 * kv + 4], x[:, 5, :], ALU.subtract).then_inc(bias_ready, 1)

            def normalise(g):
                a, b = span(steps[g][0])
                x = small[:, g % 2]
                dve.wait_ge(exp_done, g + 1)
                link(dve.tensor_tensor(x[:, 6, :], x[:, 3, :], x[:, 4, :], ALU.add))
                link(dve.reciprocal(x[:, 7, :], x[:, 6, :]))
                for j in range(QPK):
                    row = s[:, g % 2, j, a:b]
                    last = dve.tensor_scalar(row, row, x[:, 7, j:j + 1], None, ALU.mult)
                last.then_inc(normed, 1)

            maxima(0)
            for g in range(len(steps)):
                normalise(g)
                if g + 1 < len(steps):
                    maxima(g + 1)
                copy_out(dve, g, 1)


def out_stage(nc, m, d, name, layer, inT, w_dram, sources, affT):
    tiles = []
    for src, n, s in sources:
        tiles += [(src[i * P:(i + 1) * P, :], s) for i in range(n)]
    N = len(tiles)
    w = m.ring[:, 0:K * D].rearrange("p (k n) -> p k n", k=K)
    at = 8 * D
    xt = m.ring[:, at:at + 2 * D].rearrange("p (b n) -> p b n", b=2)
    x1 = m.ring[:, at + 2 * D:at + 4 * D].rearrange("p (b n) -> p b n", b=2)
    xn = m.ring[:, at + 4 * D:at + 6 * D].rearrange("p (b n) -> p b n", b=2)
    gates = m.ring[:, at + 6 * D:at + 8 * D].rearrange("p (b n) -> p b n", b=2)
    junk = m.ring[:, at + 8 * D:at + 9 * D]
    h2 = m.A[:, 0:2 * D].rearrange("p (b k t) -> p b k t", b=2, k=K)
    rw = m.A[:, 2 * D:2 * D + K * NE].rearrange("p (k e) -> p k e", k=K)
    st = m.A[:, 2 * D + 256:2 * D + 512].rearrange("p (b x) -> p b x", b=2)
    lg = m.A[:, 2 * D + 512:2 * D + 512 + 4 * NE].rearrange("p (b x e) -> p b x e", b=2, x=2)
    with stage_of(nc) as ctx:
        w_in, aux_in, y_done, y_read, sq, chain, sd_done, xn_done, turned, ev_act, ev_dve = semaphores(
            nc, ctx, " ".join(f"{name}_{x}" for x in
                              "w aux y yread sq chain sd xn turn eva evd".split()))
        lg_done, nmax, ex_done, aff_done, afft_done, afft_out, x1_done = semaphores(
            nc, ctx, " ".join(f"{name}_{x}" for x in "lg nmax ex aff afft afftout x1".split()))
        x_in, x1_out, xn_out = ([semaphore(nc, ctx, f"{name}_{x}{b}") for b in range(2)]
                                for x in ("xin", "x1o", "xno"))
        block = ctx.enter_context(nc.Block())

        def store(sp, t):
            b = t % 2
            sp.wait_ge(x1_done, t + 1)
            sp.dma_start(d["x_res"][t * P:(t + 1) * P, :], x1[:, b, :]).then_inc(x1_out[b], 16)
            sp.wait_ge(xn_done, t + 1)
            sp.dma_start(d["x_norm"][t * P:(t + 1) * P, :], xn[:, b, :]).then_inc(xn_out[b], 16)

        @block.sync
        def _(sp):
            sp.dma_start(w, w_dram).then_inc(w_in, 16)
            sp.dma_start(rw, d["router_w"][layer]).then_inc(aux_in, 16)
            for s in range(2):
                row = d["mrow"][s:s + 1, (layer * 6 + 2) * D:(layer * 6 + 3) * D]
                sp.dma_start(gates[:, s, :], row.to_broadcast((P, D))).then_inc(aux_in, 16)
            for t, (src, s) in enumerate(tiles):
                if t >= 2:
                    sp.wait_ge(x1_done, t - 1)
                sp.dma_start(xt[:, t % 2, :], src).then_inc(x_in[t % 2], 16)
                if t >= 1:
                    store(sp, t - 1)
            store(sp, N - 1)
            for b in range(2):
                sp.wait_ge(x1_out[b], 16 * ((N - b + 1) // 2))
                sp.wait_ge(xn_out[b], 16 * ((N - b + 1) // 2))

        @block.tensor
        def _(pe):
            def project(t):
                pe.wait_ge(y_read, t - 1) if t >= 2 else None
                for half in range(2):
                    for k in range(K):
                        mm = pe.matmul(m.ps[:, 2 * (t % 2) + half, :], inT[:, k, t * P:(t + 1) * P],
                                       w[:, k, half * BANK:(half + 1) * BANK], start=(k == 0), stop=(k == K - 1))
                mm.then_inc(y_done, 1)

            def turn(t):
                pe.wait_ge(xn_done, t + 1)
                if t >= 1:
                    pe.wait_ge(ev_act, t)
                    pe.wait_ge(ev_dve, t)
                for k in range(K):
                    mm = pe.transpose(m.ps[:, 4 + k // 4, (k % 4) * P:(k % 4 + 1) * P],
                                      xn[:, t % 2, k * P:(k + 1) * P], m.ident[:, :])
                mm.then_inc(turned, 1)

            def route(t):
                pe.wait_ge(ev_act, t + 1)
                pe.wait_ge(ev_dve, t + 1)
                if t >= 1:
                    pe.wait_ge(aff_done, t)
                for k in range(K):
                    mm = pe.matmul(m.ps[:, 6, 0:NE], h2[:, t % 2, k, :], rw[:, k, :], start=(k == 0), stop=(k == K - 1))
                mm.then_inc(lg_done, 1)

            def turn_affinities(t):
                pe.wait_ge(aff_done, t + 1)
                if t >= 1:
                    pe.wait_ge(afft_out, t)
                pe.transpose(m.ps[0:NE, 7, 0:P], lg[:, t % 2, 1, :], m.ident[:, :]).then_inc(afft_done, 1)

            pe.wait_ge(w_in, 16)
            pe.wait_ge(aux_in, 48)
            for t in range(N + 3):
                if t < N:
                    project(t)
                if 1 <= t <= N:
                    turn(t - 1)
                if 2 <= t <= N + 1:
                    route(t - 2)
                if t >= 3:
                    turn_affinities(t - 3)

        @block.scalar
        def _(act):
            for t in range(N + 2):
                if t < N:
                    b, s = t % 2, tiles[t][1]
                    act.wait_ge(x1_done, t + 1)
                    act.activation(junk, x1[:, b, :], ACT.Square, accum_out=st[:, b, 0:1]).then_inc(sq, 1)
                    act.wait_ge(chain, 2 * t + 1)
                    act.activation(st[:, b, 2:3], st[:, b, 1:2], ACT.Sqrt).then_inc(sd_done, 1)
                    act.wait_ge(turned, t + 1)
                    if t >= 2:
                        act.wait_ge(lg_done, t - 1)
                    for k in range(4):
                        last = act.activation(h2[:, b, k, :], m.ps[:, 4, k * P:(k + 1) * P], ACT.Identity,
                                              bias=m.mod[:, layer, 3, k, s:s + 1], scale=m.comb[:, layer, 1, k, s:s + 1])
                    last.then_inc(ev_act, 1)
                if 1 <= t <= N:
                    u = (t - 1) % 2
                    act.wait_ge(nmax, t)
                    act.activation(lg[:, u, 0, :], m.ps[:, 6, 0:NE], ACT.Exp, bias=st[:, u, 5:6],
                                   accum_out=st[:, u, 6:7]).then_inc(ex_done, 1)
                if t >= 2:
                    act.wait_ge(afft_done, t - 1)
                    act.copy(affT[:, (t - 2) * P:(t - 1) * P], m.ps[0:NE, 7, 0:P]).then_inc(afft_out, 1)

        @block.vector
        def _(dve):
            steps = semaphores(nc, ctx, f"{name}_links")[0]
            links = 0

            def link(ins):
                nonlocal links
                links += 1
                ins.then_inc(steps, 1)
                dve.wait_ge(steps, links)

            dve.wait_ge(aux_in, 48)
            for t in range(N + 1):
                if t < N:
                    b, s = t % 2, tiles[t][1]
                    dve.wait_ge(y_done, t + 1)
                    dve.wait_ge(x_in[b], 16 * (t // 2 + 1))
                    if t >= 2:
                        dve.wait_ge(x1_out[b], 16 * (t // 2))
                        dve.wait_ge(xn_out[b], 16 * (t // 2))
                        dve.wait_ge(turned, t - 1)
                    y = m.ps[:, 2 * b:2 * b + 2, :].rearrange("p b n -> p (b n)")
                    dve.tensor_tensor(x1[:, b, :], y, gates[:, s, :], ALU.mult).then_inc(y_read, 1)
                    dve.wait_ge(y_read, t + 1)
                    dve.tensor_tensor(x1[:, b, :], x1[:, b, :], xt[:, b, :], ALU.add).then_inc(x1_done, 1)
                    dve.wait_ge(sq, t + 1)
                    dve.tensor_scalar(st[:, b, 1:2], st[:, b, 0:1], 1.0 / D, EPS, ALU.mult, ALU.add).then_inc(chain, 1)
                    dve.wait_ge(sd_done, t + 1)
                    dve.reciprocal(st[:, b, 3:4], st[:, b, 2:3]).then_inc(chain, 1)
                    dve.wait_ge(chain, 2 * t + 2)
                    dve.tensor_scalar(xn[:, b, :], x1[:, b, :], st[:, b, 3:4], None, ALU.mult).then_inc(xn_done, 1)
                    dve.wait_ge(turned, t + 1)
                    if t >= 2:
                        dve.wait_ge(lg_done, t - 1)
                    for k in range(4, 8):
                        last = dve.tensor_scalar(h2[:, b, k, :], m.ps[:, 5, (k - 4) * P:(k - 3) * P],
                                                 m.comb[:, layer, 1, k, s:s + 1], m.mod[:, layer, 3, k, s:s + 1],
                                                 ALU.mult, ALU.add)
                    last.then_inc(ev_dve, 1)
                if t >= 1:
                    u = (t - 1) % 2
                    dve.wait_ge(lg_done, t)
                    if t >= 3:
                        dve.wait_ge(afft_done, t - 2)
                    link(dve.tensor_reduce(st[:, u, 4:5], m.ps[:, 6, 0:NE], AX_X, ALU.max))
                    dve.tensor_scalar(st[:, u, 5:6], st[:, u, 4:5], -1.0, None, ALU.mult).then_inc(nmax, 1)
                    dve.wait_ge(ex_done, t)
                    link(dve.reciprocal(st[:, u, 7:8], st[:, u, 6:7]))
                    dve.tensor_scalar(lg[:, u, 1, :], lg[:, u, 0, :], st[:, u, 7:8], None, ALU.mult).then_inc(aff_done, 1)


def choose_stage(nc, m, name, affT, with_context):
    sets = [(0, SEQ, CAP, m.idx, m.gate)]
    if with_context:
        sets.append((SEQ, CTX, CAPC, m.idxc, m.gatec))
    vals = m.A[0:NE, 4 * D:4 * D + CAP]
    idx = m.A[0:NE, 4 * D + 128:4 * D + 128 + CAP].bitcast(U32)
    idxf = m.A[0:NE, 4 * D + 256:4 * D + 256 + CAP]
    with stage_of(nc) as ctx:
        found, turned, copied = semaphores(nc, ctx, f"{name}_found {name}_turn {name}_copy")
        chain = semaphores(nc, ctx, f"{name}_chain")[0]
        block = ctx.enter_context(nc.Block())

        @block.vector
        def _(dve):
            links = 0

            def link(ins):
                nonlocal links
                links += 1
                ins.then_inc(chain, 1)
                dve.wait_ge(chain, links)

            for n, (t0, width, cap, idx_out, gate_out) in enumerate(sets):
                row = affT[:, t0:t0 + width]
                for i in range(cap // 8):
                    at = slice(8 * i, 8 * i + 8)
                    link(dve.max(vals[:, at], row))
                    link(dve.max_index(idx[:, at], vals[:, at], row))
                    link(dve.match_replace(row, vals[:, at], row, -1.0))
                dve.tensor_scalar(idxf[:, 0:cap], idx[:, 0:cap], float(t0), None, ALU.add).then_inc(found, 1)
                dve.wait_ge(turned, n + 1)
                dve.tensor_copy(idx_out[0:cap, 0:NE], m.ps[0:cap, 0, 0:NE]).then_inc(copied, 1)
                dve.tensor_copy(idx_out[0:cap, NE:NE + 1], m.ps[0:cap, 0, 0:1]).then_inc(copied, 1)
                dve.tensor_copy(gate_out[0:cap, :], m.ps[0:cap, 1, 0:NE]).then_inc(copied, 1)

        @block.tensor
        def _(pe):
            for n, (t0, width, cap, idx_out, gate_out) in enumerate(sets):
                pe.wait_ge(found, n + 1)
                if n:
                    pe.wait_ge(copied, 3 * n)
                pe.transpose(m.ps[0:cap, 0, 0:NE], idxf[:, 0:cap], m.ident[0:NE, 0:NE])
                pe.transpose(m.ps[0:cap, 1, 0:NE], vals[:, 0:cap], m.ident[0:NE, 0:NE]).then_inc(turned, 1)


def expert_stage(nc, m, d, name, layer, with_context):
    N = CAP + (CAPC if with_context else 0)
    PER = BANK // N
    YB = -(-K // PER)
    R = 6
    STEPS = 2 * R
    units = d["moe"][layer]
    unit = m.ring[:, :].rearrange("p (s n) -> p s n", s=R)
    w_of = lambda r, part: unit[:, r, part * D:(part + 1) * D].rearrange("p (k n) -> p k n", k=K)
    sets = [(CAP, 0, m.idx, m.gate)] + ([(CAPC, 1, m.idxc, m.gatec)] if with_context else [])
    NS = len(sets)
    OUTS = 2 * NS
    A = m.A
    xg = [A[0:cap, s * D:(s + 1) * D] for cap, s, _, _ in sets]
    ys = [A[0:cap, (2 + s) * D:(3 + s) * D] for cap, s, _, _ in sets]
    gates = [A[0:cap, (4 + s) * D:(5 + s) * D] for cap, s, _, _ in sets]
    xe = m.B[:, 0:2 * K * N].rearrange("p (b k n) -> p b k n", b=2, k=K)
    at = 3 * D
    ysb = m.B[:, at:at + K * N].rearrange("p (k n) -> p k n", k=K)
    sa = m.B[:, at + 2 * D:at + 2 * D + 2 * N].rearrange("p (b n) -> p b n", b=2)
    h = m.B[:, at + 3 * D:at + 3 * D + 2 * N].rearrange("p (b n) -> p b n", b=2)
    gcur = m.B[:, at + 4 * D:at + 4 * D + 2]
    with stage_of(nc) as ctx:
        unit_done, au_done, sa_done, h_done, y_act, y_dve = semaphores(
            nc, ctx, " ".join(f"{name}_{x}" for x in "unit au sa h ya yd".split()))
        in_done, x_act, x_dve, out_done, out_read, ys_ready, gate_ready = semaphores(
            nc, ctx, " ".join(f"{name}_{x}" for x in "in xa xd out outr ys gcur".split()))
        gates_in, gathered, scattered = semaphores(
            nc, ctx, " ".join(f"{name}_{x}" for x in "gates gat scat".split()))
        unit_in = [semaphore(nc, ctx, f"{name}_w{r}") for r in range(R)]
        block = ctx.enter_context(nc.Block())

        def need(engine, sem, value):
            if not isinstance(value, int) or value > 0:
                engine.wait_ge(sem, value)

        def experts(engine, body):
            body(0, 0)
            body(1, 1)
            with engine.Fori(1, NE // 2) as i:
                body(i * 2, 0)
                body(i * 2 + 1, 1)

        @block.sync
        def _(sp):
            for cap, s, _, _ in sets:
                row = d["mrow"][s:s + 1, (layer * 6 + 5) * D:(layer * 6 + 6) * D]
                sp.dma_start(gates[s], row.to_broadcast((cap, D))).then_inc(gates_in, 16)

            def expert(e, b):
                for j in range(FJ):
                    if j >= R:
                        need(sp, unit_done, e * FJ + (j - R + 1))
                    else:
                        old = j + R if j + R < FJ else j
                        need(sp, unit_done, e * FJ + (old + 1 - FJ))
                    sp.dma_start(unit[:, j % R, :], units[e * FJ + j]).then_inc(unit_in[j % R], 16)
            experts(sp, expert)

        @block.gpsimd
        def _(pool):
            def gather(e):
                need(pool, in_done, e)
                for cap, s, idx, _ in sets:
                    pool.indirect_dma_start(xg[s], None, d["x_norm"], bass.IndirectOffsetOnAxis(
                        ap=idx[0:cap, e:e + 1], axis=0)).then_inc(gathered, 16)

            def scatter(e):
                pool.wait_ge(ys_ready, e + 1)
                for cap, s, idx, _ in sets:
                    pool.indirect_dma_start(d["x_res"], bass.IndirectOffsetOnAxis(ap=idx[0:cap, e:e + 1], axis=0),
                                            ys[s], None, compute_op=ALU.add).then_inc(scattered, 16)

            gather(0)
            for e in range(NE):
                gather(e + 1)
                if e:
                    scatter(e - 1)
            scatter(NE - 1)
            pool.wait_ge(scattered, 16 * NS * NE)
            pool.wait_ge(gathered, 16 * NS * (NE + 1))

        @block.tensor
        def _(pe):
            def turn_in(e):
                pe.wait_ge(gathered, e * (16 * NS) + 16 * NS)
                need(pe, out_read, e * OUTS - OUTS)
                for k in range(K):
                    mm = pe.transpose(m.ps[:, 5 + k // 4, (k % 4) * P:(k % 4 + 1) * P],
                                      xg[0][:, k * P:(k + 1) * P], m.ident[:, :])
                for k in range(K if NS > 1 else 0):
                    mm = pe.transpose(m.ps[:, 7, k * CAPC:(k + 1) * CAPC], xg[1][:, k * P:(k + 1) * P],
                                      m.ident[0:CAPC, 0:CAPC])
                mm.then_inc(in_done, 1)

            def turn_out(e):
                pe.wait_ge(y_act, e + 1)
                pe.wait_ge(y_dve, e + 1)
                for piece in range(OUTS):
                    cap, s, _, _ = sets[piece // 2]
                    if piece == 3:
                        pe.wait_ge(out_read, e * OUTS + 1)
                    for q in range(4):
                        mm = pe.transpose(m.ps[0:cap, 5 + piece % 3, q * P:(q + 1) * P],
                                          ysb[:, 4 * (piece % 2) + q, s * CAP:s * CAP + cap], m.ident[:, :])
                    mm.then_inc(out_done, 1)

            def up(e, b, j):
                if j == 0:
                    pe.wait_ge(x_act, e + 1)
                    pe.wait_ge(x_dve, e + 1)
                pe.wait_ge(unit_in[j % R], (e * 16 + 16) if j % R == R - 1 else (e * 32 + (16 + 16 * (j // R))))
                need(pe, h_done, e * FJ + (j - 1))
                for part in range(2):
                    for k in range(K):
                        mm = pe.matmul(m.ps[:, (b + j) % 2, 256 * part:256 * part + N],
                                       w_of(j % R, part)[:, k, :], xe[:, b, k, :], start=(k == 0), stop=(k == K - 1))
                mm.then_inc(au_done, 1)

            def down(e, b, j):
                pe.wait_ge(h_done, e * FJ + (j + 1))
                if j == 0:
                    need(pe, y_act, e)
                    need(pe, y_dve, e)
                w = unit[:, j % R, 2 * D:3 * D]
                for i in range(K):
                    mm = pe.matmul(m.ps[:, 2 + i // PER, (i % PER) * N:(i % PER + 1) * N], w[:, i * P:(i + 1) * P],
                                   h[:, (b + j) % 2, :], start=(j == 0 and i % PER == 0), stop=(j == FJ - 1),
                                   skip_group_check=True)
                mm.then_inc(unit_done, 1)

            def expert(e, b):
                for j in range(FJ):
                    up(e, b, j)
                    if j:
                        down(e, b, j - 1)
                    elif not isinstance(e, int) or e > 0:
                        down(e - 1, 1 - b, FJ - 1)
                    if j == 3 and (not isinstance(e, int) or e > 0):
                        turn_out(e - 1)
                    if j == 6:
                        turn_in(e + 1)

            turn_in(0)
            experts(pe, expert)
            down(NE - 1, 1, FJ - 1)
            turn_out(NE - 1)

        def copy_in(engine, e, b, half):
            engine.wait_ge(in_done, e + 1)
            need(engine, au_done, e * FJ - FJ)
            for cap, s, _, _ in sets:
                for k in range(4 * half, 4 * half + 4) if s == 0 else range(K if half else 0):
                    src = m.ps[:, 5 + half, (k % 4) * P:(k % 4 + 1) * P] if s == 0 else m.ps[:, 7, k * CAPC:(k + 1) * CAPC]
                    out = xe[:, b, k, s * CAP:s * CAP + cap]
                    gain, shift = m.comb[:, layer, 1, k, s:s + 1], m.mod[:, layer, 3, k, s:s + 1]
                    if half == 0:
                        last = engine.activation(out, src, ACT.Identity, bias=shift, scale=gain)
                    else:
                        last = engine.tensor_scalar(out, src, gain, shift, ALU.mult, ALU.add)
            last.then_inc(x_dve if half else x_act, 1)

        def copy_y(engine, e, half):
            engine.wait_ge(unit_done, e * FJ + FJ)
            need(engine, out_done, e * OUTS)
            for bank in range(half, YB, 2):
                n = min(PER, K - bank * PER)
                dst = ysb[:, bank * PER:bank * PER + n, :]
                src = m.ps[:, 2 + bank, 0:n * N].rearrange("p (k n) -> p k n", k=n)
                last = engine.tensor_copy(dst, src) if half else engine.copy(dst, src)
            last.then_inc(y_dve if half else y_act, 1)

        @block.scalar
        def _(act):
            def expert(e, b):
                for j in range(FJ):
                    act.wait_ge(au_done, e * FJ + (j + 1))
                    need(act, h_done, e * FJ + (j - 1))
                    act.activation(sa[:, (b + j) % 2, :], m.ps[:, (b + j) % 2, 0:N], ACT.Silu).then_inc(sa_done, 1)
                    if j == 0 and (not isinstance(e, int) or e > 0):
                        copy_y(act, e - 1, 0)
                    if j == 6:
                        copy_in(act, e + 1, 1 - b, 0)
            copy_in(act, 0, 0, 0)
            experts(act, expert)
            copy_y(act, NE - 1, 0)

        @block.vector
        def _(dve):
            def weigh(e):
                dve.wait_ge(gate_ready, e * NS + NS)
                need(dve, scattered, e * (16 * NS))
                for piece in range(OUTS):
                    cap, s, _, _ = sets[piece // 2]
                    half = slice((piece % 2) * BANK, (piece % 2 + 1) * BANK)
                    dve.wait_ge(out_done, e * OUTS + (piece + 1))
                    dve.scalar_tensor_tensor(ys[s][:, half], m.ps[0:cap, 5 + piece % 3, :], gcur[0:cap, s:s + 1],
                                             gates[s][:, half], ALU.mult, ALU.mult).then_inc(out_read, 1)
                dve.wait_ge(out_read, e * OUTS + OUTS)
                dve.nop().then_inc(ys_ready, 1)

            def take_gates(e):
                need(dve, out_read, e * OUTS)
                for cap, s, _, gate in sets:
                    dve.tensor_copy(gcur[0:cap, s:s + 1], gate[0:cap, bass.ds(e, 1)]).then_inc(gate_ready, 1)

            def expert(e, b):
                for j in range(FJ):
                    dve.wait_ge(sa_done, e * FJ + (j + 1))
                    need(dve, unit_done, e * FJ + (j - 1))
                    dve.tensor_tensor(h[:, (b + j) % 2, :], m.ps[:, (b + j) % 2, 256:256 + N], sa[:, (b + j) % 2, :],
                                      ALU.mult).then_inc(h_done, 1)
                    later = not isinstance(e, int) or e > 0
                    if j == 0 and later:
                        copy_y(dve, e - 1, 1)
                    if j == 2 and later:
                        take_gates(e - 1)
                    if j == 3 and later:
                        weigh(e - 1)
                    if j == 6:
                        copy_in(dve, e + 1, 1 - b, 1)
            dve.wait_ge(gates_in, 16 * NS)
            copy_in(dve, 0, 0, 1)
            experts(dve, expert)
            copy_y(dve, NE - 1, 1)
            take_gates(NE - 1)
            weigh(NE - 1)


def odd_mixer_stage(nc, m, d):
    hT = m.A.rearrange("p (k t) -> p k t", k=K)
    yT = m.C.rearrange("p (k t) -> p k t", k=K)
    w = m.ring[:, 0:16 * D].rearrange("p (s k n) -> p s k n", s=16, k=K)
    lw = m.B[:, 0:D].rearrange("p (b x n) -> p b x n", b=2, x=4)
    UP = TOK + 6
    UC = TOK + 3
    up = m.ring[:, 16 * D:16 * D + UP]
    uc = m.B[:, D:D + 2 * UC].rearrange("p (b n) -> p b n", b=2)
    at = D + 2 * UC
    r, ig, a, mu, h1 = (m.B[:, at + i * TOK:at + (i + 1) * TOK] for i in range(5))
    h0 = m.rope[:, :, :].rearrange("p a n -> p (a n)")[:, 0:TOK]
    coef = m.mask[:, 0:16 * 6].rearrange("p (x c) -> p x c", x=6)
    gap = UC - TOK

    plan = []
    for h in range(K + 1):
        if h < K:
            plan += [("u", h, ch) for ch in range(3)]
        if h:
            plan += [(kind, h - 1, 0, ch) for kind in ("r", "i") for ch in range(3)]
        if h < K:
            plan += [("g", h, ch) for ch in range(2)]
        if h:
            plan += [(kind, h - 1, 1, ch) for kind in ("r", "i") for ch in range(3)]

    with stage_of(nc) as ctx:
        banks = Banks(nc, ctx, "oi", plan, 8)
        w_in = [semaphore(nc, ctx, f"oi_w{g}") for g in range(4)]
        lw_in = [semaphore(nc, ctx, f"oi_lw{b}") for b in range(2)]
        u_out, conv_done, sig_done, exp_done, tanh_done, a2_done, iu_done, m2_done, mu_done = semaphores(
            nc, ctx, " ".join(f"oi_{x}" for x in "uo conv sig exp tanh a2 iu m2 mu".split()))
        scan_done, gelu_done, coef_done, chain, absexp = semaphores(
            nc, ctx, " ".join(f"oi_{x}" for x in "scan gelu coef chain absexp".split()))
        block = ctx.enter_context(nc.Block())

        @block.sync
        def _(sp):
            for g in range(4):
                sp.dma_start(m.ring[:, 4 * D * g:4 * D * (g + 1)], d["od_in"][g]).then_inc(w_in[g], 16)
            for h in range(K):
                if h >= 2:
                    last = (("i", h - 2, 1, 2))
                    sp.wait_ge(banks.done, banks.number(last))
                sp.dma_start(lw[:, h % 2, :, :], d["od_gates"][h]).then_inc(lw_in[h % 2], 16)

        @block.tensor
        def _(pe):
            for key in plan:
                kind, h, ch = key[0], key[1], key[-1]
                if banks.uses(key):
                    pe.wait_ge(banks.sem(key), banks.uses(key))
                bank = m.ps[:, banks.bank(key), :]
                t0, n = CHUNKS[ch]
                if kind in "ug":
                    slot = 2 * h + (kind == "g")
                    if kind == "u" and h % 2 == 0 and ch == 0:
                        pe.wait_ge(w_in[h // 2], 16)
                    for k in range(K):
                        mm = pe.matmul(bank[:, 0:n], w[:, slot, k, :], hT[:, k, t0:t0 + n], start=(k == 0), stop=(k == K - 1))
                else:
                    x = 2 * key[2] + (kind == "i")
                    if x == 0 and ch == 0:
                        pe.wait_ge(lw_in[h % 2], 16 * (h // 2 + 1))
                        pe.wait_ge(conv_done, h + 1)
                    c0 = t0 if ch < 2 else t0 + gap
                    mm = pe.matmul(bank[:, 0:n], lw[:, h % 2, x, :], uc[:, h % 2, c0:c0 + n], start=True, stop=True)
                mm.then_inc(banks.done, 1)

        @block.scalar
        def _(act):
            lam = m.cols[:, C_LAM:C_LAM + 16]
            act.activation(coef[:, 0, :], lam, ACT.Abs).then_inc(absexp, 1)
            act.wait_ge(absexp, 1)
            act.activation(coef[:, 1, :], coef[:, 0, :], ACT.Exp, scale=-1.0).then_inc(absexp, 1)

            def root(x):
                act.wait_ge(m2_done, x + 1)
                act.activation(mu, mu, ACT.Sqrt).then_inc(mu_done, 1)

            for key in plan:
                kind, h, ch = key[0], key[1], key[-1]
                t0, n = CHUNKS[ch]
                src = m.ps[:, banks.bank(key), 0:n]
                act.wait_ge(banks.done, banks.number(key))
                if kind == "u":
                    if ch == 0 and h:
                        act.wait_ge(conv_done, h)
                    elif ch == 0:
                        act.wait_ge(coef_done, 1)
                    c0 = t0 + 2 if ch < 2 else t0 + 5
                    act.copy(up[:, c0:c0 + n], src).then_inc(banks.sem(key), 1)
                    if ch == 2:
                        for k2 in (("u", h, 0), ("u", h, 1), key):
                            act.wait_ge(banks.sem(k2), banks.uses(k2) + 1)
                        act.nop().then_inc(u_out, 1)
                        if h >= 2:
                            root(2 * (h - 2) + 1)
                elif kind == "g":
                    act.activation(yT[:, h, t0:t0 + n], src, ACT.Gelu_apprx_tanh).then_inc(banks.sem(key), 1)
                    if ch == 1:
                        for k2 in (("g", h, 0), key):
                            act.wait_ge(banks.sem(k2), banks.uses(k2) + 1)
                        act.nop().then_inc(gelu_done, 1)
                        if h:
                            root(2 * (h - 1))
                else:
                    dr = key[2]
                    x = 2 * h + dr
                    if ch == 0 and kind == "r" and x == 2 * K - 2:
                        root(x - 1)
                    if ch == 0 and kind == "r" and x:
                        act.wait_ge(m2_done, x)
                        act.wait_ge(scan_done, x)
                    bias = C_BA if kind == "r" else C_BX
                    act.activation((r if kind == "r" else ig)[:, t0:t0 + n], src, ACT.Sigmoid,
                                   bias=m.cols[:, bias + K * dr + h:bias + K * dr + h + 1]).then_inc(banks.sem(key), 1)
                    if ch == 2:
                        for c in range(3):
                            k2 = (kind, h, dr, c)
                            act.wait_ge(banks.sem(k2), banks.uses(k2) + 1)
                        act.nop().then_inc(sig_done, 1)
                    if ch == 2 and kind == "i":
                        if x == 0:
                            act.wait_ge(coef_done, 2)
                        c = K * dr + h
                        act.activation(a, r, ACT.Exp, scale=coef[:, 4, c:c + 1]).then_inc(exp_done, 1)
                        act.wait_ge(exp_done, x + 1)
                        act.activation(r, r, ACT.Tanh, scale=coef[:, 5, c:c + 1]).then_inc(tanh_done, 1)
                        if h == K - 1:
                            root(x)

        @block.gpsimd
        def _(pool):
            for x in range(2 * K):
                h = x // 2
                pool.wait_ge(sig_done, 2 * x + 2)
                pool.wait_ge(conv_done, h + 1)
                pool.tensor_tensor(ig[:, 0:SEQ], ig[:, 0:SEQ], uc[:, h % 2, 0:SEQ], ALU.mult)
                pool.tensor_tensor(ig[:, SEQ:TOK], ig[:, SEQ:TOK], uc[:, h % 2, SEQ + gap:UC], ALU.mult).then_inc(iu_done, 1)
                pool.wait_ge(exp_done, x + 1)
                if x:
                    pool.wait_ge(scan_done, x)
                pool.tensor_tensor(mu, a, a, ALU.mult).then_inc(a2_done, 1)

        @block.vector
        def _(dve):
            links = 0

            def link(ins):
                nonlocal links
                links += 1
                ins.then_inc(chain, 1)
                dve.wait_ge(chain, links)

            dve.memset(up, 0.0).then_inc(coef_done, 1)
            dve.wait_ge(absexp, 2)
            lam = m.cols[:, C_LAM:C_LAM + 16]
            e, z, z2, p = coef[:, 1, :], coef[:, 2, :], coef[:, 3, :], coef[:, 0, :]
            link(dve.tensor_scalar(z, e, 2.0, None, ALU.add))
            link(dve.reciprocal(z2, z))
            link(dve.tensor_tensor(z, e, z2, ALU.mult))
            link(dve.tensor_tensor(z2, z, z, ALU.mult))
            link(dve.tensor_scalar(p, z2, 1.0 / 17, None, ALU.mult))
            for c in (15, 13, 11, 9, 7, 5, 3):
                link(dve.scalar_tensor_tensor(p, p, 1.0 / c, z2, ALU.add, ALU.mult))
            link(dve.scalar_tensor_tensor(p, p, 1.0, z, ALU.add, ALU.mult))
            link(dve.tensor_scalar(e, lam, -1.0, 0.0, ALU.mult, ALU.max))
            link(dve.scalar_tensor_tensor(e, p, 2.0, e, ALU.mult, ALU.add))
            link(dve.tensor_scalar(coef[:, 4, :], e, -8.0, None, ALU.mult))
            dve.tensor_scalar(coef[:, 5, :], e, 8.0, None, ALU.mult).then_inc(coef_done, 1)

            def convolve(h):
                dve.wait_ge(u_out, h + 1)
                if h >= 2:
                    dve.wait_ge(banks.done, banks.number(("i", h - 2, 1, 2)))
                    dve.wait_ge(iu_done, 2 * (h - 2) + 2)
                out = uc[:, h % 2, :]
                tap = lambda k: m.cols[:, C_ODW + K * k + h:C_ODW + K * k + h + 1]
                link(dve.tensor_scalar(out, up[:, 0:UC], tap(0), m.cols[:, C_ODB + h:C_ODB + h + 1], ALU.mult, ALU.add))
                for k in (1, 2):
                    link(dve.scalar_tensor_tensor(out, up[:, k:k + UC], tap(k), out, ALU.mult, ALU.add))
                dve.scalar_tensor_tensor(out, up[:, 3:3 + UC], tap(3), out, ALU.mult, ALU.add).then_inc(conv_done, 1)

            def recur(x):
                h, dr = x // 2, x % 2
                dve.wait_ge(a2_done, x + 1)
                dve.wait_ge(tanh_done, x + 1)
                dve.scalar_tensor_tensor(mu, mu, 1.0, r, ALU.add, ALU.mult).then_inc(m2_done, 1)
                dve.wait_ge(mu_done, x + 1)
                dve.wait_ge(iu_done, x + 1)
                link(dve.tensor_tensor(ig, ig, mu, ALU.mult))
                if dr == 0:
                    link(dve.tensor_tensor_scan(h0[:, SEQ:TOK], a[:, SEQ:TOK], ig[:, SEQ:TOK], 0.0, ALU.mult, ALU.add))
                    dve.tensor_tensor_scan(h0[:, 0:SEQ], a[:, 0:SEQ], ig[:, 0:SEQ], h0[:, TOK - 1:TOK],
                                           ALU.mult, ALU.add).then_inc(scan_done, 1)
                else:
                    dve.tensor_tensor_scan(h1[:, ::-1], a[:, ::-1], ig[:, ::-1], 0.0, ALU.mult, ALU.add).then_inc(scan_done, 1)
                    dve.wait_ge(scan_done, x + 1)
                    link(dve.tensor_tensor(h0[:, 0:SEQ], h0[:, 0:SEQ], h1[:, 0:SEQ], ALU.add))
                    dve.wait_ge(gelu_done, h + 1)
                    link(dve.tensor_tensor(yT[:, h, :], yT[:, h, :], h0[:, 0:SEQ], ALU.mult))

            convolve(0)
            for h in range(K):
                recur(2 * h)
                if h + 1 < K:
                    convolve(h + 1)
                recur(2 * h + 1)


def final_stage(nc, m, d):
    with stage_of(nc) as ctx:
        sq, ms_done, sd_done, rs_done, xn_done, out_done, g_in = semaphores(
            nc, ctx, " ".join(f"f_{x}" for x in "sq ms sd rs xn out g".split()))
        x_in = semaphores(nc, ctx, "f_x0 f_x1")
        stored = semaphores(nc, ctx, "f_o0 f_o1")
        xt = m.A[:, 0:2 * D].rearrange("p (b n) -> p b n", b=2)
        yt = m.A[:, 2 * D:4 * D].rearrange("p (b n) -> p b n", b=2)
        junk, gain = m.A[:, 4 * D:5 * D], m.A[:, 5 * D:6 * D]
        st = m.A[:, 6 * D:6 * D + 8]
        block = ctx.enter_context(nc.Block())

        @block.sync
        def _(sp):
            sp.dma_start(gain, d["final_g"].to_broadcast((P, D))).then_inc(g_in, 16)
            with sp.Fori(0, LT // 2) as i:
                for b in range(2):
                    sp.wait_ge(xn_done, i * 2 + (b + 1))
                    sp.dma_start(xt[:, b, :], d["x_res"][bass.ds((i * 2 + b) * P, P), :]).then_inc(x_in[b], 16)

        @block.scalar
        def _(act):
            with act.Fori(0, LT // 2) as i:
                for b in range(2):
                    t = i * 2 + b
                    act.wait_ge(x_in[b], i * 16 + 16)
                    act.activation(junk, xt[:, b, :], ACT.Square, accum_out=st[:, b:b + 1]).then_inc(sq, 1)
                    act.wait_ge(ms_done, t + 1)
                    act.activation(st[:, 4 + b:5 + b], st[:, 2 + b:3 + b], ACT.Sqrt).then_inc(sd_done, 1)
                    act.wait_ge(out_done, t + 1)
                    act.dma_start(d["out"][bass.ds((i * 2 + b) * P, P), :], yt[:, b, :]).then_inc(stored[b], 16)
            for b in range(2):
                act.wait_ge(stored[b], 16 * LT // 2)

        @block.vector
        def _(dve):
            dve.wait_ge(g_in, 16)
            dve.nop().then_inc(xn_done, 2)

            def tile(i, b):
                t = i * 2 + b
                dve.wait_ge(sq, t + 1)
                dve.tensor_scalar(st[:, 2 + b:3 + b], st[:, b:b + 1], 1.0 / D, EPS, ALU.mult, ALU.add).then_inc(ms_done, 1)
                dve.wait_ge(sd_done, t + 1)
                dve.reciprocal(st[:, 6 + b:7 + b], st[:, 4 + b:5 + b]).then_inc(rs_done, 1)
                dve.wait_ge(rs_done, t + 1)
                if not isinstance(i, int):
                    dve.wait_ge(stored[b], i * 16)
                dve.tensor_scalar(yt[:, b, :], xt[:, b, :], st[:, 6 + b:7 + b], None, ALU.mult).then_inc(xn_done, 1)
                dve.wait_ge(xn_done, t + 3)
                dve.tensor_tensor(yt[:, b, :], yt[:, b, :], gain, ALU.mult).then_inc(out_done, 1)

            for b in range(2):
                tile(0, b)
            with dve.Fori(1, LT // 2) as i:
                for b in range(2):
                    tile(i, b)


def build(nc, d, stop=99):
    with ExitStack() as ctx:
        m = Memory(nc, ctx)
        hT = m.A.rearrange("p (k t) -> p k t", k=K)
        affT = m.A[0:NE, 6 * D:6 * D + TOK]
        inputs = [(d["x"], 0, LT, 0), (d["ctx"], 0, NT - LT, 1)]
        stages = [
            lambda: ada_stage(nc, m, d),
            lambda: norm_stage(nc, m, "n0", 0, inputs, hT),
            lambda: even_in_stage(nc, m, d),
            lambda: attention_stage(nc, m),
            lambda: out_stage(nc, m, d, "o0", 0, m.B.rearrange("p (k t) -> p k t", k=K), d["ev_out"],
                              [(d["x"], LT, 0), (d["ctx"], NT - LT, 1)], affT),
            lambda: choose_stage(nc, m, "c0", affT, True),
            lambda: expert_stage(nc, m, d, "e0", 0, True),
            lambda: norm_stage(nc, m, "n1", 1, [(d["x_res"], 0, LT, 0), (d["x_res"], SEQ, NT - LT, 1)], hT),
            lambda: odd_mixer_stage(nc, m, d),
            lambda: out_stage(nc, m, d, "o1", 1, m.C.rearrange("p (k t) -> p k t", k=K), d["od_out"],
                              [(d["x_res"][0:SEQ, :], LT, 0)], affT),
            lambda: choose_stage(nc, m, "c1", affT, False),
            lambda: expert_stage(nc, m, d, "e1", 1, False),
            lambda: final_stage(nc, m, d),
        ]
        for stage in stages[:stop]:
            stage()


def column_tiles(w):
    n = w.shape[-1] // P
    return w.reshape(K, P, n, P).transpose(2, 1, 0, 3)


def constants():
    f = np.arange(P) % 16
    inv = (10000.0 ** (-np.arange(16, dtype=np.float32) / 16)).astype(np.float32)[f]
    t = np.arange(SEQ)
    pos = np.where(((np.arange(P) % DH) < DH // 2)[:, None], (t // GRID_W)[None, :], (t % GRID_W)[None, :])
    ang = (pos.astype(np.float32) * inv[:, None]).astype(np.float32)
    rope = np.stack([np.cos(ang), np.sin(ang)], axis=1).astype(np.float32)
    rot = np.zeros((P, P), np.float32)
    for i in range(P):
        if i % 32 < 16:
            rot[i + 16, i] = -1.0
        else:
            rot[i - 16, i] = 1.0
    i, j = np.arange(P)[:, None], np.arange(P)[None, :]
    mask = np.zeros((P, 5 * P), np.float32)
    mask[:, 0:P] = np.where(j >= i, 0.0, NEG / DH ** -0.5)
    mask[:, 4 * P:5 * P] = np.where(j <= i, 0.0, NEG / DH ** -0.5)
    return {"rope": rope, "rot": rot, "mask": mask, "ident": np.eye(P, dtype=np.float32)}


def lay_out(x, c, ctx, c_ctx, ada_w, ada_b, norm_mix_g, norm_ffn_g, ev_w_in, ev_w_out, ev_sink, ev_conv_w,
            ev_conv_b, od_w_in, od_w_out, od_conv_w, od_conv_b, od_wa, od_ba, od_wx, od_bx, od_lambda,
            router_w, w_gate, w_up, w_down, final_g):
    col = lambda v: v.reshape(-1, P)
    cond = np.stack([c.reshape(K, P), c_ctx.reshape(K, P)], axis=1)
    cols = np.concatenate([col(v) for v in (cond, norm_mix_g, norm_ffn_g, ev_conv_w, ev_conv_b, od_conv_w,
                                            od_conv_b, od_ba, od_bx, od_lambda)]).T
    pair = lambda w: w.reshape(w.shape[0], NKV, QPK, DH).transpose(0, 2, 1, 3).reshape(w.shape[0], -1)
    w = ev_w_in[0]
    t = column_tiles(np.concatenate([pair(w[:, 0:512]), w[:, 512:]], axis=1))
    order = [0, 1, 2, 3, 4, 5] + [b + c for c in range(CB) for b in (10, 14, 6)]
    ev_in = t[order].reshape(6, 3, P, D).transpose(0, 2, 1, 3).reshape(6, P, 3 * D)
    wo = ev_w_out[0]
    wo = np.concatenate([pair(wo[0:512].T).T, wo[512:]])
    t = column_tiles(od_w_in[0])
    order = [x for h in range(K) for x in (K + h, h)]
    od_in = t[order].reshape(4, 4, P, D).transpose(0, 2, 1, 3).reshape(4, P, 4 * D)
    rows = lambda w: w.reshape(K, P, D).transpose(1, 0, 2)
    gates = np.stack([od_wa[0, 0], od_wx[0, 0], od_wa[0, 1], od_wx[0, 1]], axis=2)
    up = lambda w: w.reshape(2, NE, K, P, FJ, P).transpose(0, 1, 4, 3, 2, 5).reshape(2, NE * FJ, P, D)
    moe = np.concatenate([up(w_gate), up(w_up), w_down.reshape(2, NE * FJ, P, D)], axis=3)
    ada = ada_w.reshape(2, K, P, 12, BANK).transpose(0, 3, 2, 1, 4).reshape(24, P, K, BANK)
    router = router_w.reshape(2, K, P, NE).transpose(0, 2, 1, 3)
    return {"x": x[0], "ctx": ctx[0], "cols": cols, "ada_w": ada, "ada_b": ada_b, "ev_in": ev_in,
            "ev_out": rows(wo), "ev_sink": ev_sink, "od_in": od_in, "od_out": rows(od_w_out[0]),
            "od_gates": gates, "router_w": router, "moe": moe, "final_g": final_g.reshape(1, D), **constants()}


def kernel(_stop=99, **inputs):
    import concourse.bacc as bacc
    from concourse.bass_utils import run_bass_kernel_spmd

    nc = bacc.Bacc("TRN2", target_bir_lowering=False, num_devices=1)
    arrays = {f"in_{k}": np.ascontiguousarray(a) for k, a in lay_out(**{k: np.asarray(v) for k, v in inputs.items()}).items()}
    d = {k[3:]: nc.dram_tensor(k, a.shape, F32, kind="ExternalInput").ap() for k, a in arrays.items()}
    d["out"] = nc.dram_tensor("out", (SEQ, D), F32, kind="ExternalOutput").ap()
    d["x_res"] = nc.dram_tensor("x_res", (TOK, D), F32, kind="Internal").ap()
    d["x_norm"] = nc.dram_tensor("x_norm", (TOK, D), F32, kind="Internal").ap()
    d["mrow"] = nc.dram_tensor("mrow", (2, 12 * D), F32, kind="Internal").ap()
    build(nc, d, _stop)
    result = run_bass_kernel_spmd(nc, [arrays], core_ids=[0])
    return result.results[0]["out"].reshape(1, SEQ, D)
```

```python
from contextlib import ExitStack, contextmanager

import numpy as np

import concourse.bass as bass
from concourse import mybir

F32 = mybir.dt.float32
F32R = mybir.dt.float32r
U32 = mybir.dt.uint32
ALU = mybir.AluOpType
ACT = mybir.ActivationFunctionType
AX_X = mybir.AxisListType.X

P = 128
D = 1024
K = D // P
SEQ = 1024
CTX = 256
TOK = SEQ + CTX
LT = SEQ // P
NT = TOK // P
EPS = 1e-6
DH = 64
NKV = 2
QPK = 4
GRID_W = 64
NE = 16
FF = 1408
FJ = FF // P
CAP = 2 * SEQ // NE
CAPC = 2 * CTX // NE
NEG = -1e30
CB = D // 2 // P
BANK = 512
CHUNKS = [(0, 512), (512, 512), (SEQ, CTX)]

C_COND, C_GMIX, C_GFFN = 0, 16, 32
C_EVW, C_EVB, C_ODW, C_ODB = 48, 60, 64, 96
C_BA, C_BX, C_LAM, C_ALL = 104, 120, 136, 152


class Memory:

    def __init__(self, nc, ctx):
        sb = lambda name, shape, dt=F32: ctx.enter_context(nc.sbuf_tensor(name, shape, dt))
        self.cols = sb("cols", [P, C_ALL])
        self.ident = sb("ident_sb", [P, P])
        self.rope = sb("rope_sb", [P, 2, SEQ])
        self.mask = sb("mask_sb", [P, 5 * P])
        self.mod = sb("mod", [P, 2, 6, K, 2])
        self.comb = sb("comb", [P, 2, 2, K, 2])
        self.sink = sb("sink_sb", [P, 8])
        self.idx = sb("idx", [P, NE + 1], U32)
        self.idxc = sb("idxc", [P, NE + 1], U32)
        self.gate = sb("gate", [P, NE])
        self.gatec = sb("gatec", [P, NE])
        self.ps = ctx.enter_context(nc.psum_tensor("ps", [P, 8, BANK], F32))

    @contextmanager
    def regions(self, nc, name):
        with ExitStack() as ctx:
            self.ring = ctx.enter_context(nc.sbuf_tensor(f"ring_{name}", [P, 18 * D], F32))
            self.big = ctx.enter_context(nc.sbuf_tensor(f"big_{name}", [P, 28 * D], F32))
            self.A = self.big[:, 0:10 * D]
            self.B = self.big[:, 10 * D:20 * D]
            self.C = self.big[:, 20 * D:28 * D]
            yield


@contextmanager
def stage_of(nc):
    with ExitStack() as ctx:
        ctx.taken = []
        ctx.callback(nc.all_engine_barrier)
        ctx.callback(lambda: nc.clear_and_free_semaphores(ctx.taken))
        yield ctx


def semaphore(nc, ctx, name):
    ctx.taken.append(nc.alloc_semaphore(name))
    return ctx.taken[-1]


def semaphores(nc, ctx, names):
    return [semaphore(nc, ctx, n) for n in names.split()]


def ada_stage(nc, m, d):
    UNITS, SLOTS = 24, 4
    with stage_of(nc) as ctx:
        cols_in, bias_in, silu_done, mm_done, row_done, turned, stored0, stored1, col_done = semaphores(
            nc, ctx, "a_cols a_bias a_silu a_mm a_row a_turn a_st0 a_st1 a_col")
        stored = [stored0, stored1]
        unit_in = [semaphore(nc, ctx, f"a_unit{i}") for i in range(SLOTS)]
        comb_step = semaphores(nc, ctx, "a_comb")[0]
        consts_in = semaphores(nc, ctx, "a_consts")[0]
        w = m.ring[:, 0:SLOTS * 4 * D].rearrange("p (s k n) -> p s k n", s=SLOTS, k=K)
        bias = m.A[0:2, 0:10 * D]
        bias2 = m.B[0:2, 0:2 * D]
        row = m.C[0:2, 0:2 * BANK].rearrange("p (b n) -> p b n", b=2)
        cond = m.C[:, 4 * BANK:4 * BANK + 2 * K]
        modc = m.mod[:, :, :, :, :].rearrange("p l j k s -> p (l j k) s")
        block = ctx.enter_context(nc.Block())

        @block.sync
        def _(sp):
            sp.dma_start(m.cols[:, :], d["cols"]).then_inc(cols_in, 16)
            flat = d["ada_b"].rearrange("(o l) n -> o (l n)", o=1)
            sp.dma_start(bias, flat[:, 0:10 * D].to_broadcast((2, 10 * D))).then_inc(bias_in, 16)
            sp.dma_start(bias2, flat[:, 10 * D:12 * D].to_broadcast((2, 2 * D))).then_inc(bias_in, 16)
            with sp.Fori(0, UNITS // SLOTS) as i:
                for s in range(SLOTS):
                    sp.wait_ge(mm_done, i * SLOTS + s + 1)
                    sp.dma_start(w[:, s, :, :], d["ada_w"][i * SLOTS + s]).then_inc(unit_in[s], 16)

        @block.scalar
        def _(act):
            act.dma_start(m.ident[:, :], d["ident"]).then_inc(consts_in, 16)
            act.dma_start(m.rope[:, :, :], d["rope"]).then_inc(consts_in, 16)
            act.dma_start(m.mask[:, :], d["mask"]).then_inc(consts_in, 16)
            act.dma_start(m.sink[:, :], d["ev_sink"].to_broadcast((P, 8))).then_inc(consts_in, 16)
            act.wait_ge(cols_in, 16)
            act.activation(cond, m.cols[:, C_COND:C_COND + 2 * K], ACT.Silu).then_inc(silu_done, 1)
            with act.Fori(0, UNITS // 2) as i:
                for b in range(2):
                    act.wait_ge(row_done, 2 * i + b + 1)
                    act.dma_start(d["mrow"][:, bass.ds((2 * i + b) * BANK, BANK)], row[:, b, :]).then_inc(stored[b], 16)
            for b in range(2):
                act.wait_ge(stored[b], 16 * UNITS // 2)
            act.wait_ge(consts_in, 64)

        @block.tensor
        def _(pe):
            pe.wait_ge(silu_done, 1)
            pe.wait_ge(consts_in, 64)
            pe.nop().then_inc(mm_done, SLOTS)

            def product(i, u):
                n = i * SLOTS + u
                pe.wait_ge(unit_in[u], 16 * i + 16)
                for k in range(K):
                    mm = pe.matmul(m.ps[0:2, u % 2, :], cond[:, 2 * k:2 * k + 2], w[:, u, k, :],
                                   start=(k == 0), stop=(k == K - 1))
                mm.then_inc(mm_done, 1)

            def turn(n, b):
                pe.wait_ge(row_done, n + 1)
                for q in range(4):
                    mm = pe.matmul(m.ps[:, 2 + b, 2 * q:2 * q + 2], row[:, b, q * P:(q + 1) * P],
                                   m.ident[0:2, 0:2], start=True, stop=True)
                mm.then_inc(turned, 1)

            with pe.Fori(0, UNITS // SLOTS) as i:
                for u in range(SLOTS):
                    product(i, u)
                    turn(i * SLOTS + u, u % 2)

        @block.vector
        def _(dve):
            dve.wait_ge(bias_in, 32)

            def unit(n, b, bias_ap, first):
                dve.wait_ge(mm_done, n + 1 + SLOTS)
                if not first:
                    dve.wait_ge(stored[b], (n - b) * 8)
                    dve.wait_ge(turned, n - 1)
                dve.tensor_tensor(row[:, b, :], m.ps[0:2, b, :], bias_ap, ALU.add).then_inc(row_done, 1)
                dve.wait_ge(turned, n + 1)
                dve.tensor_copy(modc[:, bass.ds(n * 4, 4), :],
                                m.ps[:, 2 + b, 0:8].rearrange("p (q s) -> p q s", s=2)).then_inc(col_done, 1)

            for b in range(2):
                unit(b, b, bias[:, b * BANK:(b + 1) * BANK], True)
            with dve.Fori(1, 10) as i:
                for b in range(2):
                    unit(2 * i + b, b, bias[:, bass.ds(i * D + b * BANK, BANK)], False)
            for n in range(20, 24):
                unit(n, n % 2, bias2[:, (n - 20) * BANK:(n - 19) * BANK], False)
            dve.wait_ge(col_done, UNITS)
            step = 0
            for l in range(2):
                for part, gain in ((1, C_GMIX), (4, C_GFFN)):
                    g = m.cols[:, gain + K * l:gain + K * (l + 1)]
                    for s in range(2):
                        out = m.comb[:, l, part // 4, :, s]
                        dve.scalar_tensor_tensor(out, m.mod[:, l, part, :, s], 1.0, g, ALU.add, ALU.mult).then_inc(
                            comb_step, 1)


def norm_stage(nc, m, name, layer, sources, hT):
    with stage_of(nc) as ctx:
        sq, ms_done, sd_done, rs_done, xn_done, turned, ev_act, ev_dve = semaphores(
            nc, ctx, " ".join(f"{name}_{x}" for x in "sq ms sd rs xn turn eva evd".split()))
        x_in = [semaphore(nc, ctx, f"{name}_x{b}") for b in range(2)]
        xt = m.B[:, 0:2 * D].rearrange("p (b n) -> p b n", b=2)
        xn = m.B[:, 2 * D:4 * D].rearrange("p (b n) -> p b n", b=2)
        junk = m.B[:, 4 * D:5 * D]
        st = m.B[:, 5 * D:5 * D + 8]
        block = ctx.enter_context(nc.Block())

        def tiles(engine, body):
            base = 0
            for src, first, n, s in sources:
                if n > 2:
                    with engine.Fori(0, n // 2) as i:
                        for b in range(2):
                            body(i * 2 + b + base, i, src, first + (i * 2 + b) * P, s, b)
                else:
                    for b in range(2):
                        body(base + b, base // 2, src, first + b * P, s, b)
                base += n

        @block.sync
        def _(sp):
            def load(t, half, src, row, s, b):
                sp.wait_ge(xn_done, t + 1)
                sp.dma_start(xt[:, b, :], src[bass.ds(row, P), :]).then_inc(x_in[b], 16)
            tiles(sp, load)

        @block.scalar
        def _(act):
            act.nop().then_inc(ev_act, 2)

            def tile(t, half, src, row, s, b):
                act.wait_ge(x_in[b], 16 * half + 16)
                act.activation(junk, xt[:, b, :], ACT.Square, accum_out=st[:, b:b + 1]).then_inc(sq, 1)
                act.wait_ge(ms_done, t + 1)
                act.activation(st[:, 4 + b:5 + b], st[:, 2 + b:3 + b], ACT.Sqrt).then_inc(sd_done, 1)
                act.wait_ge(turned, t + 3)
                for k in range(4):
                    last = act.activation(hT[:, k, bass.ds(t * P, P)], m.ps[:, 2 * b, k * P:(k + 1) * P],
                                          ACT.Identity, bias=m.mod[:, layer, 0, k, s:s + 1],
                                          scale=m.comb[:, layer, 0, k, s:s + 1])
                last.then_inc(ev_act, 1)
            tiles(act, tile)

        @block.vector
        def _(dve):
            dve.nop().then_inc(xn_done, 2)
            dve.nop().then_inc(ev_dve, 2)

            def tile(t, half, src, row, s, b):
                dve.wait_ge(sq, t + 1)
                dve.tensor_scalar(st[:, 2 + b:3 + b], st[:, b:b + 1], 1.0 / D, EPS, ALU.mult, ALU.add).then_inc(ms_done, 1)
                dve.wait_ge(sd_done, t + 1)
                dve.reciprocal(st[:, 6 + b:7 + b], st[:, 4 + b:5 + b]).then_inc(rs_done, 1)
                dve.wait_ge(rs_done, t + 1)
                dve.wait_ge(turned, t + 1)
                dve.tensor_scalar(xn[:, b, :], xt[:, b, :], st[:, 6 + b:7 + b], None, ALU.mult).then_inc(xn_done, 1)
                dve.wait_ge(turned, t + 3)
                for k in range(4, 8):
                    last = dve.tensor_scalar(hT[:, k, bass.ds(t * P, P)], m.ps[:, 2 * b + 1, (k - 4) * P:(k - 3) * P],
                                             m.comb[:, layer, 0, k, s:s + 1], m.mod[:, layer, 0, k, s:s + 1],
                                             ALU.mult, ALU.add)
                last.then_inc(ev_dve, 1)
            tiles(dve, tile)

        @block.tensor
        def _(pe):
            pe.nop().then_inc(turned, 2)

            def tile(t, half, src, row, s, b):
                pe.wait_ge(xn_done, t + 3)
                pe.wait_ge(ev_act, t + 1)
                pe.wait_ge(ev_dve, t + 1)
                for k in range(K):
                    mm = pe.transpose(m.ps[:, 2 * b + k // 4, (k % 4) * P:(k % 4 + 1) * P],
                                      xn[:, b, k * P:(k + 1) * P], m.ident[:, :])
                mm.then_inc(turned, 1)
            tiles(pe, tile)


class Banks:

    def __init__(self, nc, ctx, name, plan, n, first=0):
        self.n, self.first = n, first
        self.at = {key: i for i, key in enumerate(plan)}
        assert len(self.at) == len(plan)
        self.free = [semaphore(nc, ctx, f"{name}_bank{b}") for b in range(n)]
        self.done = semaphore(nc, ctx, f"{name}_mm")

    def bank(self, key):
        return self.first + self.at[key] % self.n

    def sem(self, key):
        return self.free[self.at[key] % self.n]

    def uses(self, key):
        return self.at[key] // self.n

    def number(self, key):
        return self.at[key] + 1


def even_in_stage(nc, m, d):
    hT = m.A.rearrange("p (k t) -> p k t", k=K)
    cat = m.B.rearrange("p (k t) -> p k t", k=K)
    q = m.C[:, 0:4 * TOK].rearrange("p (j t) -> p j t", j=4)
    kk = m.C[:, 4 * TOK:5 * TOK]
    v = m.C[:, 5 * TOK:6 * TOK].rearrange("p (t c) -> p t c", t=NT)
    tmp = m.C[:, 6 * TOK:6 * TOK + BANK]
    gcb = m.B[:, 0:TOK]
    WP = TOK + 4
    prod = m.B[:, TOK:TOK + WP]
    acc = m.B[:, TOK + WP:TOK + WP + TOK + 2]
    at = 2 * TOK + WP + 2
    qraw = m.B[:, at:at + 2 * BANK].rearrange("p (b n) -> p b n", b=2)
    w = m.ring[:, :].rearrange("p (s k n) -> p s k n", s=18, k=K)
    slot = lambda kind, c: {"qk": c, "v": 5, "gc": 6 + 3 * c, "u": 7 + 3 * c, "gb": 8 + 3 * c}[kind]
    place = lambda c0: c0 + 1 if c0 < SEQ else c0 + 3
    after = lambda c0: c0 if c0 < SEQ else c0 + 2

    plan = []
    for j in range(5):
        plan += [("qk", j, 0), ("qk", j, 1), ("rot", j, 0), ("qk", j, 2), ("rot", j, 1)]
    plan += [("v", t, 0) for t in range(NT)]
    for c in range(CB):
        plan += [(kind, c, ch) for kind in ("gc", "u", "gb") for ch in range(3)]

    with stage_of(nc) as ctx:
        banks = Banks(nc, ctx, "ei", plan, 6)
        w_in = [semaphore(nc, ctx, f"ei_w{g}") for g in range(6)]
        rot_in, qraw_ready, roped, gc_ready, prod_done, chain = semaphores(
            nc, ctx, "ei_rot ei_qraw ei_roped ei_gc ei_prod ei_chain")
        block = ctx.enter_context(nc.Block())

        @block.sync
        def _(sp):
            for g in range(6):
                sp.dma_start(m.ring[:, 3 * D * g:3 * D * (g + 1)], d["ev_in"][g]).then_inc(w_in[g], 16)
            sp.dma_start(m.B[:, 4900:4900 + P], d["rot"]).then_inc(rot_in, 16)

        rot = m.B[:, 4900:4900 + P]

        @block.tensor
        def _(pe):
            seen = set()
            for key in plan:
                kind, c, ch = key
                if banks.uses(key):
                    pe.wait_ge(banks.sem(key), banks.uses(key))
                bank = m.ps[:, banks.bank(key), :]
                if kind == "rot":
                    if not seen & {"rot"}:
                        pe.wait_ge(rot_in, 16)
                        seen.add("rot")
                    pe.wait_ge(qraw_ready, 2 * c + ch + 1)
                    pe.matmul(bank, rot, qraw[:, ch, :], start=True, stop=True).then_inc(banks.done, 1)
                    continue
                g = slot(kind, c) // 3
                if g not in seen:
                    pe.wait_ge(w_in[g], 16)
                    seen.add(g)
                for k in range(K):
                    if kind == "v":
                        mm = pe.matmul(bank[:, 0:P], hT[:, k, c * P:(c + 1) * P], w[:, 5, k, :],
                                       start=(k == 0), stop=(k == K - 1))
                    else:
                        t0, n = CHUNKS[ch]
                        mm = pe.matmul(bank[:, 0:n], w[:, slot(kind, c), k, :], hT[:, k, t0:t0 + n],
                                       start=(k == 0), stop=(k == K - 1))
                mm.then_inc(banks.done, 1)

        @block.scalar
        def _(act):
            for key in plan:
                kind, c, ch = key
                if kind not in ("qk", "v", "gc"):
                    continue
                t0, n = CHUNKS[ch]
                src = m.ps[:, banks.bank(key), 0:n]
                act.wait_ge(banks.done, banks.number(key))
                if kind == "v":
                    act.copy(v[:, c, :], src[:, 0:P]).then_inc(banks.sem(key), 1)
                elif kind == "gc":
                    if c and ch == 0:
                        act.wait_ge(prod_done, 3 * c)
                    act.copy(gcb[:, t0:t0 + n], src).then_inc(banks.sem(key), 1)
                    if ch == 2:
                        act.wait_ge(banks.sem(key), banks.uses(key) + 1)
                        act.nop().then_inc(gc_ready, 1)
                elif ch == 2:
                    dst = q[:, c, t0:t0 + n] if c < 4 else kk[:, t0:t0 + n]
                    act.copy(dst, src).then_inc(banks.sem(key), 1)
                else:
                    if c:
                        act.wait_ge(roped, 2 * (c - 1) + ch + 1)
                    act.copy(qraw[:, ch, :], src).then_inc(banks.sem(key), 1)
                    act.wait_ge(banks.sem(key), banks.uses(key) + 1)
                    act.nop().then_inc(qraw_ready, 1)

        @block.vector
        def _(dve):
            links = 0

            def link(ins):
                nonlocal links
                links += 1
                ins.then_inc(chain, 1)
                dve.wait_ge(chain, links)

            link(dve.memset(prod, 0.0))
            for key in plan:
                kind, c, ch = key
                if kind not in ("rot", "u", "gb"):
                    continue
                t0, n = CHUNKS[ch]
                src = m.ps[:, banks.bank(key), 0:n]
                dve.wait_ge(banks.done, banks.number(key))
                if kind == "rot":
                    dst = q[:, c, t0:t0 + n] if c < 4 else kk[:, t0:t0 + n]
                    link(dve.tensor_tensor(qraw[:, ch, :], qraw[:, ch, :], m.rope[:, 0, t0:t0 + n], ALU.mult))
                    dve.tensor_tensor(tmp, src, m.rope[:, 1, t0:t0 + n], ALU.mult).then_inc(banks.sem(key), 1)
                    dve.wait_ge(banks.sem(key), banks.uses(key) + 1)
                    dve.tensor_tensor(dst, qraw[:, ch, :], tmp, ALU.add).then_inc(roped, 1)
                    dve.wait_ge(roped, 2 * c + ch + 1)
                elif kind == "u":
                    dve.wait_ge(gc_ready, c + 1)
                    dve.tensor_tensor(prod[:, place(t0):place(t0) + n], src, gcb[:, t0:t0 + n], ALU.mult).then_inc(
                        banks.sem(key), 1)
                    dve.wait_ge(banks.sem(key), banks.uses(key) + 1)
                    dve.nop().then_inc(prod_done, 1)
                    if ch == 2:
                        tap = lambda k: m.cols[:, C_EVW + 4 * k + c:C_EVW + 4 * k + c + 1]
                        link(dve.tensor_scalar(acc, prod[:, 0:TOK + 2], tap(0), m.cols[:, C_EVB + c:C_EVB + c + 1],
                                               ALU.mult, ALU.add))
                        for k in (1, 2):
                            link(dve.scalar_tensor_tensor(acc, prod[:, k:k + TOK + 2], tap(k), acc, ALU.mult, ALU.add))
                else:
                    dve.tensor_tensor(cat[:, 4 + c, t0:t0 + n], src, acc[:, after(t0):after(t0) + n],
                                      ALU.mult).then_inc(banks.sem(key), 1)


def attention_stage(nc, m):
    cat = m.B.rearrange("p (k t) -> p k t", k=K)
    q = m.C[:, 0:4 * TOK].rearrange("p (j t) -> p j t", j=4)
    kk = m.C[:, 4 * TOK:5 * TOK]
    v = m.C[:, 5 * TOK:6 * TOK].rearrange("p (t c) -> p t c", t=NT)
    W = 5 * P
    s = m.A[:, 0:2 * QPK * W].rearrange("p (b j n) -> p b j n", b=2, j=QPK)
    pt = m.ring[:, 0:2 * 5 * BANK].rearrange("p (b c n) -> p b c n", b=2, c=5)
    small = m.ring[:, 6 * D:6 * D + 128].rearrange("p (b x j) -> p b x j", b=2, j=4)
    steps = [(n, kv) for n in range(NT) for kv in range(NKV)]

    def span(n):
        if n >= LT:
            return P, 3 * P
        return (P if n == 0 else 0), (4 * P if n == LT - 1 else 5 * P)

    def key_tile(n, c):
        return {0: n - 1, 1: LT, 2: LT + 1, 3: n, 4: n + 1}[c]

    with stage_of(nc) as ctx:
        sc_done, pt_done, o_done = semaphores(nc, ctx, "at_sc at_pt at_o")
        sc_free = semaphores(nc, ctx, "at_scf0 at_scf1")
        pt_free = semaphores(nc, ctx, "at_ptf0 at_ptf1")
        pt_act, pt_dve, bias_ready, exp_done, normed, o_out, chain = semaphores(
            nc, ctx, "at_pta at_ptd at_bias at_exp at_norm at_out at_chain")
        block = ctx.enter_context(nc.Block())
        pieces = [(g, c) for g, (n, kv) in enumerate(steps) for c in range(span(n)[0] // P, span(n)[1] // P)]
        piece_at = {x: i for i, x in enumerate(pieces)}
        by_act = [sum(1 for i in range(j) if i % 2 == 0) for j in range(len(pieces) + 1)]
        last_piece = [max(piece_at[x] for x in pieces if x[0] == g) for g in range(len(steps))]

        @block.tensor
        def _(pe):
            def scores(g):
                n, kv = steps[g]
                a, b = span(n)
                rows = slice(DH * kv, DH * kv + DH)
                for j in range(QPK):
                    i = QPK * g + j
                    if i >= 2:
                        pe.wait_ge(sc_free[i % 2], i // 2)
                    ps = m.ps[:, 2 * (i % 2):2 * (i % 2) + 2, :].rearrange("p b n -> p (b n)")
                    lhs = q[rows, j, n * P:(n + 1) * P]
                    if a == 0:
                        pe.matmul(ps[:, 3 * P:4 * P], lhs, kk[rows, (n - 1) * P:n * P], start=True, stop=True)
                    mm = pe.matmul(ps[:, 4 * P:6 * P], lhs, kk[rows, SEQ:TOK], start=True, stop=True)
                    if b > 3 * P:
                        mm = pe.matmul(ps[:, 6 * P:3 * P + b], lhs, kk[rows, n * P:n * P + b - 3 * P],
                                       start=True, stop=True)
                    mm.then_inc(sc_done, 1)

            def context_product(g):
                n, kv = steps[g]
                pe.wait_ge(normed, g + 1)
                for c in range(span(n)[0] // P, span(n)[1] // P):
                    i = piece_at[g, c]
                    if i >= 2:
                        pe.wait_ge(pt_free[i % 2], i // 2)
                    for j in range(QPK):
                        mm = pe.transpose(m.ps[:, 4 + i % 2, j * P:(j + 1) * P],
                                          s[:, g % 2, j, c * P:(c + 1) * P], m.ident[:, :])
                    mm.then_inc(pt_done, 1)
                if g >= 2:
                    pe.wait_ge(o_out, g - 1)
                rows = slice(DH * kv, DH * kv + DH)
                chunks = range(span(n)[0] // P, span(n)[1] // P)
                for c in chunks:
                    i = piece_at[g, c]
                    pe.wait_ge(pt_free[i % 2], i // 2 + 1)
                    mm = pe.matmul(m.ps[rows, 6 + g % 2, :], v[:, key_tile(n, c), rows], pt[:, g % 2, c, :],
                                   start=(c == chunks[0]), stop=(c == chunks[-1]))
                mm.then_inc(o_done, 1)

            scores(0)
            for g in range(len(steps)):
                if g + 1 < len(steps):
                    scores(g + 1)
                context_product(g)

        def copy_out(engine, g, parity):
            for c in range(span(steps[g][0])[0] // P, span(steps[g][0])[1] // P):
                i = piece_at[g, c]
                if i % 2 == parity:
                    engine.wait_ge(pt_done, i + 1)
                    if g >= 2:
                        engine.wait_ge(o_done, g - 1)
                    copy = engine.copy if parity == 0 else engine.tensor_copy
                    copy(pt[:, g % 2, c, :], m.ps[:, 4 + parity, :]).then_inc(pt_free[parity], 1)

        @block.scalar
        def _(act):
            def exps(g):
                a, b = span(steps[g][0])
                act.wait_ge(bias_ready, g + 1)
                for j in range(QPK):
                    row = s[:, g % 2, j, a:b]
                    act.activation(row, row, ACT.Exp, bias=small[:, g % 2, 1, j:j + 1],
                                   accum_out=small[:, g % 2, 3, j:j + 1])
                act.activation(small[:, g % 2, 4, :], small[:, g % 2, 2, :], ACT.Exp).then_inc(exp_done, 1)

            exps(0)
            for g, (n, kv) in enumerate(steps):
                if g + 1 < len(steps):
                    exps(g + 1)
                copy_out(act, g, 0)
                act.wait_ge(o_done, g + 1)
                rows = slice(DH * kv, DH * kv + DH)
                act.copy(cat[rows, 0:QPK, n * P:(n + 1) * P],
                         m.ps[rows, 6 + g % 2, :].rearrange("p (j t) -> p j t", j=QPK)).then_inc(o_out, 1)

        @block.vector
        def _(dve):
            links = 0

            def link(ins):
                nonlocal links
                links += 1
                ins.then_inc(chain, 1)
                dve.wait_ge(chain, links)

            def maxima(g):
                n, kv = steps[g]
                a, b = span(n)
                if g >= 2:
                    dve.wait_ge(pt_done, last_piece[g - 2] + 1)
                x = small[:, g % 2]
                for j in range(QPK):
                    i = QPK * g + j
                    dve.wait_ge(sc_done, i + 1)
                    ps = m.ps[:, 2 * (i % 2):2 * (i % 2) + 2, :].rearrange("p b n -> p (b n)")
                    dve.tensor_tensor_reduce(s[:, g % 2, j, a:b], ps[:, 3 * P + a:3 * P + b], m.mask[:, a:b],
                                             DH ** -0.5, -3.0e38, ALU.add, ALU.max,
                                             x[:, 0, j:j + 1]).then_inc(sc_free[i % 2], 1)
                for i in (QPK * g + 2, QPK * g + 3):
                    dve.wait_ge(sc_free[i % 2], i // 2 + 1)
                link(dve.tensor_tensor(x[:, 5, :], x[:, 0, :], m.sink[:, 4 * kv:4 * kv + 4], ALU.max))
                link(dve.tensor_scalar(x[:, 1, :], x[:, 5, :], -1.0, None, ALU.mult))
                dve.tensor_tensor(x[:, 2, :], m.sink[:, 4 * kv:4 * kv + 4], x[:, 5, :], ALU.subtract).then_inc(bias_ready, 1)

            def normalise(g):
                a, b = span(steps[g][0])
                x = small[:, g % 2]
                dve.wait_ge(exp_done, g + 1)
                link(dve.tensor_tensor(x[:, 6, :], x[:, 3, :], x[:, 4, :], ALU.add))
                link(dve.reciprocal(x[:, 7, :], x[:, 6, :]))
                for j in range(QPK):
                    row = s[:, g % 2, j, a:b]
                    last = dve.tensor_scalar(row, row, x[:, 7, j:j + 1], None, ALU.mult)
                last.then_inc(normed, 1)

            maxima(0)
            for g in range(len(steps)):
                normalise(g)
                if g + 1 < len(steps):
                    maxima(g + 1)
                copy_out(dve, g, 1)


def out_stage(nc, m, d, name, layer, inT, w_dram, sources, affT):
    tiles = []
    for src, n, s in sources:
        tiles += [(src[i * P:(i + 1) * P, :], s) for i in range(n)]
    N = len(tiles)
    w = m.ring[:, 0:K * D].rearrange("p (k n) -> p k n", k=K)
    at = 8 * D
    xt = m.ring[:, at:at + 2 * D].rearrange("p (b n) -> p b n", b=2)
    x1 = m.ring[:, at + 2 * D:at + 4 * D].rearrange("p (b n) -> p b n", b=2)
    xn = m.ring[:, at + 4 * D:at + 6 * D].rearrange("p (b n) -> p b n", b=2)
    gates = m.ring[:, at + 6 * D:at + 8 * D].rearrange("p (b n) -> p b n", b=2)
    junk = m.ring[:, at + 8 * D:at + 9 * D]
    h2 = m.A[:, 0:2 * D].rearrange("p (b k t) -> p b k t", b=2, k=K)
    rw = m.A[:, 2 * D:2 * D + K * NE].rearrange("p (k e) -> p k e", k=K)
    st = m.A[:, 2 * D + 256:2 * D + 512].rearrange("p (b x) -> p b x", b=2)
    lg = m.A[:, 2 * D + 512:2 * D + 512 + 4 * NE].rearrange("p (b x e) -> p b x e", b=2, x=2)
    with stage_of(nc) as ctx:
        w_in, aux_in, y_done, y_read, sq, chain, sd_done, xn_done, turned, ev_act, ev_dve = semaphores(
            nc, ctx, " ".join(f"{name}_{x}" for x in
                              "w aux y yread sq chain sd xn turn eva evd".split()))
        lg_done, nmax, ex_done, aff_done, afft_done, afft_out, x1_done = semaphores(
            nc, ctx, " ".join(f"{name}_{x}" for x in "lg nmax ex aff afft afftout x1".split()))
        x_in, x1_out, xn_out = ([semaphore(nc, ctx, f"{name}_{x}{b}") for b in range(2)]
                                for x in ("xin", "x1o", "xno"))
        block = ctx.enter_context(nc.Block())

        def store(sp, t):
            b = t % 2
            sp.wait_ge(x1_done, t + 1)
            sp.dma_start(d["x_res"][t * P:(t + 1) * P, :], x1[:, b, :]).then_inc(x1_out[b], 16)
            sp.wait_ge(xn_done, t + 1)
            sp.dma_start(d["x_norm"][t * P:(t + 1) * P, :], xn[:, b, :]).then_inc(xn_out[b], 16)

        @block.sync
        def _(sp):
            sp.dma_start(w, w_dram).then_inc(w_in, 16)
            sp.dma_start(rw, d["router_w"][layer]).then_inc(aux_in, 16)
            for s in range(2):
                row = d["mrow"][s:s + 1, (layer * 6 + 2) * D:(layer * 6 + 3) * D]
                sp.dma_start(gates[:, s, :], row.to_broadcast((P, D))).then_inc(aux_in, 16)
            for t, (src, s) in enumerate(tiles):
                if t >= 2:
                    sp.wait_ge(x1_done, t - 1)
                sp.dma_start(xt[:, t % 2, :], src).then_inc(x_in[t % 2], 16)
                if t >= 1:
                    store(sp, t - 1)
            store(sp, N - 1)
            for b in range(2):
                sp.wait_ge(x1_out[b], 16 * ((N - b + 1) // 2))
                sp.wait_ge(xn_out[b], 16 * ((N - b + 1) // 2))

        @block.tensor
        def _(pe):
            def project(t):
                pe.wait_ge(y_read, t - 1) if t >= 2 else None
                for half in range(2):
                    for k in range(K):
                        mm = pe.matmul(m.ps[:, 2 * (t % 2) + half, :], inT[:, k, t * P:(t + 1) * P],
                                       w[:, k, half * BANK:(half + 1) * BANK], start=(k == 0), stop=(k == K - 1))
                mm.then_inc(y_done, 1)

            def turn(t):
                pe.wait_ge(xn_done, t + 1)
                if t >= 1:
                    pe.wait_ge(ev_act, t)
                    pe.wait_ge(ev_dve, t)
                for k in range(K):
                    mm = pe.transpose(m.ps[:, 4 + k // 4, (k % 4) * P:(k % 4 + 1) * P],
                                      xn[:, t % 2, k * P:(k + 1) * P], m.ident[:, :])
                mm.then_inc(turned, 1)

            def route(t):
                pe.wait_ge(ev_act, t + 1)
                pe.wait_ge(ev_dve, t + 1)
                if t >= 1:
                    pe.wait_ge(aff_done, t)
                for k in range(K):
                    mm = pe.matmul(m.ps[:, 6, 0:NE], h2[:, t % 2, k, :], rw[:, k, :], start=(k == 0), stop=(k == K - 1))
                mm.then_inc(lg_done, 1)

            def turn_affinities(t):
                pe.wait_ge(aff_done, t + 1)
                if t >= 1:
                    pe.wait_ge(afft_out, t)
                pe.transpose(m.ps[0:NE, 7, 0:P], lg[:, t % 2, 1, :], m.ident[:, :]).then_inc(afft_done, 1)

            pe.wait_ge(w_in, 16)
            pe.wait_ge(aux_in, 48)
            for t in range(N + 3):
                if t < N:
                    project(t)
                if 1 <= t <= N:
                    turn(t - 1)
                if 2 <= t <= N + 1:
                    route(t - 2)
                if t >= 3:
                    turn_affinities(t - 3)

        @block.scalar
        def _(act):
            for t in range(N + 2):
                if t < N:
                    b, s = t % 2, tiles[t][1]
                    act.wait_ge(x1_done, t + 1)
                    act.activation(junk, x1[:, b, :], ACT.Square, accum_out=st[:, b, 0:1]).then_inc(sq, 1)
                    act.wait_ge(chain, 2 * t + 1)
                    act.activation(st[:, b, 2:3], st[:, b, 1:2], ACT.Sqrt).then_inc(sd_done, 1)
                    act.wait_ge(turned, t + 1)
                    if t >= 2:
                        act.wait_ge(lg_done, t - 1)
                    for k in range(4):
                        last = act.activation(h2[:, b, k, :], m.ps[:, 4, k * P:(k + 1) * P], ACT.Identity,
                                              bias=m.mod[:, layer, 3, k, s:s + 1], scale=m.comb[:, layer, 1, k, s:s + 1])
                    last.then_inc(ev_act, 1)
                if 1 <= t <= N:
                    u = (t - 1) % 2
                    act.wait_ge(nmax, t)
                    act.activation(lg[:, u, 0, :], m.ps[:, 6, 0:NE], ACT.Exp, bias=st[:, u, 5:6],
                                   accum_out=st[:, u, 6:7]).then_inc(ex_done, 1)
                if t >= 2:
                    act.wait_ge(afft_done, t - 1)
                    act.copy(affT[:, (t - 2) * P:(t - 1) * P], m.ps[0:NE, 7, 0:P]).then_inc(afft_out, 1)

        @block.vector
        def _(dve):
            steps = semaphores(nc, ctx, f"{name}_links")[0]
            links = 0

            def link(ins):
                nonlocal links
                links += 1
                ins.then_inc(steps, 1)
                dve.wait_ge(steps, links)

            dve.wait_ge(aux_in, 48)
            for t in range(N + 1):
                if t < N:
                    b, s = t % 2, tiles[t][1]
                    dve.wait_ge(y_done, t + 1)
                    dve.wait_ge(x_in[b], 16 * (t // 2 + 1))
                    if t >= 2:
                        dve.wait_ge(x1_out[b], 16 * (t // 2))
                        dve.wait_ge(xn_out[b], 16 * (t // 2))
                        dve.wait_ge(turned, t - 1)
                    y = m.ps[:, 2 * b:2 * b + 2, :].rearrange("p b n -> p (b n)")
                    dve.tensor_tensor(x1[:, b, :], y, gates[:, s, :], ALU.mult).then_inc(y_read, 1)
                    dve.wait_ge(y_read, t + 1)
                    dve.tensor_tensor(x1[:, b, :], x1[:, b, :], xt[:, b, :], ALU.add).then_inc(x1_done, 1)
                    dve.wait_ge(sq, t + 1)
                    dve.tensor_scalar(st[:, b, 1:2], st[:, b, 0:1], 1.0 / D, EPS, ALU.mult, ALU.add).then_inc(chain, 1)
                    dve.wait_ge(sd_done, t + 1)
                    dve.reciprocal(st[:, b, 3:4], st[:, b, 2:3]).then_inc(chain, 1)
                    dve.wait_ge(chain, 2 * t + 2)
                    dve.tensor_scalar(xn[:, b, :], x1[:, b, :], st[:, b, 3:4], None, ALU.mult).then_inc(xn_done, 1)
                    dve.wait_ge(turned, t + 1)
                    if t >= 2:
                        dve.wait_ge(lg_done, t - 1)
                    for k in range(4, 8):
                        last = dve.tensor_scalar(h2[:, b, k, :], m.ps[:, 5, (k - 4) * P:(k - 3) * P],
                                                 m.comb[:, layer, 1, k, s:s + 1], m.mod[:, layer, 3, k, s:s + 1],
                                                 ALU.mult, ALU.add)
                    last.then_inc(ev_dve, 1)
                if t >= 1:
                    u = (t - 1) % 2
                    dve.wait_ge(lg_done, t)
                    if t >= 3:
                        dve.wait_ge(afft_done, t - 2)
                    link(dve.tensor_reduce(st[:, u, 4:5], m.ps[:, 6, 0:NE], AX_X, ALU.max))
                    dve.tensor_scalar(st[:, u, 5:6], st[:, u, 4:5], -1.0, None, ALU.mult).then_inc(nmax, 1)
                    dve.wait_ge(ex_done, t)
                    link(dve.reciprocal(st[:, u, 7:8], st[:, u, 6:7]))
                    dve.tensor_scalar(lg[:, u, 1, :], lg[:, u, 0, :], st[:, u, 7:8], None, ALU.mult).then_inc(aff_done, 1)


def choose_stage(nc, m, name, affT, with_context):
    sets = [(0, SEQ, CAP, m.idx, m.gate)]
    if with_context:
        sets.append((SEQ, CTX, CAPC, m.idxc, m.gatec))
    vals = m.A[0:NE, 4 * D:4 * D + CAP]
    idx = m.A[0:NE, 4 * D + 128:4 * D + 128 + CAP].bitcast(U32)
    idxf = m.A[0:NE, 4 * D + 256:4 * D + 256 + CAP]
    with stage_of(nc) as ctx:
        found, turned, copied = semaphores(nc, ctx, f"{name}_found {name}_turn {name}_copy")
        chain = semaphores(nc, ctx, f"{name}_chain")[0]
        block = ctx.enter_context(nc.Block())

        @block.vector
        def _(dve):
            links = 0

            def link(ins):
                nonlocal links
                links += 1
                ins.then_inc(chain, 1)
                dve.wait_ge(chain, links)

            for n, (t0, width, cap, idx_out, gate_out) in enumerate(sets):
                row = affT[:, t0:t0 + width]
                for i in range(cap // 8):
                    at = slice(8 * i, 8 * i + 8)
                    link(dve.max(vals[:, at], row))
                    link(dve.max_index(idx[:, at], vals[:, at], row))
                    link(dve.match_replace(row, vals[:, at], row, -1.0))
                dve.tensor_scalar(idxf[:, 0:cap], idx[:, 0:cap], float(t0), None, ALU.add).then_inc(found, 1)
                dve.wait_ge(turned, n + 1)
                dve.tensor_copy(idx_out[0:cap, 0:NE], m.ps[0:cap, 0, 0:NE]).then_inc(copied, 1)
                dve.tensor_copy(idx_out[0:cap, NE:NE + 1], m.ps[0:cap, 0, 0:1]).then_inc(copied, 1)
                dve.tensor_copy(gate_out[0:cap, :], m.ps[0:cap, 1, 0:NE]).then_inc(copied, 1)

        @block.tensor
        def _(pe):
            for n, (t0, width, cap, idx_out, gate_out) in enumerate(sets):
                pe.wait_ge(found, n + 1)
                if n:
                    pe.wait_ge(copied, 3 * n)
                pe.transpose(m.ps[0:cap, 0, 0:NE], idxf[:, 0:cap], m.ident[0:NE, 0:NE])
                pe.transpose(m.ps[0:cap, 1, 0:NE], vals[:, 0:cap], m.ident[0:NE, 0:NE]).then_inc(turned, 1)


def expert_stage(nc, m, d, name, layer, with_context):
    N = CAP + (CAPC if with_context else 0)
    PER = BANK // N
    YB = -(-K // PER)
    R = 6
    STEPS = 2 * R
    units = d["moe"]
    unit = m.ring[:, :].rearrange("p (s n) -> p s n", s=R)
    w_of = lambda r, part: unit[:, r, part * D:(part + 1) * D].rearrange("p (k n) -> p k n", k=K)
    sets = [(CAP, 0, m.idx, m.gate)] + ([(CAPC, 1, m.idxc, m.gatec)] if with_context else [])
    NS = len(sets)
    OUTS = 2 * NS
    A = m.A
    xg = [A[0:cap, s * D:(s + 1) * D] for cap, s, _, _ in sets]
    ys = [A[0:cap, (2 + s) * D:(3 + s) * D] for cap, s, _, _ in sets]
    gates = [A[0:cap, (4 + s) * D:(5 + s) * D] for cap, s, _, _ in sets]
    xe = m.B[:, 0:2 * K * N].rearrange("p (b k n) -> p b k n", b=2, k=K)
    at = 3 * D
    ysb = m.B[:, at:at + K * N].rearrange("p (k n) -> p k n", k=K)
    sa = m.B[:, at + 2 * D:at + 2 * D + 2 * N].rearrange("p (b n) -> p b n", b=2)
    h = m.B[:, at + 3 * D:at + 3 * D + 2 * N].rearrange("p (b n) -> p b n", b=2)
    gcur = m.B[:, at + 4 * D:at + 4 * D + 2]
    with stage_of(nc) as ctx:
        unit_done, au_done, sa_done, h_done, y_act, y_dve = semaphores(
            nc, ctx, " ".join(f"{name}_{x}" for x in "unit au sa h ya yd".split()))
        in_done, x_act, x_dve, out_done, out_read, ys_ready, gate_ready = semaphores(
            nc, ctx, " ".join(f"{name}_{x}" for x in "in xa xd out outr ys gcur".split()))
        gates_in, gathered, scattered = semaphores(
            nc, ctx, " ".join(f"{name}_{x}" for x in "gates gat scat".split()))
        unit_in = [semaphore(nc, ctx, f"{name}_w{r}") for r in range(R)]
        block = ctx.enter_context(nc.Block())

        def need(engine, sem, value):
            if not isinstance(value, int) or value > 0:
                engine.wait_ge(sem, value)

        def experts(engine, body):
            body(0, 0)
            body(1, 1)
            with engine.Fori(1, NE // 2) as i:
                body(i * 2, 0)
                body(i * 2 + 1, 1)

        @block.sync
        def _(sp):
            for cap, s, _, _ in sets:
                row = d["mrow"][s:s + 1, (layer * 6 + 5) * D:(layer * 6 + 6) * D]
                sp.dma_start(gates[s], row.to_broadcast((cap, D))).then_inc(gates_in, 16)

            def expert(e, b):
                for j in range(FJ):
                    if j >= R:
                        need(sp, unit_done, e * FJ + (j - R + 1))
                    else:
                        old = j + R if j + R < FJ else j
                        need(sp, unit_done, e * FJ + (old + 1 - FJ))
                    sp.dma_start(unit[:, j % R, :], units[e * FJ + j]).then_inc(unit_in[j % R], 16)
            experts(sp, expert)

        @block.gpsimd
        def _(pool):
            def gather(e):
                need(pool, in_done, e)
                for cap, s, idx, _ in sets:
                    pool.indirect_dma_start(xg[s], None, d["x_norm"], bass.IndirectOffsetOnAxis(
                        ap=idx[0:cap, e:e + 1], axis=0)).then_inc(gathered, 16)

            def scatter(e):
                pool.wait_ge(ys_ready, e + 1)
                for cap, s, idx, _ in sets:
                    pool.indirect_dma_start(d["x_res"], bass.IndirectOffsetOnAxis(ap=idx[0:cap, e:e + 1], axis=0),
                                            ys[s], None, compute_op=ALU.add).then_inc(scattered, 16)

            gather(0)
            for e in range(NE):
                gather(e + 1)
                if e:
                    scatter(e - 1)
            scatter(NE - 1)
            pool.wait_ge(scattered, 16 * NS * NE)
            pool.wait_ge(gathered, 16 * NS * (NE + 1))

        @block.tensor
        def _(pe):
            def turn_in(e):
                pe.wait_ge(gathered, e * (16 * NS) + 16 * NS)
                need(pe, out_read, e * OUTS - OUTS)
                for k in range(K):
                    mm = pe.transpose(m.ps[:, 5 + k // 4, (k % 4) * P:(k % 4 + 1) * P],
                                      xg[0][:, k * P:(k + 1) * P], m.ident[:, :])
                for k in range(K if NS > 1 else 0):
                    mm = pe.transpose(m.ps[:, 7, k * CAPC:(k + 1) * CAPC], xg[1][:, k * P:(k + 1) * P],
                                      m.ident[0:CAPC, 0:CAPC])
                mm.then_inc(in_done, 1)

            def turn_out(e):
                pe.wait_ge(y_act, e + 1)
                pe.wait_ge(y_dve, e + 1)
                for piece in range(OUTS):
                    cap, s, _, _ = sets[piece // 2]
                    if piece == 3:
                        pe.wait_ge(out_read, e * OUTS + 1)
                    for q in range(4):
                        mm = pe.transpose(m.ps[0:cap, 5 + piece % 3, q * P:(q + 1) * P],
                                          ysb[:, 4 * (piece % 2) + q, s * CAP:s * CAP + cap], m.ident[:, :])
                    mm.then_inc(out_done, 1)

            def up(e, b, j):
                if j == 0:
                    pe.wait_ge(x_act, e + 1)
                    pe.wait_ge(x_dve, e + 1)
                pe.wait_ge(unit_in[j % R], (e * 16 + 16) if j % R == R - 1 else (e * 32 + (16 + 16 * (j // R))))
                need(pe, h_done, e * FJ + (j - 1))
                for part in range(2):
                    for k in range(K):
                        mm = pe.matmul(m.ps[:, (b + j) % 2, 256 * part:256 * part + N],
                                       w_of(j % R, part)[:, k, :], xe[:, b, k, :], start=(k == 0), stop=(k == K - 1))
                mm.then_inc(au_done, 1)

            def down(e, b, j):
                pe.wait_ge(h_done, e * FJ + (j + 1))
                if j == 0:
                    need(pe, y_act, e)
                    need(pe, y_dve, e)
                w = unit[:, j % R, 2 * D:3 * D]
                for i in range(K):
                    mm = pe.matmul(m.ps[:, 2 + i // PER, (i % PER) * N:(i % PER + 1) * N], w[:, i * P:(i + 1) * P],
                                   h[:, (b + j) % 2, :], start=(j == 0 and i % PER == 0), stop=(j == FJ - 1),
                                   skip_group_check=True)
                mm.then_inc(unit_done, 1)

            def expert(e, b):
                for j in range(FJ):
                    up(e, b, j)
                    if j:
                        down(e, b, j - 1)
                    elif not isinstance(e, int) or e > 0:
                        down(e - 1, 1 - b, FJ - 1)
                    if j == 3 and (not isinstance(e, int) or e > 0):
                        turn_out(e - 1)
                    if j == 6:
                        turn_in(e + 1)

            turn_in(0)
            experts(pe, expert)
            down(NE - 1, 1, FJ - 1)
            turn_out(NE - 1)

        def copy_in(engine, e, b, half):
            engine.wait_ge(in_done, e + 1)
            need(engine, au_done, e * FJ - FJ)
            for cap, s, _, _ in sets:
                for k in range(4 * half, 4 * half + 4) if s == 0 else range(K if half else 0):
                    src = m.ps[:, 5 + half, (k % 4) * P:(k % 4 + 1) * P] if s == 0 else m.ps[:, 7, k * CAPC:(k + 1) * CAPC]
                    out = xe[:, b, k, s * CAP:s * CAP + cap]
                    gain, shift = m.comb[:, layer, 1, k, s:s + 1], m.mod[:, layer, 3, k, s:s + 1]
                    if half == 0:
                        last = engine.activation(out, src, ACT.Identity, bias=shift, scale=gain)
                    else:
                        last = engine.tensor_scalar(out, src, gain, shift, ALU.mult, ALU.add)
            last.then_inc(x_dve if half else x_act, 1)

        def copy_y(engine, e, half):
            engine.wait_ge(unit_done, e * FJ + FJ)
            need(engine, out_done, e * OUTS)
            for bank in range(half, YB, 2):
                n = min(PER, K - bank * PER)
                dst = ysb[:, bank * PER:bank * PER + n, :]
                src = m.ps[:, 2 + bank, 0:n * N].rearrange("p (k n) -> p k n", k=n)
                last = engine.tensor_copy(dst, src) if half else engine.copy(dst, src)
            last.then_inc(y_dve if half else y_act, 1)

        @block.scalar
        def _(act):
            def expert(e, b):
                for j in range(FJ):
                    act.wait_ge(au_done, e * FJ + (j + 1))
                    need(act, h_done, e * FJ + (j - 1))
                    act.activation(sa[:, (b + j) % 2, :], m.ps[:, (b + j) % 2, 0:N], ACT.Silu).then_inc(sa_done, 1)
                    if j == 0 and (not isinstance(e, int) or e > 0):
                        copy_y(act, e - 1, 0)
                    if j == 6:
                        copy_in(act, e + 1, 1 - b, 0)
            copy_in(act, 0, 0, 0)
            experts(act, expert)
            copy_y(act, NE - 1, 0)

        @block.vector
        def _(dve):
            def weigh(e):
                dve.wait_ge(gate_ready, e * NS + NS)
                need(dve, scattered, e * (16 * NS))
                for piece in range(OUTS):
                    cap, s, _, _ = sets[piece // 2]
                    half = slice((piece % 2) * BANK, (piece % 2 + 1) * BANK)
                    dve.wait_ge(out_done, e * OUTS + (piece + 1))
                    dve.scalar_tensor_tensor(ys[s][:, half], m.ps[0:cap, 5 + piece % 3, :], gcur[0:cap, s:s + 1],
                                             gates[s][:, half], ALU.mult, ALU.mult).then_inc(out_read, 1)
                dve.wait_ge(out_read, e * OUTS + OUTS)
                dve.nop().then_inc(ys_ready, 1)

            def take_gates(e):
                need(dve, out_read, e * OUTS)
                for cap, s, _, gate in sets:
                    dve.tensor_copy(gcur[0:cap, s:s + 1], gate[0:cap, bass.ds(e, 1)]).then_inc(gate_ready, 1)

            def expert(e, b):
                for j in range(FJ):
                    dve.wait_ge(sa_done, e * FJ + (j + 1))
                    need(dve, unit_done, e * FJ + (j - 1))
                    dve.tensor_tensor(h[:, (b + j) % 2, :], m.ps[:, (b + j) % 2, 256:256 + N], sa[:, (b + j) % 2, :],
                                      ALU.mult).then_inc(h_done, 1)
                    later = not isinstance(e, int) or e > 0
                    if j == 0 and later:
                        copy_y(dve, e - 1, 1)
                    if j == 2 and later:
                        take_gates(e - 1)
                    if j == 3 and later:
                        weigh(e - 1)
                    if j == 6:
                        copy_in(dve, e + 1, 1 - b, 1)
            dve.wait_ge(gates_in, 16 * NS)
            copy_in(dve, 0, 0, 1)
            experts(dve, expert)
            copy_y(dve, NE - 1, 1)
            take_gates(NE - 1)
            weigh(NE - 1)


def expert_rows_stage(nc, m, d, name, layer):
    UNITS = 4
    U = FF // UNITS
    PIECE = K * U
    assert PIECE == FJ * (D // 4)
    SLOTS = 4
    TURN = 12
    DOWN = range(2, 6)
    GROUPS = [range(0, 2), range(2, 5), range(5, 8), range(8, 11)]
    pieces = d["moe_rows"]
    with stage_of(nc) as ctx:
        sb = lambda what, shape, dt=F32: ctx.enter_context(nc.sbuf_tensor(f"{name}_{what}", shape, dt))
        raw = sb("raw_sb", [P, SLOTS, PIECE])
        high, low = sb("high_sb", [P, SLOTS, PIECE], F32R), sb("low_sb", [P, SLOTS, PIECE], F32R)
        xg, ys, gates = sb("xg_sb", [P, D]), sb("ys_sb", [P, D]), sb("gates_sb", [P, D])
        xm = sb("xm_sb", [P, D])
        x_hi, x_lo = sb("xhi_sb", [P, 2, K, P], F32R), sb("xlo_sb", [P, 2, K, P], F32R)
        h = sb("h_sb", [P, FF])
        hT_hi, hT_lo = sb("hthi_sb", [P, FJ, P], F32R), sb("htlo_sb", [P, FJ, P], F32R)
        sa = sb("sa_sb", [P, 2, U])
        gcur = sb("gcur_sb", [P, 2])
        piece_done, high_done, low_done, sa_done, h_done, h_turned, hT_high, hT_low = semaphores(
            nc, ctx, " ".join(f"{name}_{x}" for x in "piece high low sa h hturn hthi htlo".split()))
        x_turned, x_read, x_high, x_low, y_read, ys_ready, gate_ready = semaphores(
            nc, ctx, " ".join(f"{name}_{x}" for x in "xturn xread xhi xlo yread ys gcur".split()))
        gates_in, gathered, scattered, x_parts = semaphores(
            nc, ctx, " ".join(f"{name}_{x}" for x in "gates gat scat xparts".split()))
        piece_in = [semaphore(nc, ctx, f"{name}_w{r}") for r in range(SLOTS)]
        block = ctx.enter_context(nc.Block())

        def exists(e, p):
            return not isinstance(e, int) or (0 <= e < NE and not (e == 0 and p in DOWN)) or (e == NE and p in DOWN)

        def number(e, p):
            if isinstance(e, int) and e == 0 and p < DOWN[0]:
                return p + 1
            return e * TURN + (p + 1 - len(DOWN)) - (DOWN[0] if isinstance(e, int) and e == NE else 0)

        def before(e, p, places):
            while True:
                e, p = (e, p - places) if p >= places else (e - 1, p - places + TURN)
                if isinstance(e, int) and e < 0:
                    return None
                if exists(e, p):
                    return number(e, p)

        def need(engine, sem, value):
            if value is not None and (not isinstance(value, int) or value > 0):
                engine.wait_ge(sem, value)

        def turns(engine, body):
            body(0, 0)
            with engine.Fori(0, NE // 2 - 1) as i:
                body(i * 2 + 1, 1)
                body(i * 2 + 2, 0)
            body(NE - 1, 1)
            body(NE, 0)

        def later(e):
            return not isinstance(e, int) or e > 0

        def expert(e):
            return not isinstance(e, int) or e < NE

        @block.sync
        def _(sp):
            sp.dma_start(gates[:, :], d["mrow"][0:1, (layer * 6 + 5) * D:(layer * 6 + 6) * D].to_broadcast((P, D))).then_inc(gates_in, 16)

            def turn(e, b):
                for p in range(TURN):
                    if exists(e, p):
                        need(sp, low_done, before(e, p, SLOTS))
                        src = e * TURN + (p if p < 2 else p - 4 if p >= 6 else p + 6 - TURN)
                        sp.dma_start(raw[:, p % SLOTS, :], pieces[src]).then_inc(piece_in[p % SLOTS], 16)
            turns(sp, turn)

        @block.gpsimd
        def _(pool):
            def gather(e):
                need(pool, x_turned, 2 * e)
                pool.indirect_dma_start(xg[:, :], None, d["x_norm"], bass.IndirectOffsetOnAxis(
                    ap=m.idx[:, e:e + 1], axis=0)).then_inc(gathered, 16)

            def scatter(e):
                pool.wait_ge(ys_ready, 2 * e + 2)
                pool.indirect_dma_start(d["x_res"], bass.IndirectOffsetOnAxis(ap=m.idx[:, e:e + 1], axis=0),
                                        ys[:, :], None, compute_op=ALU.add).then_inc(scattered, 16)

            gather(0)
            for e in range(NE):
                if e + 1 < NE:
                    gather(e + 1)
                if e:
                    scatter(e - 1)
            scatter(NE - 1)
            pool.wait_ge(scattered, 16 * NE)
            pool.wait_ge(gathered, 16 * NE)

        @block.tensor
        def _(pe):
            def ready(e, p):
                pe.wait_ge(high_done, number(e, p))
                pe.wait_ge(low_done, number(e, p))

            def products(out, x_high_part, x_low_part, w_high_part, w_low_part, first, last):
                pe.matmul(out, x_high_part, w_high_part, start=first, stop=False)
                pe.matmul(out, x_high_part, w_low_part, start=False, stop=False)
                return pe.matmul(out, x_low_part, w_high_part, start=False, stop=last)

            def up(e, b, p, u, part):
                if part == 0 and u == 0:
                    pe.wait_ge(x_high, e + 1)
                    pe.wait_ge(x_low, e + 1)
                if part == 0:
                    need(pe, h_done, e * UNITS + (u - 1))
                ready(e, p)
                wh = high[:, p % SLOTS, :].rearrange("p (k n) -> p k n", k=K)
                wl = low[:, p % SLOTS, :].rearrange("p (k n) -> p k n", k=K)
                for k in range(K):
                    mm = products(m.ps[:, 2 * (u % 2) + part, 0:U], x_hi[:, b, k, :], x_lo[:, b, k, :],
                                  wh[:, k, :], wl[:, k, :], k == 0, k == K - 1)
                mm.then_inc(piece_done, 1)

            def down(e, p):
                q = p - DOWN[0]
                if q == 0:
                    pe.wait_ge(hT_high, e * UNITS)
                    pe.wait_ge(hT_low, e * UNITS)
                if q % 2 == 0:
                    pe.wait_ge(y_read, e * 2 + (q // 2 - 1))
                ready(e, p)
                wh = high[:, p % SLOTS, :].rearrange("p (j n) -> p j n", j=FJ)
                wl = low[:, p % SLOTS, :].rearrange("p (j n) -> p j n", j=FJ)
                n = D // 4
                for j in range(FJ):
                    mm = products(m.ps[:, 4 + q // 2, (q % 2) * n:(q % 2 + 1) * n], hT_hi[:, j, :], hT_lo[:, j, :],
                                  wh[:, j, :], wl[:, j, :], j == 0, j == FJ - 1)
                mm.then_inc(piece_done, 1)

            def turn_h(e, g):
                pe.wait_ge(h_done, e * UNITS + (g + 1))
                if g < 2 and not (isinstance(e, int) and e == NE - 1):
                    pe.wait_ge(x_read, e * 2 + (g + 3))
                elif g < 2:
                    pe.wait_ge(hT_low, e * UNITS + (g - 1))
                else:
                    pe.wait_ge(hT_low, e * UNITS + (g - 1))
                for i, j in enumerate(GROUPS[g]):
                    mm = pe.transpose(m.ps[:, 6 + (g + 1) % 2, i * P:(i + 1) * P], h[:, j * P:(j + 1) * P], m.ident[:, :])
                mm.then_inc(h_turned, 1)

            def turn_x(e):
                pe.wait_ge(gathered, e * 16 + 16)
                for half in range(2):
                    need(pe, hT_low, (e - 1) * UNITS + (half - 1))
                    for q in range(4):
                        mm = pe.transpose(m.ps[:, 7 - half, q * P:(q + 1) * P], xg[:, (4 * half + q) * P:(4 * half + q + 1) * P],
                                          m.ident[:, :])
                    mm.then_inc(x_turned, 1)

            def turn(e, b):
                if expert(e):
                    up(e, b, 0, 0, 0)
                if later(e):
                    turn_h(e - 1, 3)
                if expert(e):
                    up(e, b, 1, 0, 1)
                for p in DOWN:
                    if later(e):
                        down(e, p)
                    if p == 4 and (not isinstance(e, int) or e + 1 < NE):
                        turn_x(e + 1)
                for u in range(1, UNITS) if expert(e) else ():
                    up(e, b, 4 + 2 * u, u, 0)
                    turn_h(e, u - 1)
                    up(e, b, 5 + 2 * u, u, 1)

            turn_x(0)
            turns(pe, turn)

        @block.scalar
        def _(act):
            def split(e, p):
                if not exists(e, p):
                    return
                nth = p // SLOTS
                if isinstance(e, int) and e == 0 and p < DOWN[0]:
                    nth = 1
                elif isinstance(e, int) and e == NE:
                    nth = 0
                landed = e * 48 + 16 * nth
                act.wait_ge(piece_in[p % SLOTS], landed)
                need(act, piece_done, before(e, p, SLOTS))
                act.copy(high[:, p % SLOTS, :], raw[:, p % SLOTS, :]).then_inc(high_done, 1)

            def copy_x(e, b):
                need(act, x_low, e)
                for k in range(K):
                    if k % 4 == 0:
                        act.wait_ge(x_turned, e * 2 + (k // 4 + 1))
                    ins = act.activation(xm[:, k * P:(k + 1) * P], m.ps[:, 7 - k // 4, (k % 4) * P:(k % 4 + 1) * P],
                                         ACT.Identity, bias=m.mod[:, layer, 3, k, 0:1], scale=m.comb[:, layer, 1, k, 0:1])
                    if k % 4 == 3:
                        ins.then_inc(x_read, 1)
                act.wait_ge(x_read, e * 2 + 2)
                need(act, piece_done, number(e - 2, TURN - 1) if not isinstance(e, int) or e >= 2 else None)
                act.copy(x_hi[:, b, :, :].rearrange("p k n -> p (k n)"), xm[:, :]).then_inc(x_high, 1)

            def silu(e, p, u):
                act.wait_ge(piece_done, number(e, p))
                need(act, h_done, e * UNITS + (u - 1))
                act.activation(sa[:, u % 2, :], m.ps[:, 2 * (u % 2), 0:U], ACT.Silu).then_inc(sa_done, 1)

            def copy_h(e, g):
                act.wait_ge(h_turned, e * UNITS + (g + 1))
                if g < 3:
                    need(act, piece_done, number(e, DOWN[-1]) if later(e) else None)
                n, j = len(GROUPS[g]), GROUPS[g][0]
                act.copy(hT_hi[:, j:j + n, :].rearrange("p j n -> p (j n)"), m.ps[:, 6 + (g + 1) % 2, 0:n * P]).then_inc(hT_high, 1)

            def turn(e, b):
                for p in range(TURN):
                    if p == 0 or p in (6, 8, 10):
                        if expert(e):
                            silu(e, p, max(0, p // 2 - 2))
                    if p == 0 and later(e):
                        copy_h(e - 1, 3)
                    if p in (6, 8, 10) and expert(e):
                        copy_h(e, p // 2 - 3)
                    if p == 4 and (not isinstance(e, int) or e + 1 < NE):
                        copy_x(e + 1, 1 - b)
                    q = p + SLOTS
                    if q < TURN:
                        split(e, q)
                    elif expert(e):
                        split(e + 1, q - TURN)

            copy_x(0, 0)
            for p in range(SLOTS):
                split(0, p)
            turns(act, turn)

        @block.vector
        def _(dve):
            def split(e, p):
                if exists(e, p):
                    dve.wait_ge(high_done, number(e, p))
                    need(dve, piece_done, before(e, p, SLOTS))
                    dve.tensor_tensor(low[:, p % SLOTS, :], raw[:, p % SLOTS, :], high[:, p % SLOTS, :].bitcast(F32),
                                      ALU.subtract).then_inc(low_done, 1)

            def split_x(e, b):
                dve.wait_ge(x_high, e + 1)
                flat = lambda x: x[:, b, :, :].rearrange("p k n -> p (k n)")
                dve.tensor_tensor(flat(x_lo), xm[:, :], flat(x_hi).bitcast(F32), ALU.subtract).then_inc(x_low, 1)

            def multiply(e, p, u):
                dve.wait_ge(sa_done, e * UNITS + (u + 1))
                dve.wait_ge(piece_done, number(e, p))
                need(dve, h_turned, (e - 1) * UNITS + (min(u + 1, 3) + 1))
                dve.tensor_tensor(h[:, u * U:(u + 1) * U], m.ps[:, 2 * (u % 2) + 1, 0:U], sa[:, u % 2, :],
                                  ALU.mult).then_inc(h_done, 1)

            def split_h(e, g):
                dve.wait_ge(hT_high, e * UNITS + (g + 1))
                n, j = len(GROUPS[g]), GROUPS[g][0]
                flat = lambda x: x[:, j:j + n, :].rearrange("p j n -> p (j n)")
                dve.tensor_tensor(flat(hT_lo), m.ps[:, 6 + (g + 1) % 2, 0:n * P], flat(hT_hi).bitcast(F32),
                                  ALU.subtract).then_inc(hT_low, 1)

            def weigh(e, half):
                if half == 0:
                    dve.wait_ge(y_read, e * 2 + 2)
                    dve.tensor_copy(gcur[:, 0:1], m.gate[:, bass.ds(e, 1)]).then_inc(gate_ready, 1)
                    dve.wait_ge(gate_ready, e + 1)
                    need(dve, scattered, e * 16)
                dve.wait_ge(piece_done, number(e + 1, DOWN[2 * half + 1]))
                at = slice(half * BANK, (half + 1) * BANK)
                dve.scalar_tensor_tensor(ys[:, at], m.ps[:, 4 + half, :], gcur[:, 0:1], gates[:, at],
                                         ALU.mult, ALU.mult).then_inc(y_read, 1)
                dve.wait_ge(y_read, e * 2 + (half + 3))
                dve.nop().then_inc(ys_ready, 1)

            def turn(e, b):
                for p in range(TURN):
                    if p in (1, 7, 9, 11) and expert(e):
                        multiply(e, p, (p - 5) // 2 if p > 1 else 0)
                    if p == 0 and later(e):
                        split_h(e - 1, 3)
                    if p in (6, 8, 10) and expert(e):
                        split_h(e, p // 2 - 3)
                    if p in (3, 5) and later(e):
                        weigh(e - 1, p // 2 - 1)
                    if p == 4 and (not isinstance(e, int) or e + 1 < NE):
                        split_x(e + 1, 1 - b)
                    q = p + SLOTS
                    if q < TURN:
                        split(e, q)
                    elif expert(e):
                        split(e + 1, q - TURN)

            dve.nop().then_inc(y_read, 2)
            dve.wait_ge(gates_in, 16)
            split_x(0, 0)
            for p in range(SLOTS):
                split(0, p)
            turns(dve, turn)


def odd_mixer_stage(nc, m, d):
    hT = m.A.rearrange("p (k t) -> p k t", k=K)
    yT = m.C.rearrange("p (k t) -> p k t", k=K)
    w = m.ring[:, 0:16 * D].rearrange("p (s k n) -> p s k n", s=16, k=K)
    lw = m.B[:, 0:D].rearrange("p (b x n) -> p b x n", b=2, x=4)
    UP = TOK + 6
    UC = TOK + 3
    up = m.ring[:, 16 * D:16 * D + UP]
    uc = m.B[:, D:D + 2 * UC].rearrange("p (b n) -> p b n", b=2)
    at = D + 2 * UC
    r, ig, a, mu, h1 = (m.B[:, at + i * TOK:at + (i + 1) * TOK] for i in range(5))
    h0 = m.rope[:, :, :].rearrange("p a n -> p (a n)")[:, 0:TOK]
    coef = m.mask[:, 0:16 * 6].rearrange("p (x c) -> p x c", x=6)
    gap = UC - TOK

    plan = []
    for h in range(K + 1):
        if h < K:
            plan += [("u", h, ch) for ch in range(3)]
        if h:
            plan += [(kind, h - 1, 0, ch) for kind in ("r", "i") for ch in range(3)]
        if h < K:
            plan += [("g", h, ch) for ch in range(2)]
        if h:
            plan += [(kind, h - 1, 1, ch) for kind in ("r", "i") for ch in range(3)]

    with stage_of(nc) as ctx:
        banks = Banks(nc, ctx, "oi", plan, 8)
        w_in = [semaphore(nc, ctx, f"oi_w{g}") for g in range(4)]
        lw_in = [semaphore(nc, ctx, f"oi_lw{b}") for b in range(2)]
        u_out, conv_done, sig_done, exp_done, tanh_done, a2_done, iu_done, m2_done, mu_done = semaphores(
            nc, ctx, " ".join(f"oi_{x}" for x in "uo conv sig exp tanh a2 iu m2 mu".split()))
        scan_done, gelu_done, coef_done, chain, absexp = semaphores(
            nc, ctx, " ".join(f"oi_{x}" for x in "scan gelu coef chain absexp".split()))
        block = ctx.enter_context(nc.Block())

        @block.sync
        def _(sp):
            for g in range(4):
                sp.dma_start(m.ring[:, 4 * D * g:4 * D * (g + 1)], d["od_in"][g]).then_inc(w_in[g], 16)
            for h in range(K):
                if h >= 2:
                    last = (("i", h - 2, 1, 2))
                    sp.wait_ge(banks.done, banks.number(last))
                sp.dma_start(lw[:, h % 2, :, :], d["od_gates"][h]).then_inc(lw_in[h % 2], 16)

        @block.tensor
        def _(pe):
            for key in plan:
                kind, h, ch = key[0], key[1], key[-1]
                if banks.uses(key):
                    pe.wait_ge(banks.sem(key), banks.uses(key))
                bank = m.ps[:, banks.bank(key), :]
                t0, n = CHUNKS[ch]
                if kind in "ug":
                    slot = 2 * h + (kind == "g")
                    if kind == "u" and h % 2 == 0 and ch == 0:
                        pe.wait_ge(w_in[h // 2], 16)
                    for k in range(K):
                        mm = pe.matmul(bank[:, 0:n], w[:, slot, k, :], hT[:, k, t0:t0 + n], start=(k == 0), stop=(k == K - 1))
                else:
                    x = 2 * key[2] + (kind == "i")
                    if x == 0 and ch == 0:
                        pe.wait_ge(lw_in[h % 2], 16 * (h // 2 + 1))
                        pe.wait_ge(conv_done, h + 1)
                    c0 = t0 if ch < 2 else t0 + gap
                    mm = pe.matmul(bank[:, 0:n], lw[:, h % 2, x, :], uc[:, h % 2, c0:c0 + n], start=True, stop=True)
                mm.then_inc(banks.done, 1)

        @block.scalar
        def _(act):
            lam = m.cols[:, C_LAM:C_LAM + 16]
            act.activation(coef[:, 0, :], lam, ACT.Abs).then_inc(absexp, 1)
            act.wait_ge(absexp, 1)
            act.activation(coef[:, 1, :], coef[:, 0, :], ACT.Exp, scale=-1.0).then_inc(absexp, 1)

            def root(x):
                act.wait_ge(m2_done, x + 1)
                act.activation(mu, mu, ACT.Sqrt).then_inc(mu_done, 1)

            for key in plan:
                kind, h, ch = key[0], key[1], key[-1]
                t0, n = CHUNKS[ch]
                src = m.ps[:, banks.bank(key), 0:n]
                act.wait_ge(banks.done, banks.number(key))
                if kind == "u":
                    if ch == 0 and h:
                        act.wait_ge(conv_done, h)
                    elif ch == 0:
                        act.wait_ge(coef_done, 1)
                    c0 = t0 + 2 if ch < 2 else t0 + 5
                    act.copy(up[:, c0:c0 + n], src).then_inc(banks.sem(key), 1)
                    if ch == 2:
                        for k2 in (("u", h, 0), ("u", h, 1), key):
                            act.wait_ge(banks.sem(k2), banks.uses(k2) + 1)
                        act.nop().then_inc(u_out, 1)
                        if h >= 2:
                            root(2 * (h - 2) + 1)
                elif kind == "g":
                    act.activation(yT[:, h, t0:t0 + n], src, ACT.Gelu_apprx_tanh).then_inc(banks.sem(key), 1)
                    if ch == 1:
                        for k2 in (("g", h, 0), key):
                            act.wait_ge(banks.sem(k2), banks.uses(k2) + 1)
                        act.nop().then_inc(gelu_done, 1)
                        if h:
                            root(2 * (h - 1))
                else:
                    dr = key[2]
                    x = 2 * h + dr
                    if ch == 0 and kind == "r" and x == 2 * K - 2:
                        root(x - 1)
                    if ch == 0 and kind == "r" and x:
                        act.wait_ge(m2_done, x)
                        act.wait_ge(scan_done, x)
                    bias = C_BA if kind == "r" else C_BX
                    act.activation((r if kind == "r" else ig)[:, t0:t0 + n], src, ACT.Sigmoid,
                                   bias=m.cols[:, bias + K * dr + h:bias + K * dr + h + 1]).then_inc(banks.sem(key), 1)
                    if ch == 2:
                        for c in range(3):
                            k2 = (kind, h, dr, c)
                            act.wait_ge(banks.sem(k2), banks.uses(k2) + 1)
                        act.nop().then_inc(sig_done, 1)
                    if ch == 2 and kind == "i":
                        if x == 0:
                            act.wait_ge(coef_done, 2)
                        c = K * dr + h
                        act.activation(a, r, ACT.Exp, scale=coef[:, 4, c:c + 1]).then_inc(exp_done, 1)
                        act.wait_ge(exp_done, x + 1)
                        act.activation(r, r, ACT.Tanh, scale=coef[:, 5, c:c + 1]).then_inc(tanh_done, 1)
                        if h == K - 1:
                            root(x)

        @block.gpsimd
        def _(pool):
            for x in range(2 * K):
                h = x // 2
                pool.wait_ge(sig_done, 2 * x + 2)
                pool.wait_ge(conv_done, h + 1)
                pool.tensor_tensor(ig[:, 0:SEQ], ig[:, 0:SEQ], uc[:, h % 2, 0:SEQ], ALU.mult)
                pool.tensor_tensor(ig[:, SEQ:TOK], ig[:, SEQ:TOK], uc[:, h % 2, SEQ + gap:UC], ALU.mult).then_inc(iu_done, 1)
                pool.wait_ge(exp_done, x + 1)
                if x:
                    pool.wait_ge(scan_done, x)
                pool.tensor_tensor(mu, a, a, ALU.mult).then_inc(a2_done, 1)

        @block.vector
        def _(dve):
            links = 0

            def link(ins):
                nonlocal links
                links += 1
                ins.then_inc(chain, 1)
                dve.wait_ge(chain, links)

            dve.memset(up, 0.0).then_inc(coef_done, 1)
            dve.wait_ge(absexp, 2)
            lam = m.cols[:, C_LAM:C_LAM + 16]
            e, z, z2, p = coef[:, 1, :], coef[:, 2, :], coef[:, 3, :], coef[:, 0, :]
            link(dve.tensor_scalar(z, e, 2.0, None, ALU.add))
            link(dve.reciprocal(z2, z))
            link(dve.tensor_tensor(z, e, z2, ALU.mult))
            link(dve.tensor_tensor(z2, z, z, ALU.mult))
            link(dve.tensor_scalar(p, z2, 1.0 / 17, None, ALU.mult))
            for c in (15, 13, 11, 9, 7, 5, 3):
                link(dve.scalar_tensor_tensor(p, p, 1.0 / c, z2, ALU.add, ALU.mult))
            link(dve.scalar_tensor_tensor(p, p, 1.0, z, ALU.add, ALU.mult))
            link(dve.tensor_scalar(e, lam, -1.0, 0.0, ALU.mult, ALU.max))
            link(dve.scalar_tensor_tensor(e, p, 2.0, e, ALU.mult, ALU.add))
            link(dve.tensor_scalar(coef[:, 4, :], e, -8.0, None, ALU.mult))
            dve.tensor_scalar(coef[:, 5, :], e, 8.0, None, ALU.mult).then_inc(coef_done, 1)

            def convolve(h):
                dve.wait_ge(u_out, h + 1)
                if h >= 2:
                    dve.wait_ge(banks.done, banks.number(("i", h - 2, 1, 2)))
                    dve.wait_ge(iu_done, 2 * (h - 2) + 2)
                out = uc[:, h % 2, :]
                tap = lambda k: m.cols[:, C_ODW + K * k + h:C_ODW + K * k + h + 1]
                link(dve.tensor_scalar(out, up[:, 0:UC], tap(0), m.cols[:, C_ODB + h:C_ODB + h + 1], ALU.mult, ALU.add))
                for k in (1, 2):
                    link(dve.scalar_tensor_tensor(out, up[:, k:k + UC], tap(k), out, ALU.mult, ALU.add))
                dve.scalar_tensor_tensor(out, up[:, 3:3 + UC], tap(3), out, ALU.mult, ALU.add).then_inc(conv_done, 1)

            def recur(x):
                h, dr = x // 2, x % 2
                dve.wait_ge(a2_done, x + 1)
                dve.wait_ge(tanh_done, x + 1)
                dve.scalar_tensor_tensor(mu, mu, 1.0, r, ALU.add, ALU.mult).then_inc(m2_done, 1)
                dve.wait_ge(mu_done, x + 1)
                dve.wait_ge(iu_done, x + 1)
                link(dve.tensor_tensor(ig, ig, mu, ALU.mult))
                if dr == 0:
                    link(dve.tensor_tensor_scan(h0[:, SEQ:TOK], a[:, SEQ:TOK], ig[:, SEQ:TOK], 0.0, ALU.mult, ALU.add))
                    dve.tensor_tensor_scan(h0[:, 0:SEQ], a[:, 0:SEQ], ig[:, 0:SEQ], h0[:, TOK - 1:TOK],
                                           ALU.mult, ALU.add).then_inc(scan_done, 1)
                else:
                    dve.tensor_tensor_scan(h1[:, ::-1], a[:, ::-1], ig[:, ::-1], 0.0, ALU.mult, ALU.add).then_inc(scan_done, 1)
                    dve.wait_ge(scan_done, x + 1)
                    link(dve.tensor_tensor(h0[:, 0:SEQ], h0[:, 0:SEQ], h1[:, 0:SEQ], ALU.add))
                    dve.wait_ge(gelu_done, h + 1)
                    link(dve.tensor_tensor(yT[:, h, :], yT[:, h, :], h0[:, 0:SEQ], ALU.mult))

            convolve(0)
            for h in range(K):
                recur(2 * h)
                if h + 1 < K:
                    convolve(h + 1)
                recur(2 * h + 1)


def final_stage(nc, m, d):
    with stage_of(nc) as ctx:
        sq, ms_done, sd_done, rs_done, xn_done, out_done, g_in = semaphores(
            nc, ctx, " ".join(f"f_{x}" for x in "sq ms sd rs xn out g".split()))
        x_in = semaphores(nc, ctx, "f_x0 f_x1")
        stored = semaphores(nc, ctx, "f_o0 f_o1")
        xt = m.A[:, 0:2 * D].rearrange("p (b n) -> p b n", b=2)
        yt = m.A[:, 2 * D:4 * D].rearrange("p (b n) -> p b n", b=2)
        junk, gain = m.A[:, 4 * D:5 * D], m.A[:, 5 * D:6 * D]
        st = m.A[:, 6 * D:6 * D + 8]
        block = ctx.enter_context(nc.Block())

        @block.sync
        def _(sp):
            sp.dma_start(gain, d["final_g"].to_broadcast((P, D))).then_inc(g_in, 16)
            with sp.Fori(0, LT // 2) as i:
                for b in range(2):
                    sp.wait_ge(xn_done, i * 2 + (b + 1))
                    sp.dma_start(xt[:, b, :], d["x_res"][bass.ds((i * 2 + b) * P, P), :]).then_inc(x_in[b], 16)

        @block.scalar
        def _(act):
            with act.Fori(0, LT // 2) as i:
                for b in range(2):
                    t = i * 2 + b
                    act.wait_ge(x_in[b], i * 16 + 16)
                    act.activation(junk, xt[:, b, :], ACT.Square, accum_out=st[:, b:b + 1]).then_inc(sq, 1)
                    act.wait_ge(ms_done, t + 1)
                    act.activation(st[:, 4 + b:5 + b], st[:, 2 + b:3 + b], ACT.Sqrt).then_inc(sd_done, 1)
                    act.wait_ge(out_done, t + 1)
                    act.dma_start(d["out"][bass.ds((i * 2 + b) * P, P), :], yt[:, b, :]).then_inc(stored[b], 16)
            for b in range(2):
                act.wait_ge(stored[b], 16 * LT // 2)

        @block.vector
        def _(dve):
            dve.wait_ge(g_in, 16)
            dve.nop().then_inc(xn_done, 2)

            def tile(i, b):
                t = i * 2 + b
                dve.wait_ge(sq, t + 1)
                dve.tensor_scalar(st[:, 2 + b:3 + b], st[:, b:b + 1], 1.0 / D, EPS, ALU.mult, ALU.add).then_inc(ms_done, 1)
                dve.wait_ge(sd_done, t + 1)
                dve.reciprocal(st[:, 6 + b:7 + b], st[:, 4 + b:5 + b]).then_inc(rs_done, 1)
                dve.wait_ge(rs_done, t + 1)
                if not isinstance(i, int):
                    dve.wait_ge(stored[b], i * 16)
                dve.tensor_scalar(yt[:, b, :], xt[:, b, :], st[:, 6 + b:7 + b], None, ALU.mult).then_inc(xn_done, 1)
                dve.wait_ge(xn_done, t + 3)
                dve.tensor_tensor(yt[:, b, :], yt[:, b, :], gain, ALU.mult).then_inc(out_done, 1)

            for b in range(2):
                tile(0, b)
            with dve.Fori(1, LT // 2) as i:
                for b in range(2):
                    tile(i, b)


def build(nc, d, stop=99):
    with ExitStack() as ctx:
        m = Memory(nc, ctx)
        hT = lambda: m.A.rearrange("p (k t) -> p k t", k=K)
        affT = lambda: m.A[0:NE, 6 * D:6 * D + TOK]
        inputs = [(d["x"], 0, LT, 0), (d["ctx"], 0, NT - LT, 1)]
        stages = [
            lambda: ada_stage(nc, m, d),
            lambda: norm_stage(nc, m, "n0", 0, inputs, hT()),
            lambda: even_in_stage(nc, m, d),
            lambda: attention_stage(nc, m),
            lambda: out_stage(nc, m, d, "o0", 0, m.B.rearrange("p (k t) -> p k t", k=K), d["ev_out"],
                              [(d["x"], LT, 0), (d["ctx"], NT - LT, 1)], affT()),
            lambda: choose_stage(nc, m, "c0", affT(), True),
            lambda: expert_stage(nc, m, d, "e0", 0, True),
            lambda: norm_stage(nc, m, "n1", 1, [(d["x_res"], 0, LT, 0), (d["x_res"], SEQ, NT - LT, 1)], hT()),
            lambda: odd_mixer_stage(nc, m, d),
            lambda: out_stage(nc, m, d, "o1", 1, m.C.rearrange("p (k t) -> p k t", k=K), d["od_out"],
                              [(d["x_res"][0:SEQ, :], LT, 0)], affT()),
            lambda: choose_stage(nc, m, "c1", affT(), False),
        ]
        with m.regions(nc, "first"):
            for stage in stages[:stop]:
                stage()
        if stop > 11:
            expert_rows_stage(nc, m, d, "e1", 1)
        if stop > 12:
            with m.regions(nc, "last"):
                final_stage(nc, m, d)


def column_tiles(w):
    n = w.shape[-1] // P
    return w.reshape(K, P, n, P).transpose(2, 1, 0, 3)


def constants():
    f = np.arange(P) % 16
    inv = (10000.0 ** (-np.arange(16, dtype=np.float32) / 16)).astype(np.float32)[f]
    t = np.arange(SEQ)
    pos = np.where(((np.arange(P) % DH) < DH // 2)[:, None], (t // GRID_W)[None, :], (t % GRID_W)[None, :])
    ang = (pos.astype(np.float32) * inv[:, None]).astype(np.float32)
    rope = np.stack([np.cos(ang), np.sin(ang)], axis=1).astype(np.float32)
    rot = np.zeros((P, P), np.float32)
    for i in range(P):
        if i % 32 < 16:
            rot[i + 16, i] = -1.0
        else:
            rot[i - 16, i] = 1.0
    i, j = np.arange(P)[:, None], np.arange(P)[None, :]
    mask = np.zeros((P, 5 * P), np.float32)
    mask[:, 0:P] = np.where(j >= i, 0.0, NEG / DH ** -0.5)
    mask[:, 4 * P:5 * P] = np.where(j <= i, 0.0, NEG / DH ** -0.5)
    return {"rope": rope, "rot": rot, "mask": mask, "ident": np.eye(P, dtype=np.float32)}


def lay_out(x, c, ctx, c_ctx, ada_w, ada_b, norm_mix_g, norm_ffn_g, ev_w_in, ev_w_out, ev_sink, ev_conv_w,
            ev_conv_b, od_w_in, od_w_out, od_conv_w, od_conv_b, od_wa, od_ba, od_wx, od_bx, od_lambda,
            router_w, w_gate, w_up, w_down, final_g):
    col = lambda v: v.reshape(-1, P)
    cond = np.stack([c.reshape(K, P), c_ctx.reshape(K, P)], axis=1)
    cols = np.concatenate([col(v) for v in (cond, norm_mix_g, norm_ffn_g, ev_conv_w, ev_conv_b, od_conv_w,
                                            od_conv_b, od_ba, od_bx, od_lambda)]).T
    pair = lambda w: w.reshape(w.shape[0], NKV, QPK, DH).transpose(0, 2, 1, 3).reshape(w.shape[0], -1)
    w = ev_w_in[0]
    t = column_tiles(np.concatenate([pair(w[:, 0:512]), w[:, 512:]], axis=1))
    order = [0, 1, 2, 3, 4, 5] + [b + c for c in range(CB) for b in (10, 14, 6)]
    ev_in = t[order].reshape(6, 3, P, D).transpose(0, 2, 1, 3).reshape(6, P, 3 * D)
    wo = ev_w_out[0]
    wo = np.concatenate([pair(wo[0:512].T).T, wo[512:]])
    t = column_tiles(od_w_in[0])
    order = [x for h in range(K) for x in (K + h, h)]
    od_in = t[order].reshape(4, 4, P, D).transpose(0, 2, 1, 3).reshape(4, P, 4 * D)
    rows = lambda w: w.reshape(K, P, D).transpose(1, 0, 2)
    gates = np.stack([od_wa[0, 0], od_wx[0, 0], od_wa[0, 1], od_wx[0, 1]], axis=2)
    up = lambda w: w.reshape(NE, K, P, FJ, P).transpose(0, 3, 2, 1, 4).reshape(NE * FJ, P, D)
    moe = np.concatenate([up(w_gate[0]), up(w_up[0]), w_down[0].reshape(NE * FJ, P, D)], axis=2)
    U = FF // 4
    up = lambda w: w.reshape(NE, K, P, 4, U).transpose(0, 3, 2, 1, 4).reshape(NE, 4, 1, P, K * U)
    down = w_down[1].reshape(NE, FJ, P, 4, D // 4).transpose(0, 3, 2, 1, 4).reshape(NE, 4, P, K * U)
    moe_rows = np.concatenate([np.concatenate([up(w_gate[1]), up(w_up[1])], axis=2).reshape(NE, 8, P, K * U), down],
                              axis=1).reshape(NE * 12, P, K * U)
    ada = ada_w.reshape(2, K, P, 12, BANK).transpose(0, 3, 2, 1, 4).reshape(24, P, K, BANK)
    router = router_w.reshape(2, K, P, NE).transpose(0, 2, 1, 3)
    return {"x": x[0], "ctx": ctx[0], "cols": cols, "ada_w": ada, "ada_b": ada_b, "ev_in": ev_in,
            "ev_out": rows(wo), "ev_sink": ev_sink, "od_in": od_in, "od_out": rows(od_w_out[0]),
            "od_gates": gates, "router_w": router, "moe": moe, "moe_rows": moe_rows, "final_g": final_g.reshape(1, D), **constants()}


def kernel(_stop=99, **inputs):
    import concourse.bacc as bacc
    from concourse.bass_utils import run_bass_kernel_spmd

    nc = bacc.Bacc("TRN2", target_bir_lowering=False, num_devices=1)
    arrays = {f"in_{k}": np.ascontiguousarray(a) for k, a in lay_out(**{k: np.asarray(v) for k, v in inputs.items()}).items()}
    d = {k[3:]: nc.dram_tensor(k, a.shape, F32, kind="ExternalInput").ap() for k, a in arrays.items()}
    d["out"] = nc.dram_tensor("out", (SEQ, D), F32, kind="ExternalOutput").ap()
    d["x_res"] = nc.dram_tensor("x_res", (TOK, D), F32, kind="Internal").ap()
    d["x_norm"] = nc.dram_tensor("x_norm", (TOK, D), F32, kind="Internal").ap()
    d["mrow"] = nc.dram_tensor("mrow", (2, 12 * D), F32, kind="Internal").ap()
    build(nc, d, _stop)
    result = run_bass_kernel_spmd(nc, [arrays], core_ids=[0])
    return result.results[0]["out"].reshape(1, SEQ, D)
```

```python
from contextlib import ExitStack, contextmanager

import numpy as np

import concourse.bass as bass
from concourse import mybir

F32 = mybir.dt.float32
F32R = mybir.dt.float32r
U32 = mybir.dt.uint32
ALU = mybir.AluOpType
ACT = mybir.ActivationFunctionType
AX_X = mybir.AxisListType.X

P = 128
D = 1024
K = D // P
SEQ = 1024
CTX = 256
TOK = SEQ + CTX
LT = SEQ // P
NT = TOK // P
EPS = 1e-6
DH = 64
NKV = 2
QPK = 4
GRID_W = 64
NE = 16
FF = 1408
FJ = FF // P
CAP = 2 * SEQ // NE
CAPC = 2 * CTX // NE
NEG = -1e30
CB = D // 2 // P
BANK = 512
CHUNKS = [(0, 512), (512, 512), (SEQ, CTX)]

C_COND, C_GMIX, C_GFFN = 0, 16, 32
C_EVW, C_EVB, C_ODW, C_ODB = 48, 60, 64, 96
C_BA, C_BX, C_LAM, C_ALL = 104, 120, 136, 152


class Memory:

    def __init__(self, nc, ctx):
        sb = lambda name, shape, dt=F32: ctx.enter_context(nc.sbuf_tensor(name, shape, dt))
        self.cols = sb("cols", [P, C_ALL])
        self.ident = sb("ident_sb", [P, P])
        self.rope = sb("rope_sb", [P, 2, SEQ])
        self.mask = sb("mask_sb", [P, 5 * P])
        self.mod = sb("mod", [P, 2, 6, K, 2])
        self.comb = sb("comb", [P, 2, 2, K, 2])
        self.sink = sb("sink_sb", [P, 8])
        self.idx = sb("idx", [P, NE + 1], U32)
        self.idxc = sb("idxc", [P, NE + 1], U32)
        self.gate = sb("gate", [P, NE])
        self.gatec = sb("gatec", [P, NE])
        self.ps = ctx.enter_context(nc.psum_tensor("ps", [P, 8, BANK], F32))

    @contextmanager
    def regions(self, nc, name):
        with ExitStack() as ctx:
            self.B = ctx.enter_context(nc.sbuf_tensor(f"B_{name}", [P, 10 * D], F32))
            self.C = ctx.enter_context(nc.sbuf_tensor(f"C_{name}", [P, 8 * D], F32))
            yield

    @contextmanager
    def plain(self, nc, name):
        with ExitStack() as ctx:
            self.ring = ctx.enter_context(nc.sbuf_tensor(f"ring_{name}", [P, 18 * D], F32))
            self.A = ctx.enter_context(nc.sbuf_tensor(f"A_{name}", [P, 10 * D], F32))
            yield

    @contextmanager
    def for_rows(self, nc, name):
        with ExitStack() as ctx:
            self.rows = RowBuffers(nc, ctx)
            yield

    @contextmanager
    def split(self, nc, name):
        with ExitStack() as ctx:
            sb = lambda what, shape, dt: ctx.enter_context(nc.sbuf_tensor(f"{what}_{name}", shape, dt))
            self.h_hi, self.h_lo = sb("h_hi", [P, K, TOK], F32R), sb("h_lo", [P, K, TOK], F32R)
            self.w_raw = sb("w_raw", [P, 2, D], F32)
            self.w_hi, self.w_lo = sb("w_hi", [P, 2, D], F32R), sb("w_lo", [P, 2, D], F32R)
            self.border = sb("border", [P, TOK + 6], F32)
            yield


@contextmanager
def stage_of(nc):
    with ExitStack() as ctx:
        ctx.taken = []
        ctx.callback(nc.all_engine_barrier)
        ctx.callback(lambda: nc.clear_and_free_semaphores(ctx.taken))
        yield ctx


def semaphore(nc, ctx, name):
    ctx.taken.append(nc.alloc_semaphore(name))
    return ctx.taken[-1]


def semaphores(nc, ctx, names):
    return [semaphore(nc, ctx, n) for n in names.split()]


class AdaUnits:
    UNITS, SLOTS = 12, 4

    def __init__(self, nc, ctx, m, d, layer, bank0):
        self.m, self.d, self.layer, self.bank0 = m, d, layer, bank0
        self.w = m.ring[:, 0:self.SLOTS * 4 * D].rearrange("p (s k n) -> p s k n", s=self.SLOTS, k=K)
        self.bias = m.B[0:2, 0:6 * D]
        self.product_rows = m.C[0:2, 0:2 * BANK].rearrange("p (b n) -> p b n", b=2)
        self.rows = m.C[0:2, 2 * BANK:4 * BANK].rearrange("p (b n) -> p b n", b=2)
        self.columns = m.mod[:, layer, :, :, :].rearrange("p j k s -> p (j k) s")
        self.bias_in, self.mm_done, self.copied, self.row_done, self.turned, self.col_done, self.comb_done = semaphores(
            nc, ctx, " ".join(f"a{layer}_{x}" for x in "bias mm copy row turn col comb".split()))
        self.stored = [semaphore(nc, ctx, f"a{layer}_st{b}") for b in range(2)]
        self.unit_in = [semaphore(nc, ctx, f"a{layer}_unit{s}") for s in range(self.SLOTS)]

    def units(self, engine, body):
        for s in range(self.SLOTS):
            body(s, 0, s)
        with engine.Fori(1, self.UNITS // self.SLOTS) as i:
            for s in range(self.SLOTS):
                body(i * self.SLOTS + s, i, s)

    @staticmethod
    def need(engine, sem, value):
        if not isinstance(value, int) or value > 0:
            engine.wait_ge(sem, value)

    def on_sync(self, sp):
        row = self.d["ada_b"][self.layer:self.layer + 1, :]
        sp.dma_start(self.bias, row.to_broadcast((2, 6 * D))).then_inc(self.bias_in, 16)

        def unit(n, i, s):
            self.need(sp, self.mm_done, n - 3)
            sp.dma_start(self.w[:, s, :, :], self.d["ada_w"][n + self.layer * self.UNITS]).then_inc(self.unit_in[s], 16)
        self.units(sp, unit)

    def on_tensor(self, pe):
        m = self.m
        cond = m.cols[:, C_COND:C_COND + 2 * K]

        def turn(n, b):
            pe.wait_ge(self.row_done, n + 1)
            self.need(pe, self.col_done, n - 1)
            for q in range(4):
                mm = pe.matmul(m.ps[:, self.bank0 + 2 + b, 2 * q:2 * q + 2], self.rows[:, b, q * P:(q + 1) * P],
                               m.ident[0:2, 0:2], start=True, stop=True)
            mm.then_inc(self.turned, 1)

        def unit(n, i, s):
            pe.wait_ge(self.unit_in[s], i * 16 + 16)
            self.need(pe, self.copied, n - 1)
            for k in range(K):
                mm = pe.matmul(m.ps[0:2, self.bank0 + s % 2, :], cond[:, 2 * k:2 * k + 2], self.w[:, s, k, :],
                               start=(k == 0), stop=(k == K - 1))
            mm.then_inc(self.mm_done, 1)
            if not isinstance(n, int) or n > 0:
                turn(n - 1, 1 - s % 2)
        self.units(pe, unit)
        turn(self.UNITS - 1, 1)

    def on_scalar(self, act):
        m = self.m

        def leave(n, b):
            act.wait_ge(self.turned, n + 1)
            act.copy(self.columns[:, bass.ds(n * 4, 4), :],
                     m.ps[:, self.bank0 + 2 + b, 0:8].rearrange("p (q s) -> p q s", s=2)).then_inc(self.col_done, 1)
            act.dma_start(self.d["mrow"][:, bass.ds((n + self.layer * self.UNITS) * BANK, BANK)],
                          self.rows[:, b, :]).then_inc(self.stored[b], 16)

        def unit(n, i, s):
            act.wait_ge(self.mm_done, n + 1)
            self.need(act, self.row_done, n - 1)
            act.copy(self.product_rows[:, s % 2, :], m.ps[0:2, self.bank0 + s % 2, :]).then_inc(self.copied, 1)
            if not isinstance(n, int) or n > 0:
                leave(n - 1, 1 - s % 2)
        self.units(act, unit)
        leave(self.UNITS - 1, 1)
        for b in range(2):
            act.wait_ge(self.stored[b], 16 * self.UNITS // 2)

    def on_gpsimd(self, pool):
        pool.wait_ge(self.bias_in, 16)

        def unit(n, i, s):
            pool.wait_ge(self.copied, n + 1)
            self.need(pool, self.turned, n - 1)
            self.need(pool, self.stored[s % 2], i * 32 + (16 * (s // 2)))
            pool.tensor_tensor(self.rows[:, s % 2, :], self.product_rows[:, s % 2, :], self.bias[:, bass.ds(n * BANK, BANK)],
                               ALU.add).then_inc(self.row_done, 1)
        self.units(pool, unit)

    def on_vector(self, dve):
        dve.wait_ge(self.col_done, self.UNITS)
        m, l = self.m, self.layer
        for part, gain in ((1, C_GMIX), (4, C_GFFN)):
            g = m.cols[:, gain + K * l:gain + K * (l + 1)]
            for s in range(2):
                dve.scalar_tensor_tensor(m.comb[:, l, part // 4, :, s], m.mod[:, l, part, :, s], 1.0, g,
                                         ALU.add, ALU.mult).then_inc(self.comb_done, 1)


def ada_stage(nc, m, d):
    with stage_of(nc) as ctx:
        cols_in, ident_in, consts_in, silu_done = semaphores(nc, ctx, "a_cols a_ident a_consts a_silu")
        ada = AdaUnits(nc, ctx, m, d, 0, 0)
        cond = m.cols[:, C_COND:C_COND + 2 * K]
        block = ctx.enter_context(nc.Block())

        @block.sync
        def _(sp):
            ada.on_sync(sp)
            sp.dma_start(m.rope[:, :, :], d["rope"]).then_inc(consts_in, 16)
            sp.dma_start(m.mask[:, :], d["mask"]).then_inc(consts_in, 16)
            sp.dma_start(m.sink[:, :], d["ev_sink"].to_broadcast((P, 8))).then_inc(consts_in, 16)
            sp.wait_ge(consts_in, 48)

        @block.scalar
        def _(act):
            act.dma_start(m.cols[:, :], d["cols"]).then_inc(cols_in, 16)
            act.dma_start(m.ident[:, :], d["ident"]).then_inc(ident_in, 16)
            act.wait_ge(cols_in, 16)
            act.activation(cond, cond, ACT.Silu).then_inc(silu_done, 1)
            ada.on_scalar(act)

        @block.tensor
        def _(pe):
            pe.wait_ge(silu_done, 1)
            pe.wait_ge(ident_in, 16)
            ada.on_tensor(pe)

        @block.gpsimd
        def _(pool):
            ada.on_gpsimd(pool)

        @block.vector
        def _(dve):
            ada.on_vector(dve)


def norm_stage(nc, m, name, layer, sources):
    tiles = [(src, first + i * P, s) for src, first, n, s in sources for i in range(n)]
    with stage_of(nc) as ctx:
        sq, ms_done, sd_done, rs_done, xn_done, turned, xm_act, xm_dve, high_done, low_done = semaphores(
            nc, ctx, " ".join(f"{name}_{x}" for x in "sq ms sd rs xn turn xma xmd high low".split()))
        x_in = [semaphore(nc, ctx, f"{name}_x{b}") for b in range(2)]
        pair = lambda i: m.B[:, i * D:(i + 2) * D].rearrange("p (b n) -> p b n", b=2)
        xt, xn, xm = pair(0), pair(2), pair(4)
        junk = m.B[:, 6 * D:7 * D]
        st = m.B[:, 7 * D:7 * D + 8]
        block = ctx.enter_context(nc.Block())

        def need(engine, sem, value):
            if value > 0:
                engine.wait_ge(sem, value)

        @block.sync
        def _(sp):
            for t, (src, row, s) in enumerate(tiles):
                need(sp, xn_done, t - 1)
                sp.dma_start(xt[:, t % 2, :], src[row:row + P, :]).then_inc(x_in[t % 2], 16)

        @block.scalar
        def _(act):
            def square(t):
                act.wait_ge(x_in[t % 2], 16 * (t // 2 + 1))
                act.activation(junk, xt[:, t % 2, :], ACT.Square, accum_out=st[:, t % 2:t % 2 + 1]).then_inc(sq, 1)

            def root(t):
                b = t % 2
                act.wait_ge(ms_done, t + 1)
                act.activation(st[:, 4 + b:5 + b], st[:, 2 + b:3 + b], ACT.Sqrt).then_inc(sd_done, 1)

            square(0)
            root(0)
            for t, (_, _, s) in enumerate(tiles):
                b = t % 2
                if t + 1 < len(tiles):
                    square(t + 1)
                act.wait_ge(turned, t + 1)
                need(act, low_done, t - 1)
                for k in range(4):
                    last = act.activation(xm[:, b, k * P:(k + 1) * P], m.ps[:, 2 * b, k * P:(k + 1) * P],
                                          ACT.Identity, bias=m.mod[:, layer, 0, k, s:s + 1],
                                          scale=m.comb[:, layer, 0, k, s:s + 1])
                last.then_inc(xm_act, 1)
                if t + 1 < len(tiles):
                    root(t + 1)
                act.wait_ge(xm_act, t + 1)
                act.wait_ge(xm_dve, t + 1)
                act.copy(m.h_hi[:, :, t * P:(t + 1) * P], xm[:, b, :].rearrange("p (k n) -> p k n", k=K)).then_inc(high_done, 1)

        @block.vector
        def _(dve):
            def mean(t):
                b = t % 2
                dve.wait_ge(sq, t + 1)
                dve.tensor_scalar(st[:, 2 + b:3 + b], st[:, b:b + 1], 1.0 / D, EPS, ALU.mult, ALU.add).then_inc(ms_done, 1)

            def normalise(t):
                b = t % 2
                dve.wait_ge(sd_done, t + 1)
                dve.reciprocal(st[:, 6 + b:7 + b], st[:, 4 + b:5 + b]).then_inc(rs_done, 1)
                dve.wait_ge(rs_done, t + 1)
                need(dve, turned, t - 1)
                dve.tensor_scalar(xn[:, b, :], xt[:, b, :], st[:, 6 + b:7 + b], None, ALU.mult).then_inc(xn_done, 1)

            mean(0)
            normalise(0)
            for t, (_, _, s) in enumerate(tiles):
                b = t % 2
                if t + 1 < len(tiles):
                    mean(t + 1)
                dve.wait_ge(turned, t + 1)
                for k in range(4, 8):
                    last = dve.tensor_scalar(xm[:, b, k * P:(k + 1) * P], m.ps[:, 2 * b + 1, (k - 4) * P:(k - 3) * P],
                                             m.comb[:, layer, 0, k, s:s + 1], m.mod[:, layer, 0, k, s:s + 1],
                                             ALU.mult, ALU.add)
                last.then_inc(xm_dve, 1)
                if t + 1 < len(tiles):
                    normalise(t + 1)
                dve.wait_ge(high_done, t + 1)
                at = slice(t * P, (t + 1) * P)
                dve.tensor_tensor(m.h_lo[:, :, at], xm[:, b, :].rearrange("p (k n) -> p k n", k=K),
                                  m.h_hi[:, :, at].bitcast(F32), ALU.subtract).then_inc(low_done, 1)

        @block.tensor
        def _(pe):
            for t in range(len(tiles)):
                b = t % 2
                pe.wait_ge(xn_done, t + 1)
                need(pe, xm_act, t - 1)
                need(pe, xm_dve, t - 1)
                for k in range(K):
                    mm = pe.transpose(m.ps[:, 2 * b + k // 4, (k % 4) * P:(k % 4 + 1) * P],
                                      xn[:, b, k * P:(k + 1) * P], m.ident[:, :])
                mm.then_inc(turned, 1)


class Banks:

    def __init__(self, nc, ctx, name, plan, n, first=0):
        self.n, self.first = n, first
        self.at = {key: i for i, key in enumerate(plan)}
        assert len(self.at) == len(plan)
        self.free = [semaphore(nc, ctx, f"{name}_bank{b}") for b in range(n)]
        self.done = semaphore(nc, ctx, f"{name}_mm")

    def bank(self, key):
        return self.first + self.at[key] % self.n

    def sem(self, key):
        return self.free[self.at[key] % self.n]

    def uses(self, key):
        return self.at[key] // self.n

    def number(self, key):
        return self.at[key] + 1


class SplitTiles:

    def __init__(self, nc, ctx, name, m, tiles, banks, last):
        self.m, self.tiles, self.banks, self.last = m, tiles, banks, last
        self.high_done, self.low_done = semaphores(nc, ctx, f"{name}_whigh {name}_wlow")
        self.landed = [semaphore(nc, ctx, f"{name}_w{b}") for b in range(2)]

    def used(self, engine, n):
        if n >= 2:
            engine.wait_ge(self.banks.done, self.banks.number(self.last[n - 2]))

    def load(self, sp, n):
        if n >= 2:
            sp.wait_ge(self.low_done, n - 1)
        sp.dma_start(self.m.w_raw[:, n % 2, :], self.tiles[n]).then_inc(self.landed[n % 2], 16)

    def high(self, act, n):
        act.wait_ge(self.landed[n % 2], 16 * (n // 2 + 1))
        self.used(act, n)
        act.copy(self.m.w_hi[:, n % 2, :], self.m.w_raw[:, n % 2, :]).then_inc(self.high_done, 1)

    def low(self, pool, n):
        pool.wait_ge(self.high_done, n + 1)
        self.used(pool, n)
        pool.tensor_tensor(self.m.w_lo[:, n % 2, :], self.m.w_raw[:, n % 2, :], self.m.w_hi[:, n % 2, :].bitcast(F32),
                           ALU.subtract).then_inc(self.low_done, 1)

    def products(self, pe, out, n, t0, width):
        pe.wait_ge(self.high_done, n + 1)
        pe.wait_ge(self.low_done, n + 1)
        m = self.m
        for k in range(K):
            wh, wl = (w[:, n % 2, k * P:(k + 1) * P] for w in (m.w_hi, m.w_lo))
            xh, xl = (x[:, k, t0:t0 + width] for x in (m.h_hi, m.h_lo))
            pe.matmul(out, wh, xh, start=(k == 0), stop=False)
            pe.matmul(out, wh, xl, start=False, stop=False)
            mm = pe.matmul(out, wl, xh, start=False, stop=(k == K - 1))
        return mm


def even_in_stage(nc, m, d):
    cat = m.B.rearrange("p (k t) -> p k t", k=K)
    q = m.C[:, 0:4 * TOK].rearrange("p (j t) -> p j t", j=4)
    kk = m.C[:, 4 * TOK:5 * TOK]
    v = m.C[:, 5 * TOK:6 * TOK].rearrange("p (t c) -> p t c", t=NT)
    tmp = m.C[:, 6 * TOK:6 * TOK + BANK]
    gcb = m.B[:, 0:TOK]
    WP = TOK + 4
    prod = m.B[:, TOK:TOK + WP]
    acc = m.B[:, TOK + WP:TOK + WP + TOK + 2]
    at = 2 * TOK + WP + 2
    qraw = m.B[:, at:at + 2 * BANK].rearrange("p (b n) -> p b n", b=2)
    rot = m.B[:, 4900:4900 + P]
    tile = lambda kind, c: {"qk": c, "vT": 5, "gc": 6 + 3 * c, "u": 7 + 3 * c, "gb": 8 + 3 * c}[kind]
    place = lambda c0: c0 + 1 if c0 < SEQ else c0 + 3
    after = lambda c0: c0 if c0 < SEQ else c0 + 2

    plan = []
    for j in range(5):
        plan += [("qk", j, 0), ("qk", j, 1), ("rot", j, 0), ("qk", j, 2), ("rot", j, 1)]
    plan += [("vT", 0, ch) for ch in range(3)] + [("v", g, 0) for g in range(3)]
    for c in range(CB):
        plan += [(kind, c, ch) for kind in ("gc", "u", "gb") for ch in range(3)]

    with stage_of(nc) as ctx:
        banks = Banks(nc, ctx, "ei", plan, 6)
        reads = [k for k in plan if k[0] not in ("rot", "v")]
        last = [[k for k in reads if tile(k[0], k[1]) == n][-1] for n in range(18)]
        weights = SplitTiles(nc, ctx, "ei", m, d["ev_in"], banks, last)
        vt_ready = semaphore(nc, ctx, "ei_vt")
        rot_in, qraw_ready, roped, gc_ready, prod_done, chain = semaphores(
            nc, ctx, "ei_rot ei_qraw ei_roped ei_gc ei_prod ei_chain")
        block = ctx.enter_context(nc.Block())

        @block.sync
        def _(sp):
            sp.dma_start(rot, d["rot"]).then_inc(rot_in, 16)
            for n in range(18):
                weights.load(sp, n)

        @block.gpsimd
        def _(pool):
            for n in range(18):
                weights.low(pool, n)

        @block.tensor
        def _(pe):
            seen = set()
            for key in plan:
                kind, c, ch = key
                if banks.uses(key):
                    pe.wait_ge(banks.sem(key), banks.uses(key))
                bank = m.ps[:, banks.bank(key), :]
                if kind == "rot":
                    if not seen & {"rot"}:
                        pe.wait_ge(rot_in, 16)
                        seen.add("rot")
                    pe.wait_ge(qraw_ready, 2 * c + ch + 1)
                    pe.matmul(bank, rot, qraw[:, ch, :], start=True, stop=True).then_inc(banks.done, 1)
                    continue
                if kind == "v":
                    pe.wait_ge(vt_ready, 3)
                    for i, t in enumerate(range(4 * c, min(4 * c + 4, NT))):
                        mm = pe.transpose(bank[:, i * P:(i + 1) * P], gcb[:, t * P:(t + 1) * P], m.ident[:, :])
                    mm.then_inc(banks.done, 1)
                    continue
                t0, n = CHUNKS[ch]
                weights.products(pe, bank[:, 0:n], tile(kind, c), t0, n).then_inc(banks.done, 1)

        @block.scalar
        def _(act):
            weights.high(act, 0)
            weights.high(act, 1)
            for key in plan:
                kind, c, ch = key
                if key in last and last.index(key) + 2 < 18:
                    weights.high(act, last.index(key) + 2)
                if kind not in ("qk", "vT", "v", "gc"):
                    continue
                t0, n = CHUNKS[ch]
                src = m.ps[:, banks.bank(key), 0:n]
                act.wait_ge(banks.done, banks.number(key))
                if kind == "vT":
                    act.copy(gcb[:, t0:t0 + n], src).then_inc(banks.sem(key), 1)
                    act.wait_ge(banks.sem(key), banks.uses(key) + 1)
                    act.nop().then_inc(vt_ready, 1)
                elif kind == "v":
                    tiles = min(4, NT - 4 * c)
                    act.copy(v[:, 4 * c:4 * c + tiles, :], m.ps[:, banks.bank(key), 0:tiles * P].rearrange(
                        "p (t c) -> p t c", t=tiles)).then_inc(banks.sem(key), 1)
                elif kind == "gc":
                    if c and ch == 0:
                        act.wait_ge(prod_done, 3 * c)
                    act.copy(gcb[:, t0:t0 + n], src).then_inc(banks.sem(key), 1)
                    if ch == 2:
                        act.wait_ge(banks.sem(key), banks.uses(key) + 1)
                        act.nop().then_inc(gc_ready, 1)
                elif ch == 2:
                    dst = q[:, c, t0:t0 + n] if c < 4 else kk[:, t0:t0 + n]
                    act.copy(dst, src).then_inc(banks.sem(key), 1)
                else:
                    if c:
                        act.wait_ge(roped, 2 * (c - 1) + ch + 1)
                    act.copy(qraw[:, ch, :], src).then_inc(banks.sem(key), 1)
                    act.wait_ge(banks.sem(key), banks.uses(key) + 1)
                    act.nop().then_inc(qraw_ready, 1)

        @block.vector
        def _(dve):
            links = 0

            def link(ins):
                nonlocal links
                links += 1
                ins.then_inc(chain, 1)
                dve.wait_ge(chain, links)

            link(dve.memset(prod, 0.0))
            for key in plan:
                kind, c, ch = key
                if kind not in ("rot", "u", "gb"):
                    continue
                t0, n = CHUNKS[ch]
                src = m.ps[:, banks.bank(key), 0:n]
                dve.wait_ge(banks.done, banks.number(key))
                if kind == "rot":
                    dst = q[:, c, t0:t0 + n] if c < 4 else kk[:, t0:t0 + n]
                    link(dve.tensor_tensor(qraw[:, ch, :], qraw[:, ch, :], m.rope[:, 0, t0:t0 + n], ALU.mult))
                    dve.tensor_tensor(tmp, src, m.rope[:, 1, t0:t0 + n], ALU.mult).then_inc(banks.sem(key), 1)
                    dve.wait_ge(banks.sem(key), banks.uses(key) + 1)
                    dve.tensor_tensor(dst, qraw[:, ch, :], tmp, ALU.add).then_inc(roped, 1)
                    dve.wait_ge(roped, 2 * c + ch + 1)
                elif kind == "u":
                    dve.wait_ge(gc_ready, c + 1)
                    dve.tensor_tensor(prod[:, place(t0):place(t0) + n], src, gcb[:, t0:t0 + n], ALU.mult).then_inc(
                        banks.sem(key), 1)
                    dve.wait_ge(banks.sem(key), banks.uses(key) + 1)
                    dve.nop().then_inc(prod_done, 1)
                    if ch == 2:
                        tap = lambda k: m.cols[:, C_EVW + 4 * k + c:C_EVW + 4 * k + c + 1]
                        link(dve.tensor_scalar(acc, prod[:, 0:TOK + 2], tap(0), m.cols[:, C_EVB + c:C_EVB + c + 1],
                                               ALU.mult, ALU.add))
                        for k in (1, 2):
                            link(dve.scalar_tensor_tensor(acc, prod[:, k:k + TOK + 2], tap(k), acc, ALU.mult, ALU.add))
                else:
                    dve.tensor_tensor(cat[:, 4 + c, t0:t0 + n], src, acc[:, after(t0):after(t0) + n],
                                      ALU.mult).then_inc(banks.sem(key), 1)


def attention_stage(nc, m, d):
    cat = m.B.rearrange("p (k t) -> p k t", k=K)
    q = m.C[:, 0:4 * TOK].rearrange("p (j t) -> p j t", j=4)
    kk = m.C[:, 4 * TOK:5 * TOK]
    v = m.C[:, 5 * TOK:6 * TOK].rearrange("p (t c) -> p t c", t=NT)
    W = 5 * P
    s = m.A[:, 0:2 * QPK * W].rearrange("p (b j n) -> p b j n", b=2, j=QPK)
    pt = m.ring[:, 0:2 * 5 * BANK].rearrange("p (b c n) -> p b c n", b=2, c=5)
    small = m.ring[:, 6 * D:6 * D + 128].rearrange("p (b x j) -> p b x j", b=2, j=4)
    steps = [(n, kv) for n in range(NT) for kv in range(NKV)]

    def span(n):
        if n >= LT:
            return P, 3 * P
        return (P if n == 0 else 0), (4 * P if n == LT - 1 else 5 * P)

    def key_tile(n, c):
        return {0: n - 1, 1: LT, 2: LT + 1, 3: n, 4: n + 1}[c]

    def order(g):
        a, b = span(steps[g][0])
        turns = [("turn", c) for c in range(a // P, b // P)]
        heads = [("score", j) for j in range(QPK)] if g + 1 < len(steps) else []
        return heads[0:2] + turns[0:2] + heads[2:3] + turns[2:4] + heads[3:4] + turns[4:]

    with stage_of(nc) as ctx:
        sc_done, pt_done, o_done = semaphores(nc, ctx, "at_sc at_pt at_o")
        sc_free = semaphores(nc, ctx, "at_scf0 at_scf1")
        pt_free = semaphores(nc, ctx, "at_ptf0 at_ptf1")
        pt_act, pt_dve, bias_ready, exp_done, normed, o_out, chain = semaphores(
            nc, ctx, "at_pta at_ptd at_bias at_exp at_norm at_out at_chain")
        pieces = [(g, c) for g, (n, kv) in enumerate(steps) for c in range(span(n)[0] // P, span(n)[1] // P)]
        piece_at = {x: i for i, x in enumerate(pieces)}
        last_piece = [max(piece_at[x] for x in pieces if x[0] == g) for g in range(len(steps))]

        out_w_in = semaphore(nc, ctx, "at_wout")
        block = ctx.enter_context(nc.Block())

        @block.sync
        def _(sp):
            sp.dma_start(m.ring[:, 10 * D:18 * D].rearrange("p (k n) -> p k n", k=K), d["ev_out"]).then_inc(out_w_in, 16)
            sp.wait_ge(out_w_in, 16)

        @block.tensor
        def _(pe):
            def score(g, j):
                n, kv = steps[g]
                a, b = span(n)
                rows = slice(DH * kv, DH * kv + DH)
                i = QPK * g + j
                if i >= 2:
                    pe.wait_ge(sc_free[i % 2], i // 2)
                ps = m.ps[:, 2 * (i % 2):2 * (i % 2) + 2, :].rearrange("p b n -> p (b n)")
                lhs = q[rows, j, n * P:(n + 1) * P]
                if a == 0:
                    pe.matmul(ps[:, 3 * P:4 * P], lhs, kk[rows, (n - 1) * P:n * P], start=True, stop=True)
                mm = pe.matmul(ps[:, 4 * P:6 * P], lhs, kk[rows, SEQ:TOK], start=True, stop=True)
                if b > 3 * P:
                    mm = pe.matmul(ps[:, 6 * P:3 * P + b], lhs, kk[rows, n * P:n * P + b - 3 * P],
                                   start=True, stop=True)
                mm.then_inc(sc_done, 1)

            def turn(g, c):
                pe.wait_ge(normed, g + 1)
                i = piece_at[g, c]
                if i >= 2:
                    pe.wait_ge(pt_free[i % 2], i // 2)
                for j in range(QPK):
                    mm = pe.transpose(m.ps[:, 4 + i % 2, j * P:(j + 1) * P],
                                      s[:, g % 2, j, c * P:(c + 1) * P], m.ident[:, :])
                mm.then_inc(pt_done, 1)

            def context_product(g):
                n, kv = steps[g]
                if g >= 2:
                    pe.wait_ge(o_out, g - 1)
                rows = slice(DH * kv, DH * kv + DH)
                chunks = range(span(n)[0] // P, span(n)[1] // P)
                for c in chunks:
                    i = piece_at[g, c]
                    pe.wait_ge(pt_free[i % 2], i // 2 + 1)
                    mm = pe.matmul(m.ps[rows, 6 + g % 2, :], v[:, key_tile(n, c), rows], pt[:, g % 2, c, :],
                                   start=(c == chunks[0]), stop=(c == chunks[-1]))
                mm.then_inc(o_done, 1)

            for j in range(QPK):
                score(0, j)
            for g in range(len(steps)):
                for what, x in order(g):
                    if what == "score":
                        score(g + 1, x)
                    else:
                        turn(g, x)
                context_product(g)

        def copy_out(engine, g, c, parity):
            i = piece_at[g, c]
            if i % 2 == parity:
                engine.wait_ge(pt_done, i + 1)
                if g >= 2:
                    engine.wait_ge(o_done, g - 1)
                copy = engine.copy if parity == 0 else engine.tensor_copy
                copy(pt[:, g % 2, c, :], m.ps[:, 4 + parity, :]).then_inc(pt_free[parity], 1)

        @block.scalar
        def _(act):
            def exps(g):
                a, b = span(steps[g][0])
                act.wait_ge(bias_ready, g + 1)
                act.activation(small[:, g % 2, 4, :], small[:, g % 2, 2, :], ACT.Exp).then_inc(exp_done, 1)
                for j in range(QPK):
                    row = s[:, g % 2, j, a:b]
                    act.activation(row, row, ACT.Exp, bias=small[:, g % 2, 1, j:j + 1],
                                   accum_out=small[:, g % 2, 3, j:j + 1]).then_inc(exp_done, 1)

            exps(0)
            for g, (n, kv) in enumerate(steps):
                for what, x in order(g):
                    if what == "turn":
                        copy_out(act, g, x, 0)
                if g + 1 < len(steps):
                    exps(g + 1)
                act.wait_ge(o_done, g + 1)
                rows = slice(DH * kv, DH * kv + DH)
                act.copy(cat[rows, 0:QPK, n * P:(n + 1) * P],
                         m.ps[rows, 6 + g % 2, :].rearrange("p (j t) -> p j t", j=QPK)).then_inc(o_out, 1)

        @block.vector
        def _(dve):
            links = 0

            def link(ins):
                nonlocal links
                links += 1
                ins.then_inc(chain, 1)
                dve.wait_ge(chain, links)

            def maximum(g, j):
                a, b = span(steps[g][0])
                if g >= 2 and j == 0:
                    dve.wait_ge(pt_done, last_piece[g - 2] + 1)
                i = QPK * g + j
                dve.wait_ge(sc_done, i + 1)
                ps = m.ps[:, 2 * (i % 2):2 * (i % 2) + 2, :].rearrange("p b n -> p (b n)")
                dve.tensor_tensor_reduce(s[:, g % 2, j, a:b], ps[:, 3 * P + a:3 * P + b], m.mask[:, a:b],
                                         DH ** -0.5, -3.0e38, ALU.add, ALU.max,
                                         small[:, g % 2, 0, j:j + 1]).then_inc(sc_free[i % 2], 1)
                if j == QPK - 1:
                    biases(g)

            def biases(g):
                kv = steps[g][1]
                x = small[:, g % 2]
                for i in (QPK * g + 2, QPK * g + 3):
                    dve.wait_ge(sc_free[i % 2], i // 2 + 1)
                link(dve.tensor_tensor(x[:, 5, :], x[:, 0, :], m.sink[:, 4 * kv:4 * kv + 4], ALU.max))
                link(dve.tensor_scalar(x[:, 1, :], x[:, 5, :], -1.0, None, ALU.mult))
                dve.tensor_tensor(x[:, 2, :], m.sink[:, 4 * kv:4 * kv + 4], x[:, 5, :], ALU.subtract).then_inc(bias_ready, 1)

            def normalise(g):
                a, b = span(steps[g][0])
                x = small[:, g % 2]
                for pair in (slice(0, 2), slice(2, 4)):
                    dve.wait_ge(exp_done, (QPK + 1) * g + 1 + pair.stop)
                    link(dve.tensor_tensor(x[:, 6, pair], x[:, 3, pair], x[:, 4, pair], ALU.add))
                    link(dve.reciprocal(x[:, 7, pair], x[:, 6, pair]))
                    for j in range(pair.start, pair.stop):
                        row = s[:, g % 2, j, a:b]
                        last = dve.tensor_scalar(row, row, x[:, 7, j:j + 1], None, ALU.mult)
                last.then_inc(normed, 1)

            for j in range(QPK):
                maximum(0, j)
            for g in range(len(steps)):
                normalise(g)
                for what, x in order(g):
                    if what == "score":
                        maximum(g + 1, x)
                    else:
                        copy_out(dve, g, x, 1)


def out_stage(nc, m, d, name, layer, inT, w_dram, sources, affT):
    tiles = []
    for src, n, s in sources:
        tiles += [(src[i * P:(i + 1) * P, :], s) for i in range(n)]
    N = len(tiles)
    w = m.ring[:, 10 * D:18 * D].rearrange("p (k n) -> p k n", k=K)
    at = 0
    xt = m.ring[:, at:at + 2 * D].rearrange("p (b n) -> p b n", b=2)
    x1 = m.ring[:, at + 2 * D:at + 4 * D].rearrange("p (b n) -> p b n", b=2)
    xn = m.ring[:, at + 4 * D:at + 6 * D].rearrange("p (b n) -> p b n", b=2)
    gates = m.ring[:, at + 6 * D:at + 8 * D].rearrange("p (b n) -> p b n", b=2)
    junk = m.ring[:, at + 8 * D:at + 9 * D]
    h2 = m.A[:, 0:2 * D].rearrange("p (b k t) -> p b k t", b=2, k=K)
    rw = m.A[:, 2 * D:2 * D + K * NE].rearrange("p (k e) -> p k e", k=K)
    st = m.A[:, 2 * D + 256:2 * D + 512].rearrange("p (b x) -> p b x", b=2)
    lg = m.A[:, 2 * D + 512:2 * D + 512 + 4 * NE].rearrange("p (b x e) -> p b x e", b=2, x=2)
    with stage_of(nc) as ctx:
        aux_in, y_done, y_read, sq, chain, sd_done, xn_done, turned, ev_act, ev_dve = semaphores(
            nc, ctx, " ".join(f"{name}_{x}" for x in
                              "aux y yread sq chain sd xn turn eva evd".split()))
        lg_done, nmax, ex_done, aff_done, afft_done, afft_out, x1_done = semaphores(
            nc, ctx, " ".join(f"{name}_{x}" for x in "lg nmax ex aff afft afftout x1".split()))
        w_in = [semaphore(nc, ctx, f"{name}_w{half}") for half in range(2)]
        x_in, x1_out, xn_out = ([semaphore(nc, ctx, f"{name}_{x}{b}") for b in range(2)]
                                for x in ("xin", "x1o", "xno"))
        block = ctx.enter_context(nc.Block())

        def store(sp, t):
            b = t % 2
            sp.wait_ge(x1_done, t + 1)
            sp.dma_start(d["x_res"][t * P:(t + 1) * P, :], x1[:, b, :]).then_inc(x1_out[b], 16)
            sp.wait_ge(xn_done, t + 1)
            sp.dma_start(d["x_norm"][t * P:(t + 1) * P, :], xn[:, b, :]).then_inc(xn_out[b], 16)

        @block.sync
        def _(sp):
            sp.dma_start(rw, d["router_w"][layer]).then_inc(aux_in, 16)
            for s in range(2):
                row = d["mrow"][s:s + 1, (layer * 6 + 2) * D:(layer * 6 + 3) * D]
                sp.dma_start(gates[:, s, :], row.to_broadcast((P, D))).then_inc(aux_in, 16)
            if w_dram is not None:
                for half in range(2):
                    at = slice(half * BANK, (half + 1) * BANK)
                    sp.dma_start(w[:, :, at], w_dram[:, :, at]).then_inc(w_in[half], 16)
            for t, (src, s) in enumerate(tiles):
                if t >= 2:
                    sp.wait_ge(x1_done, t - 1)
                sp.dma_start(xt[:, t % 2, :], src).then_inc(x_in[t % 2], 16)
                if t >= 1:
                    store(sp, t - 1)
            store(sp, N - 1)
            for b in range(2):
                sp.wait_ge(x1_out[b], 16 * ((N - b + 1) // 2))
                sp.wait_ge(xn_out[b], 16 * ((N - b + 1) // 2))

        @block.tensor
        def _(pe):
            def project(t):
                pe.wait_ge(y_read, t - 1) if t >= 2 else None
                for half in range(2):
                    if t == 0 and w_dram is not None:
                        pe.wait_ge(w_in[half], 16)
                    for k in range(K):
                        mm = pe.matmul(m.ps[:, 2 * (t % 2) + half, :], inT[:, k, t * P:(t + 1) * P],
                                       w[:, k, half * BANK:(half + 1) * BANK], start=(k == 0), stop=(k == K - 1))
                mm.then_inc(y_done, 1)

            def turn(t):
                pe.wait_ge(xn_done, t + 1)
                if t >= 1:
                    pe.wait_ge(ev_act, t)
                    pe.wait_ge(ev_dve, t)
                for k in range(K):
                    mm = pe.transpose(m.ps[:, 4 + k // 4, (k % 4) * P:(k % 4 + 1) * P],
                                      xn[:, t % 2, k * P:(k + 1) * P], m.ident[:, :])
                mm.then_inc(turned, 1)

            def route(t):
                pe.wait_ge(ev_act, t + 1)
                pe.wait_ge(ev_dve, t + 1)
                if t >= 1:
                    pe.wait_ge(aff_done, t)
                for k in range(K):
                    mm = pe.matmul(m.ps[:, 6, 0:NE], h2[:, t % 2, k, :], rw[:, k, :], start=(k == 0), stop=(k == K - 1))
                mm.then_inc(lg_done, 1)

            def turn_affinities(t):
                pe.wait_ge(aff_done, t + 1)
                if t >= 1:
                    pe.wait_ge(afft_out, t)
                pe.transpose(m.ps[0:NE, 7, 0:P], lg[:, t % 2, 1, :], m.ident[:, :]).then_inc(afft_done, 1)

            pe.wait_ge(aux_in, 48)
            for t in range(N + 3):
                if t < N:
                    project(t)
                if 1 <= t <= N:
                    turn(t - 1)
                if 2 <= t <= N + 1:
                    route(t - 2)
                if t >= 3:
                    turn_affinities(t - 3)

        @block.scalar
        def _(act):
            for t in range(N + 2):
                if t < N:
                    b, s = t % 2, tiles[t][1]
                    act.wait_ge(x1_done, t + 1)
                    act.activation(junk, x1[:, b, :], ACT.Square, accum_out=st[:, b, 0:1]).then_inc(sq, 1)
                    act.wait_ge(chain, 2 * t + 1)
                    act.activation(st[:, b, 2:3], st[:, b, 1:2], ACT.Sqrt).then_inc(sd_done, 1)
                    act.wait_ge(turned, t + 1)
                    if t >= 2:
                        act.wait_ge(lg_done, t - 1)
                    for k in range(4):
                        last = act.activation(h2[:, b, k, :], m.ps[:, 4, k * P:(k + 1) * P], ACT.Identity,
                                              bias=m.mod[:, layer, 3, k, s:s + 1], scale=m.comb[:, layer, 1, k, s:s + 1])
                    last.then_inc(ev_act, 1)
                if 1 <= t <= N:
                    u = (t - 1) % 2
                    act.wait_ge(nmax, t)
                    act.activation(lg[:, u, 0, :], m.ps[:, 6, 0:NE], ACT.Exp, bias=st[:, u, 5:6],
                                   accum_out=st[:, u, 6:7]).then_inc(ex_done, 1)
                if t >= 2:
                    act.wait_ge(afft_done, t - 1)
                    act.copy(affT[:, (t - 2) * P:(t - 1) * P], m.ps[0:NE, 7, 0:P]).then_inc(afft_out, 1)

        @block.vector
        def _(dve):
            steps = semaphores(nc, ctx, f"{name}_links")[0]
            links = 0

            def link(ins):
                nonlocal links
                links += 1
                ins.then_inc(steps, 1)
                dve.wait_ge(steps, links)

            dve.wait_ge(aux_in, 48)
            for t in range(N + 1):
                if t < N:
                    b, s = t % 2, tiles[t][1]
                    dve.wait_ge(y_done, t + 1)
                    dve.wait_ge(x_in[b], 16 * (t // 2 + 1))
                    if t >= 2:
                        dve.wait_ge(x1_out[b], 16 * (t // 2))
                        dve.wait_ge(xn_out[b], 16 * (t // 2))
                        dve.wait_ge(turned, t - 1)
                    y = m.ps[:, 2 * b:2 * b + 2, :].rearrange("p b n -> p (b n)")
                    dve.tensor_tensor(x1[:, b, :], y, gates[:, s, :], ALU.mult).then_inc(y_read, 1)
                    dve.wait_ge(y_read, t + 1)
                    dve.tensor_tensor(x1[:, b, :], x1[:, b, :], xt[:, b, :], ALU.add).then_inc(x1_done, 1)
                    dve.wait_ge(sq, t + 1)
                    dve.tensor_scalar(st[:, b, 1:2], st[:, b, 0:1], 1.0 / D, EPS, ALU.mult, ALU.add).then_inc(chain, 1)
                    dve.wait_ge(sd_done, t + 1)
                    dve.reciprocal(st[:, b, 3:4], st[:, b, 2:3]).then_inc(chain, 1)
                    dve.wait_ge(chain, 2 * t + 2)
                    dve.tensor_scalar(xn[:, b, :], x1[:, b, :], st[:, b, 3:4], None, ALU.mult).then_inc(xn_done, 1)
                    dve.wait_ge(turned, t + 1)
                    if t >= 2:
                        dve.wait_ge(lg_done, t - 1)
                    for k in range(4, 8):
                        last = dve.tensor_scalar(h2[:, b, k, :], m.ps[:, 5, (k - 4) * P:(k - 3) * P],
                                                 m.comb[:, layer, 1, k, s:s + 1], m.mod[:, layer, 3, k, s:s + 1],
                                                 ALU.mult, ALU.add)
                    last.then_inc(ev_dve, 1)
                if t >= 1:
                    u = (t - 1) % 2
                    dve.wait_ge(lg_done, t)
                    if t >= 3:
                        dve.wait_ge(afft_done, t - 2)
                    link(dve.tensor_reduce(st[:, u, 4:5], m.ps[:, 6, 0:NE], AX_X, ALU.max))
                    dve.tensor_scalar(st[:, u, 5:6], st[:, u, 4:5], -1.0, None, ALU.mult).then_inc(nmax, 1)
                    dve.wait_ge(ex_done, t)
                    link(dve.reciprocal(st[:, u, 7:8], st[:, u, 6:7]))
                    dve.tensor_scalar(lg[:, u, 1, :], lg[:, u, 0, :], st[:, u, 7:8], None, ALU.mult).then_inc(aff_done, 1)


def choose_stage(nc, m, name, affT, with_context, make_beside):
    sets = [(0, SEQ, CAP, m.idx, m.gate)]
    if with_context:
        sets.append((SEQ, CTX, CAPC, m.idxc, m.gatec))
    flat = m.rope[0:NE, :, :].rearrange("p a n -> p (a n)")[:, TOK:]
    place = lambda i: [flat[:, 160 * i:160 * i + CAP], flat[:, 160 * i + CAP:160 * (i + 1)]]
    vals, idxf = place(0), place(2)
    idx = [x.bitcast(U32) for x in place(1)]
    with stage_of(nc) as ctx:
        found, turned, copied = semaphores(nc, ctx, f"{name}_found {name}_turn {name}_copy")
        chain = semaphore(nc, ctx, f"{name}_chain")
        beside = make_beside(nc, ctx)
        block = ctx.enter_context(nc.Block())

        @block.vector
        def _(dve):
            links = 0

            def link(ins):
                nonlocal links
                links += 1
                ins.then_inc(chain, 1)
                dve.wait_ge(chain, links)

            for n, (t0, width, cap, idx_out, gate_out) in enumerate(sets):
                row = affT[:, t0:t0 + width]
                for i in range(cap // 8):
                    at = slice(8 * i, 8 * i + 8)
                    link(dve.max(vals[n][:, at], row))
                    link(dve.max_index(idx[n][:, at], vals[n][:, at], row))
                    link(dve.match_replace(row, vals[n][:, at], row, -1.0))
                dve.tensor_scalar(idxf[n], idx[n], float(t0), None, ALU.add).then_inc(found, 1)
            for n, (t0, width, cap, idx_out, gate_out) in enumerate(sets):
                dve.wait_ge(turned, n + 1)
                dve.tensor_copy(idx_out[0:cap, 0:NE], m.ps[0:cap, 2 * n, 0:NE]).then_inc(copied, 1)
                dve.tensor_copy(idx_out[0:cap, NE:NE + 1], m.ps[0:cap, 2 * n, 0:1]).then_inc(copied, 1)
                dve.tensor_copy(gate_out[0:cap, :], m.ps[0:cap, 2 * n + 1, 0:NE]).then_inc(copied, 1)
            beside.on_vector(dve)

        @block.sync
        def _(sp):
            beside.on_sync(sp)

        @block.scalar
        def _(act):
            beside.on_scalar(act)

        @block.gpsimd
        def _(pool):
            beside.on_gpsimd(pool)

        @block.tensor
        def _(pe):
            beside.on_tensor(pe)
            for n, (t0, width, cap, idx_out, gate_out) in enumerate(sets):
                pe.wait_ge(found, n + 1)
                pe.transpose(m.ps[0:cap, 2 * n, 0:NE], idxf[n], m.ident[0:NE, 0:NE])
                pe.transpose(m.ps[0:cap, 2 * n + 1, 0:NE], vals[n], m.ident[0:NE, 0:NE]).then_inc(turned, 1)


def expert_stage(nc, m, d, name, layer, with_context):
    N = CAP + (CAPC if with_context else 0)
    PER = BANK // N
    YB = -(-K // PER)
    R = 6
    STEPS = 2 * R
    units = d["moe"]
    unit = m.ring[:, :].rearrange("p (s n) -> p s n", s=R)
    w_of = lambda r, part: unit[:, r, part * D:(part + 1) * D].rearrange("p (k n) -> p k n", k=K)
    sets = [(CAP, 0, m.idx, m.gate)] + ([(CAPC, 1, m.idxc, m.gatec)] if with_context else [])
    NS = len(sets)
    OUTS = 2 * NS
    A = m.A
    xg = [A[0:cap, s * D:(s + 1) * D] for cap, s, _, _ in sets]
    ys = [A[0:cap, (2 + s) * D:(3 + s) * D] for cap, s, _, _ in sets]
    gates = [A[0:cap, (4 + s) * D:(5 + s) * D] for cap, s, _, _ in sets]
    xe = m.B[:, 0:2 * K * N].rearrange("p (b k n) -> p b k n", b=2, k=K)
    at = 3 * D
    ysb = m.B[:, at:at + K * N].rearrange("p (k n) -> p k n", k=K)
    sa = m.B[:, at + 2 * D:at + 2 * D + 2 * N].rearrange("p (b n) -> p b n", b=2)
    h = m.B[:, at + 3 * D:at + 3 * D + 2 * N].rearrange("p (b n) -> p b n", b=2)
    gcur = m.B[:, at + 4 * D:at + 4 * D + 2]
    with stage_of(nc) as ctx:
        unit_done, au_done, sa_done, h_done, y_act, y_dve = semaphores(
            nc, ctx, " ".join(f"{name}_{x}" for x in "unit au sa h ya yd".split()))
        in_done, x_act, x_dve, out_done, out_read, ys_ready, gate_ready = semaphores(
            nc, ctx, " ".join(f"{name}_{x}" for x in "in xa xd out outr ys gcur".split()))
        gates_in, gathered, scattered = semaphores(
            nc, ctx, " ".join(f"{name}_{x}" for x in "gates gat scat".split()))
        unit_in = [semaphore(nc, ctx, f"{name}_w{r}") for r in range(R)]
        block = ctx.enter_context(nc.Block())

        def need(engine, sem, value):
            if not isinstance(value, int) or value > 0:
                engine.wait_ge(sem, value)

        def experts(engine, body):
            body(0, 0)
            body(1, 1)
            with engine.Fori(1, NE // 2) as i:
                body(i * 2, 0)
                body(i * 2 + 1, 1)

        @block.sync
        def _(sp):
            for cap, s, _, _ in sets:
                row = d["mrow"][s:s + 1, (layer * 6 + 5) * D:(layer * 6 + 6) * D]
                sp.dma_start(gates[s], row.to_broadcast((cap, D))).then_inc(gates_in, 16)

            def expert(e, b):
                for j in range(FJ):
                    if j >= R:
                        need(sp, unit_done, e * FJ + (j - R + 1))
                    else:
                        old = j + R if j + R < FJ else j
                        need(sp, unit_done, e * FJ + (old + 1 - FJ))
                    sp.dma_start(unit[:, j % R, :], units[e * FJ + j]).then_inc(unit_in[j % R], 16)
                    if isinstance(e, int) and e == 0 and j == 0:
                        sp.wait_ge(gathered, 16 * NS)
            experts(sp, expert)

        @block.gpsimd
        def _(pool):
            def gather(e):
                need(pool, in_done, e)
                for cap, s, idx, _ in sets:
                    pool.indirect_dma_start(xg[s], None, d["x_norm"], bass.IndirectOffsetOnAxis(
                        ap=idx[0:cap, e:e + 1], axis=0)).then_inc(gathered, 16)

            def scatter(e):
                pool.wait_ge(ys_ready, e + 1)
                for cap, s, idx, _ in sets:
                    pool.indirect_dma_start(d["x_res"], bass.IndirectOffsetOnAxis(ap=idx[0:cap, e:e + 1], axis=0),
                                            ys[s], None, compute_op=ALU.add).then_inc(scattered, 16)

            gather(0)
            for e in range(NE):
                gather(e + 1)
                if e:
                    scatter(e - 1)
            scatter(NE - 1)
            pool.wait_ge(scattered, 16 * NS * NE)
            pool.wait_ge(gathered, 16 * NS * (NE + 1))

        @block.tensor
        def _(pe):
            def turn_in(e):
                pe.wait_ge(gathered, e * (16 * NS) + 16 * NS)
                need(pe, out_read, e * OUTS - OUTS)
                for k in range(K):
                    mm = pe.transpose(m.ps[:, 5 + k // 4, (k % 4) * P:(k % 4 + 1) * P],
                                      xg[0][:, k * P:(k + 1) * P], m.ident[:, :])
                for k in range(K if NS > 1 else 0):
                    mm = pe.transpose(m.ps[:, 7, k * CAPC:(k + 1) * CAPC], xg[1][:, k * P:(k + 1) * P],
                                      m.ident[0:CAPC, 0:CAPC])
                mm.then_inc(in_done, 1)

            def turn_out(e):
                pe.wait_ge(y_act, e + 1)
                pe.wait_ge(y_dve, e + 1)
                for piece in range(OUTS):
                    cap, s, _, _ = sets[piece // 2]
                    if piece == 3:
                        pe.wait_ge(out_read, e * OUTS + 1)
                    for q in range(4):
                        mm = pe.transpose(m.ps[0:cap, 5 + piece % 3, q * P:(q + 1) * P],
                                          ysb[:, 4 * (piece % 2) + q, s * CAP:s * CAP + cap], m.ident[:, :])
                    mm.then_inc(out_done, 1)

            def up(e, b, j):
                if j == 0:
                    pe.wait_ge(x_act, e + 1)
                    pe.wait_ge(x_dve, e + 1)
                pe.wait_ge(unit_in[j % R], (e * 16 + 16) if j % R == R - 1 else (e * 32 + (16 + 16 * (j // R))))
                need(pe, h_done, e * FJ + (j - 1))
                for part in range(2):
                    for k in range(K):
                        mm = pe.matmul(m.ps[:, (b + j) % 2, 256 * part:256 * part + N],
                                       w_of(j % R, part)[:, k, :], xe[:, b, k, :], start=(k == 0), stop=(k == K - 1))
                mm.then_inc(au_done, 1)

            def down(e, b, j):
                pe.wait_ge(h_done, e * FJ + (j + 1))
                if j == 0:
                    need(pe, y_act, e)
                    need(pe, y_dve, e)
                w = unit[:, j % R, 2 * D:3 * D]
                for i in range(K):
                    mm = pe.matmul(m.ps[:, 2 + i // PER, (i % PER) * N:(i % PER + 1) * N], w[:, i * P:(i + 1) * P],
                                   h[:, (b + j) % 2, :], start=(j == 0 and i % PER == 0), stop=(j == FJ - 1),
                                   skip_group_check=True)
                mm.then_inc(unit_done, 1)

            def expert(e, b):
                for j in range(FJ):
                    up(e, b, j)
                    if j:
                        down(e, b, j - 1)
                    elif not isinstance(e, int) or e > 0:
                        down(e - 1, 1 - b, FJ - 1)
                    if j == 3 and (not isinstance(e, int) or e > 0):
                        turn_out(e - 1)
                    if j == 6:
                        turn_in(e + 1)

            turn_in(0)
            experts(pe, expert)
            down(NE - 1, 1, FJ - 1)
            turn_out(NE - 1)

        def copy_in(engine, e, b, half):
            engine.wait_ge(in_done, e + 1)
            need(engine, au_done, e * FJ - FJ)
            for cap, s, _, _ in sets:
                for k in range(4 * half, 4 * half + 4) if s == 0 else range(K if half else 0):
                    src = m.ps[:, 5 + half, (k % 4) * P:(k % 4 + 1) * P] if s == 0 else m.ps[:, 7, k * CAPC:(k + 1) * CAPC]
                    out = xe[:, b, k, s * CAP:s * CAP + cap]
                    gain, shift = m.comb[:, layer, 1, k, s:s + 1], m.mod[:, layer, 3, k, s:s + 1]
                    if half == 0:
                        last = engine.activation(out, src, ACT.Identity, bias=shift, scale=gain)
                    else:
                        last = engine.tensor_scalar(out, src, gain, shift, ALU.mult, ALU.add)
            last.then_inc(x_dve if half else x_act, 1)

        def copy_y(engine, e, half):
            engine.wait_ge(unit_done, e * FJ + FJ)
            need(engine, out_done, e * OUTS)
            for bank in range(half, YB, 2):
                n = min(PER, K - bank * PER)
                dst = ysb[:, bank * PER:bank * PER + n, :]
                src = m.ps[:, 2 + bank, 0:n * N].rearrange("p (k n) -> p k n", k=n)
                last = engine.tensor_copy(dst, src) if half else engine.copy(dst, src)
            last.then_inc(y_dve if half else y_act, 1)

        @block.scalar
        def _(act):
            def expert(e, b):
                for j in range(FJ):
                    act.wait_ge(au_done, e * FJ + (j + 1))
                    need(act, h_done, e * FJ + (j - 1))
                    act.activation(sa[:, (b + j) % 2, :], m.ps[:, (b + j) % 2, 0:N], ACT.Silu).then_inc(sa_done, 1)
                    if j == 0 and (not isinstance(e, int) or e > 0):
                        copy_y(act, e - 1, 0)
                    if j == 6:
                        copy_in(act, e + 1, 1 - b, 0)
            copy_in(act, 0, 0, 0)
            experts(act, expert)
            copy_y(act, NE - 1, 0)

        @block.vector
        def _(dve):
            def weigh(e):
                dve.wait_ge(gate_ready, e * NS + NS)
                need(dve, scattered, e * (16 * NS))
                for piece in range(OUTS):
                    cap, s, _, _ = sets[piece // 2]
                    half = slice((piece % 2) * BANK, (piece % 2 + 1) * BANK)
                    dve.wait_ge(out_done, e * OUTS + (piece + 1))
                    dve.scalar_tensor_tensor(ys[s][:, half], m.ps[0:cap, 5 + piece % 3, :], gcur[0:cap, s:s + 1],
                                             gates[s][:, half], ALU.mult, ALU.mult).then_inc(out_read, 1)
                dve.wait_ge(out_read, e * OUTS + OUTS)
                dve.nop().then_inc(ys_ready, 1)

            def take_gates(e):
                need(dve, out_read, e * OUTS)
                for cap, s, _, gate in sets:
                    dve.tensor_copy(gcur[0:cap, s:s + 1], gate[0:cap, bass.ds(e, 1)]).then_inc(gate_ready, 1)

            def expert(e, b):
                for j in range(FJ):
                    dve.wait_ge(sa_done, e * FJ + (j + 1))
                    need(dve, unit_done, e * FJ + (j - 1))
                    dve.tensor_tensor(h[:, (b + j) % 2, :], m.ps[:, (b + j) % 2, 256:256 + N], sa[:, (b + j) % 2, :],
                                      ALU.mult).then_inc(h_done, 1)
                    later = not isinstance(e, int) or e > 0
                    if j == 0 and later:
                        copy_y(dve, e - 1, 1)
                    if j == 2 and later:
                        take_gates(e - 1)
                    if j == 3 and later:
                        weigh(e - 1)
                    if j == 6:
                        copy_in(dve, e + 1, 1 - b, 1)
            dve.wait_ge(gates_in, 16 * NS)
            copy_in(dve, 0, 0, 1)
            experts(dve, expert)
            copy_y(dve, NE - 1, 1)
            take_gates(NE - 1)
            weigh(NE - 1)


ROW_UNITS, ROW_SLOTS = 4, 4
ROW_U = FF // ROW_UNITS
ROW_PIECE = K * ROW_U
assert ROW_PIECE == FJ * (D // 4)


class RowBuffers:

    def __init__(self, nc, ctx):
        sb = lambda what, shape, dt=F32: ctx.enter_context(nc.sbuf_tensor(f"rows_{what}", shape, dt))
        self.raw = sb("raw", [P, ROW_SLOTS, ROW_PIECE])
        self.high, self.low = (sb(x, [P, ROW_SLOTS, ROW_PIECE], F32R) for x in ("high", "low"))
        self.xg, self.xm = sb("xg", [P, D]), sb("xm", [P, D])
        self.ys, self.gates = sb("ys", [P, D]), sb("gates", [P, D])
        self.x_hi, self.x_lo = (sb(x, [P, 2, K, P], F32R) for x in ("xhi", "xlo"))
        self.h = sb("h", [P, FF])
        self.hT_hi, self.hT_lo = (sb(x, [P, FJ, P], F32R) for x in ("hthi", "htlo"))
        self.sa = sb("sa", [P, 2, ROW_U])
        self.gcur = sb("gcur", [P, 2])


class FirstPieces:

    def __init__(self, nc, ctx, m, d):
        self.m, self.d = m, d
        self.high_done, self.low_done = semaphores(nc, ctx, "fp_high fp_low")
        self.landed = [semaphore(nc, ctx, f"fp_in{s}") for s in range(ROW_SLOTS)]

    def on_sync(self, sp):
        for n in range(2 * ROW_SLOTS):
            s = n % ROW_SLOTS
            if n >= ROW_SLOTS:
                sp.wait_ge(self.low_done, s + 1)
            sp.dma_start(self.m.rows.raw[:, s, :], self.d["moe_rows"][n]).then_inc(self.landed[s], 16)
        for s in range(ROW_SLOTS):
            sp.wait_ge(self.landed[s], 32)

    def on_scalar(self, act):
        r = self.m.rows
        for s in range(ROW_SLOTS):
            act.wait_ge(self.landed[s], 16)
            act.copy(r.high[:, s, :], r.raw[:, s, :]).then_inc(self.high_done, 1)

    def on_gpsimd(self, pool):
        r = self.m.rows
        for s in range(ROW_SLOTS):
            pool.wait_ge(self.high_done, s + 1)
            pool.tensor_tensor(r.low[:, s, :], r.raw[:, s, :], r.high[:, s, :].bitcast(F32), ALU.subtract).then_inc(
                self.low_done, 1)

    def on_tensor(self, pe):
        pass

    def on_vector(self, dve):
        pass


def expert_rows_stage(nc, m, d, name, layer):
    UNITS, U, PIECE, SLOTS = ROW_UNITS, ROW_U, ROW_PIECE, ROW_SLOTS
    TURN = 12
    DOWN = range(2, 6)
    GROUPS = [range(0, 2), range(2, 5), range(5, 8), range(8, 11)]
    pieces = d["moe_rows"]
    r = m.rows
    raw, high, low, xg, xm, ys, gates = r.raw, r.high, r.low, r.xg, r.xm, r.ys, r.gates
    x_hi, x_lo, h, hT_hi, hT_lo, sa, gcur = r.x_hi, r.x_lo, r.h, r.hT_hi, r.hT_lo, r.sa, r.gcur
    with stage_of(nc) as ctx:
        piece_done, high_done, low_done, sa_done, h_done, h_turned, hT_high, hT_low = semaphores(
            nc, ctx, " ".join(f"{name}_{x}" for x in "piece high low sa h hturn hthi htlo".split()))
        x_turned, x_read, x_high, x_low, y_read, ys_ready, gate_ready = semaphores(
            nc, ctx, " ".join(f"{name}_{x}" for x in "xturn xread xhi xlo yread ys gcur".split()))
        gates_in, gathered, scattered, x_parts = semaphores(
            nc, ctx, " ".join(f"{name}_{x}" for x in "gates gat scat xparts".split()))
        piece_in = [semaphore(nc, ctx, f"{name}_w{r}") for r in range(SLOTS)]
        block = ctx.enter_context(nc.Block())

        def prepared(e, p):
            return isinstance(e, int) and e == 0 and p in (0, 1, 6, 7)

        def exists(e, p):
            return not isinstance(e, int) or (0 <= e < NE and not (e == 0 and p in DOWN)) or (e == NE and p in DOWN)

        def number(e, p):
            if isinstance(e, int) and e == 0 and p < DOWN[0]:
                return p + 1
            return e * TURN + (p + 1 - len(DOWN)) - (DOWN[0] if isinstance(e, int) and e == NE else 0)

        def before(e, p, places):
            while True:
                e, p = (e, p - places) if p >= places else (e - 1, p - places + TURN)
                if isinstance(e, int) and e < 0:
                    return None
                if exists(e, p):
                    return number(e, p)

        def need(engine, sem, value):
            if value is not None and (not isinstance(value, int) or value > 0):
                engine.wait_ge(sem, value)

        def turns(engine, body):
            body(0, 0)
            with engine.Fori(0, NE // 2 - 1) as i:
                body(i * 2 + 1, 1)
                body(i * 2 + 2, 0)
            body(NE - 1, 1)
            body(NE, 0)

        def later(e):
            return not isinstance(e, int) or e > 0

        def expert(e):
            return not isinstance(e, int) or e < NE

        @block.sync
        def _(sp):
            sp.dma_start(gates[:, :], d["mrow"][0:1, (layer * 6 + 5) * D:(layer * 6 + 6) * D].to_broadcast((P, D))).then_inc(gates_in, 16)

            def turn(e, b):
                for p in range(TURN):
                    if exists(e, p) and not (isinstance(e, int) and e == 0):
                        need(sp, low_done, before(e, p, SLOTS))
                        src = e * TURN + (p if p < 2 else p - 4 if p >= 6 else p + 6 - TURN)
                        sp.dma_start(raw[:, p % SLOTS, :], pieces[src]).then_inc(piece_in[p % SLOTS], 16)
            for r in range(SLOTS):
                sp.nop().then_inc(piece_in[r], 32)
            turns(sp, turn)

        @block.gpsimd
        def _(pool):
            def gather(e):
                need(pool, x_turned, 2 * e)
                pool.indirect_dma_start(xg[:, :], None, d["x_norm"], bass.IndirectOffsetOnAxis(
                    ap=m.idx[:, e:e + 1], axis=0)).then_inc(gathered, 16)

            def scatter(e):
                pool.wait_ge(ys_ready, 2 * e + 2)
                pool.indirect_dma_start(d["x_res"], bass.IndirectOffsetOnAxis(ap=m.idx[:, e:e + 1], axis=0),
                                        ys[:, :], None, compute_op=ALU.add).then_inc(scattered, 16)

            gather(0)
            for e in range(NE):
                if e + 1 < NE:
                    gather(e + 1)
                if e:
                    scatter(e - 1)
            scatter(NE - 1)
            pool.wait_ge(scattered, 16 * NE)
            pool.wait_ge(gathered, 16 * NE)

        @block.tensor
        def _(pe):
            def ready(e, p):
                pe.wait_ge(high_done, number(e, p))
                pe.wait_ge(low_done, number(e, p))

            def products(out, x_high_part, x_low_part, w_high_part, w_low_part, first, last):
                pe.matmul(out, x_high_part, w_high_part, start=first, stop=False)
                pe.matmul(out, x_high_part, w_low_part, start=False, stop=False)
                return pe.matmul(out, x_low_part, w_high_part, start=False, stop=last)

            def up(e, b, p, u, part):
                if part == 0 and u == 0:
                    pe.wait_ge(x_high, e + 1)
                    pe.wait_ge(x_low, e + 1)
                if part == 0:
                    need(pe, h_done, e * UNITS + (u - 1))
                ready(e, p)
                wh = high[:, p % SLOTS, :].rearrange("p (k n) -> p k n", k=K)
                wl = low[:, p % SLOTS, :].rearrange("p (k n) -> p k n", k=K)
                for k in range(K):
                    mm = products(m.ps[:, 2 * (u % 2) + part, 0:U], x_hi[:, b, k, :], x_lo[:, b, k, :],
                                  wh[:, k, :], wl[:, k, :], k == 0, k == K - 1)
                mm.then_inc(piece_done, 1)

            def down(e, p):
                q = p - DOWN[0]
                if q == 0:
                    pe.wait_ge(hT_high, e * UNITS)
                    pe.wait_ge(hT_low, e * UNITS)
                if q % 2 == 0:
                    pe.wait_ge(y_read, e * 2 + (q // 2 - 1))
                ready(e, p)
                wh = high[:, p % SLOTS, :].rearrange("p (j n) -> p j n", j=FJ)
                wl = low[:, p % SLOTS, :].rearrange("p (j n) -> p j n", j=FJ)
                n = D // 4
                for j in range(FJ):
                    mm = products(m.ps[:, 4 + q // 2, (q % 2) * n:(q % 2 + 1) * n], hT_hi[:, j, :], hT_lo[:, j, :],
                                  wh[:, j, :], wl[:, j, :], j == 0, j == FJ - 1)
                mm.then_inc(piece_done, 1)

            def turn_h(e, g):
                pe.wait_ge(h_done, e * UNITS + (g + 1))
                if g < 2 and not (isinstance(e, int) and e == NE - 1):
                    pe.wait_ge(x_read, e * 2 + (g + 3))
                elif g < 2:
                    pe.wait_ge(hT_low, e * UNITS + (g - 1))
                else:
                    pe.wait_ge(hT_low, e * UNITS + (g - 1))
                for i, j in enumerate(GROUPS[g]):
                    mm = pe.transpose(m.ps[:, 6 + (g + 1) % 2, i * P:(i + 1) * P], h[:, j * P:(j + 1) * P], m.ident[:, :])
                mm.then_inc(h_turned, 1)

            def turn_x(e):
                pe.wait_ge(gathered, e * 16 + 16)
                for half in range(2):
                    need(pe, hT_low, (e - 1) * UNITS + (half - 1))
                    for q in range(4):
                        mm = pe.transpose(m.ps[:, 7 - half, q * P:(q + 1) * P], xg[:, (4 * half + q) * P:(4 * half + q + 1) * P],
                                          m.ident[:, :])
                    mm.then_inc(x_turned, 1)

            def turn(e, b):
                if expert(e):
                    up(e, b, 0, 0, 0)
                if later(e):
                    turn_h(e - 1, 3)
                if expert(e):
                    up(e, b, 1, 0, 1)
                for p in DOWN:
                    if later(e):
                        down(e, p)
                    if p == 4 and (not isinstance(e, int) or e + 1 < NE):
                        turn_x(e + 1)
                for u in range(1, UNITS) if expert(e) else ():
                    up(e, b, 4 + 2 * u, u, 0)
                    turn_h(e, u - 1)
                    up(e, b, 5 + 2 * u, u, 1)

            turn_x(0)
            turns(pe, turn)

        @block.scalar
        def _(act):
            def split(e, p):
                if not exists(e, p) or prepared(e, p):
                    return
                nth = p // SLOTS
                if isinstance(e, int) and e == 0 and p < DOWN[0]:
                    nth = 1
                elif isinstance(e, int) and e == NE:
                    nth = 0
                landed = e * 48 + 16 * nth
                act.wait_ge(piece_in[p % SLOTS], landed)
                need(act, piece_done, before(e, p, SLOTS))
                act.copy(high[:, p % SLOTS, :], raw[:, p % SLOTS, :]).then_inc(high_done, 1)

            def copy_x(e, b):
                need(act, x_low, e)
                for k in range(K):
                    if k % 4 == 0:
                        act.wait_ge(x_turned, e * 2 + (k // 4 + 1))
                    ins = act.activation(xm[:, k * P:(k + 1) * P], m.ps[:, 7 - k // 4, (k % 4) * P:(k % 4 + 1) * P],
                                         ACT.Identity, bias=m.mod[:, layer, 3, k, 0:1], scale=m.comb[:, layer, 1, k, 0:1])
                    if k % 4 == 3:
                        ins.then_inc(x_read, 1)
                act.wait_ge(x_read, e * 2 + 2)
                need(act, piece_done, number(e - 2, TURN - 1) if not isinstance(e, int) or e >= 2 else None)
                act.copy(x_hi[:, b, :, :].rearrange("p k n -> p (k n)"), xm[:, :]).then_inc(x_high, 1)

            def silu(e, p, u):
                act.wait_ge(piece_done, number(e, p))
                need(act, h_done, e * UNITS + (u - 1))
                act.activation(sa[:, u % 2, :], m.ps[:, 2 * (u % 2), 0:U], ACT.Silu).then_inc(sa_done, 1)

            def copy_h(e, g):
                act.wait_ge(h_turned, e * UNITS + (g + 1))
                if g < 3:
                    need(act, piece_done, number(e, DOWN[-1]) if later(e) else None)
                n, j = len(GROUPS[g]), GROUPS[g][0]
                act.copy(hT_hi[:, j:j + n, :].rearrange("p j n -> p (j n)"), m.ps[:, 6 + (g + 1) % 2, 0:n * P]).then_inc(hT_high, 1)

            def turn(e, b):
                for p in range(TURN):
                    if p == 0 or p in (6, 8, 10):
                        if expert(e):
                            silu(e, p, max(0, p // 2 - 2))
                    if p == 0 and later(e):
                        copy_h(e - 1, 3)
                    if p in (6, 8, 10) and expert(e):
                        copy_h(e, p // 2 - 3)
                    if p == 4 and (not isinstance(e, int) or e + 1 < NE):
                        copy_x(e + 1, 1 - b)
                    q = p + SLOTS
                    if q < TURN:
                        split(e, q)
                    elif expert(e):
                        split(e + 1, q - TURN)

            act.nop().then_inc(high_done, SLOTS)
            copy_x(0, 0)
            turns(act, turn)

        @block.vector
        def _(dve):
            def split(e, p):
                if exists(e, p) and not prepared(e, p):
                    dve.wait_ge(high_done, number(e, p))
                    need(dve, piece_done, before(e, p, SLOTS))
                    dve.tensor_tensor(low[:, p % SLOTS, :], raw[:, p % SLOTS, :], high[:, p % SLOTS, :].bitcast(F32),
                                      ALU.subtract).then_inc(low_done, 1)

            def split_x(e, b):
                dve.wait_ge(x_high, e + 1)
                flat = lambda x: x[:, b, :, :].rearrange("p k n -> p (k n)")
                dve.tensor_tensor(flat(x_lo), xm[:, :], flat(x_hi).bitcast(F32), ALU.subtract).then_inc(x_low, 1)

            def multiply(e, p, u):
                dve.wait_ge(sa_done, e * UNITS + (u + 1))
                dve.wait_ge(piece_done, number(e, p))
                need(dve, h_turned, (e - 1) * UNITS + (min(u + 1, 3) + 1))
                dve.tensor_tensor(h[:, u * U:(u + 1) * U], m.ps[:, 2 * (u % 2) + 1, 0:U], sa[:, u % 2, :],
                                  ALU.mult).then_inc(h_done, 1)

            def split_h(e, g):
                dve.wait_ge(hT_high, e * UNITS + (g + 1))
                n, j = len(GROUPS[g]), GROUPS[g][0]
                flat = lambda x: x[:, j:j + n, :].rearrange("p j n -> p (j n)")
                dve.tensor_tensor(flat(hT_lo), m.ps[:, 6 + (g + 1) % 2, 0:n * P], flat(hT_hi).bitcast(F32),
                                  ALU.subtract).then_inc(hT_low, 1)

            def weigh(e, half):
                if half == 0:
                    dve.wait_ge(y_read, e * 2 + 2)
                    dve.tensor_copy(gcur[:, 0:1], m.gate[:, bass.ds(e, 1)]).then_inc(gate_ready, 1)
                    dve.wait_ge(gate_ready, e + 1)
                    need(dve, scattered, e * 16)
                dve.wait_ge(piece_done, number(e + 1, DOWN[2 * half + 1]))
                at = slice(half * BANK, (half + 1) * BANK)
                dve.scalar_tensor_tensor(ys[:, at], m.ps[:, 4 + half, :], gcur[:, 0:1], gates[:, at],
                                         ALU.mult, ALU.mult).then_inc(y_read, 1)
                dve.wait_ge(y_read, e * 2 + (half + 3))
                dve.nop().then_inc(ys_ready, 1)

            def turn(e, b):
                for p in range(TURN):
                    if p in (1, 7, 9, 11) and expert(e):
                        multiply(e, p, (p - 5) // 2 if p > 1 else 0)
                    if p == 0 and later(e):
                        split_h(e - 1, 3)
                    if p in (6, 8, 10) and expert(e):
                        split_h(e, p // 2 - 3)
                    if p in (3, 5) and later(e):
                        weigh(e - 1, p // 2 - 1)
                    if p == 4 and (not isinstance(e, int) or e + 1 < NE):
                        split_x(e + 1, 1 - b)
                    q = p + SLOTS
                    if q < TURN:
                        split(e, q)
                    elif expert(e):
                        split(e + 1, q - TURN)

            dve.nop().then_inc(y_read, 2)
            dve.wait_ge(gates_in, 16)
            dve.nop().then_inc(low_done, SLOTS)
            split_x(0, 0)
            turns(dve, turn)


def odd_mixer_stage(nc, m, d):
    yT = m.C.rearrange("p (k t) -> p k t", k=K)
    lw = m.B[:, 0:D].rearrange("p (b x n) -> p b x n", b=2, x=4)
    UP = TOK + 6
    UC = TOK + 3
    up = m.border[:, :]
    uc = m.B[:, D:D + 2 * UC].rearrange("p (b n) -> p b n", b=2)
    at = D + 2 * UC
    r, ig, a, mu, h1 = (m.B[:, at + i * TOK:at + (i + 1) * TOK] for i in range(5))
    h0 = m.rope[:, :, :].rearrange("p a n -> p (a n)")[:, 0:TOK]
    coef = m.mask[:, 0:16 * 6].rearrange("p (x c) -> p x c", x=6)
    gap = UC - TOK

    plan = []
    for h in range(K + 1):
        if h < K:
            plan += [("u", h, ch) for ch in range(3)]
        if h:
            plan += [(kind, h - 1, 0, ch) for kind in ("r", "i") for ch in range(3)]
        if h < K:
            plan += [("g", h, ch) for ch in range(2)]
        if h:
            plan += [(kind, h - 1, 1, ch) for kind in ("r", "i") for ch in range(3)]

    with stage_of(nc) as ctx:
        banks = Banks(nc, ctx, "oi", plan, 8)
        last = [("g", n // 2, 1) if n % 2 else ("u", n // 2, 2) for n in range(16)]
        weights = SplitTiles(nc, ctx, "oi", m, d["od_in"], banks, last)
        lw_in = [semaphore(nc, ctx, f"oi_lw{b}") for b in range(2)]
        u_out, conv_done, sig_done, exp_done, tanh_done, a2_done, iu_done, m2_done, mu_done = semaphores(
            nc, ctx, " ".join(f"oi_{x}" for x in "uo conv sig exp tanh a2 iu m2 mu".split()))
        scan_done, gelu_done, coef_done, chain, absexp = semaphores(
            nc, ctx, " ".join(f"oi_{x}" for x in "scan gelu coef chain absexp".split()))
        block = ctx.enter_context(nc.Block())

        @block.sync
        def _(sp):
            for h in range(K):
                weights.load(sp, 2 * h)
                weights.load(sp, 2 * h + 1)
                if h >= 2:
                    sp.wait_ge(banks.done, banks.number(("i", h - 2, 1, 2)))
                sp.dma_start(lw[:, h % 2, :, :], d["od_gates"][h]).then_inc(lw_in[h % 2], 16)

        @block.tensor
        def _(pe):
            for key in plan:
                kind, h, ch = key[0], key[1], key[-1]
                if banks.uses(key):
                    pe.wait_ge(banks.sem(key), banks.uses(key))
                bank = m.ps[:, banks.bank(key), :]
                t0, n = CHUNKS[ch]
                if kind in "ug":
                    mm = weights.products(pe, bank[:, 0:n], 2 * h + (kind == "g"), t0, n)
                else:
                    x = 2 * key[2] + (kind == "i")
                    if x == 0 and ch == 0:
                        pe.wait_ge(lw_in[h % 2], 16 * (h // 2 + 1))
                        pe.wait_ge(conv_done, h + 1)
                    c0 = t0 if ch < 2 else t0 + gap
                    mm = pe.matmul(bank[:, 0:n], lw[:, h % 2, x, :], uc[:, h % 2, c0:c0 + n], start=True, stop=True)
                mm.then_inc(banks.done, 1)

        @block.scalar
        def _(act):
            lam = m.cols[:, C_LAM:C_LAM + 16]
            act.activation(coef[:, 0, :], lam, ACT.Abs).then_inc(absexp, 1)
            act.wait_ge(absexp, 1)
            act.activation(coef[:, 1, :], coef[:, 0, :], ACT.Exp, scale=-1.0).then_inc(absexp, 1)

            def root(x):
                act.wait_ge(m2_done, x + 1)
                act.activation(mu, mu, ACT.Sqrt).then_inc(mu_done, 1)

            weights.high(act, 0)
            weights.high(act, 1)
            for key in plan:
                kind, h, ch = key[0], key[1], key[-1]
                t0, n = CHUNKS[ch]
                src = m.ps[:, banks.bank(key), 0:n]
                act.wait_ge(banks.done, banks.number(key))
                if kind == "u":
                    if ch == 0 and h:
                        act.wait_ge(conv_done, h)
                    elif ch == 0:
                        act.wait_ge(coef_done, 1)
                    c0 = t0 + 2 if ch < 2 else t0 + 5
                    act.copy(up[:, c0:c0 + n], src).then_inc(banks.sem(key), 1)
                    if ch == 2:
                        for k2 in (("u", h, 0), ("u", h, 1), key):
                            act.wait_ge(banks.sem(k2), banks.uses(k2) + 1)
                        act.nop().then_inc(u_out, 1)
                        if h >= 2:
                            root(2 * (h - 2) + 1)
                elif kind == "g":
                    act.activation(yT[:, h, t0:t0 + n], src, ACT.Gelu_apprx_tanh).then_inc(banks.sem(key), 1)
                    if ch == 1:
                        for k2 in (("g", h, 0), key):
                            act.wait_ge(banks.sem(k2), banks.uses(k2) + 1)
                        act.nop().then_inc(gelu_done, 1)
                        if h:
                            root(2 * (h - 1))
                else:
                    dr = key[2]
                    x = 2 * h + dr
                    if ch == 0 and kind == "r" and x == 2 * K - 2:
                        root(x - 1)
                    if ch == 0 and kind == "r" and x:
                        act.wait_ge(m2_done, x)
                        act.wait_ge(scan_done, x)
                    bias = C_BA if kind == "r" else C_BX
                    act.activation((r if kind == "r" else ig)[:, t0:t0 + n], src, ACT.Sigmoid,
                                   bias=m.cols[:, bias + K * dr + h:bias + K * dr + h + 1]).then_inc(banks.sem(key), 1)
                    if ch == 2:
                        for c in range(3):
                            k2 = (kind, h, dr, c)
                            act.wait_ge(banks.sem(k2), banks.uses(k2) + 1)
                        act.nop().then_inc(sig_done, 1)
                    if ch == 2 and kind == "i":
                        if x == 0:
                            act.wait_ge(coef_done, 2)
                        c = K * dr + h
                        act.activation(a, r, ACT.Exp, scale=coef[:, 4, c:c + 1]).then_inc(exp_done, 1)
                        act.wait_ge(exp_done, x + 1)
                        act.activation(r, r, ACT.Tanh, scale=coef[:, 5, c:c + 1]).then_inc(tanh_done, 1)
                        if h == K - 1:
                            root(x)
                if key in last and last.index(key) + 2 < 16:
                    weights.high(act, last.index(key) + 2)

        @block.gpsimd
        def _(pool):
            for n in range(4):
                weights.low(pool, n)
            for x in range(2 * K):
                h = x // 2
                if x % 2 and x + 3 < 2 * K:
                    weights.low(pool, x + 3)
                pool.wait_ge(sig_done, 2 * x + 2)
                pool.wait_ge(conv_done, h + 1)
                pool.tensor_tensor(ig[:, 0:SEQ], ig[:, 0:SEQ], uc[:, h % 2, 0:SEQ], ALU.mult)
                pool.tensor_tensor(ig[:, SEQ:TOK], ig[:, SEQ:TOK], uc[:, h % 2, SEQ + gap:UC], ALU.mult).then_inc(iu_done, 1)
                if x % 2 and x + 4 < 2 * K:
                    weights.low(pool, x + 4)
                pool.wait_ge(exp_done, x + 1)
                if x:
                    pool.wait_ge(scan_done, x)
                pool.tensor_tensor(mu, a, a, ALU.mult).then_inc(a2_done, 1)

        @block.vector
        def _(dve):
            links = 0

            def link(ins):
                nonlocal links
                links += 1
                ins.then_inc(chain, 1)
                dve.wait_ge(chain, links)

            dve.memset(up, 0.0).then_inc(coef_done, 1)
            dve.wait_ge(absexp, 2)
            lam = m.cols[:, C_LAM:C_LAM + 16]
            e, z, z2, p = coef[:, 1, :], coef[:, 2, :], coef[:, 3, :], coef[:, 0, :]
            link(dve.tensor_scalar(z, e, 2.0, None, ALU.add))
            link(dve.reciprocal(z2, z))
            link(dve.tensor_tensor(z, e, z2, ALU.mult))
            link(dve.tensor_tensor(z2, z, z, ALU.mult))
            link(dve.tensor_scalar(p, z2, 1.0 / 17, None, ALU.mult))
            for c in (15, 13, 11, 9, 7, 5, 3):
                link(dve.scalar_tensor_tensor(p, p, 1.0 / c, z2, ALU.add, ALU.mult))
            link(dve.scalar_tensor_tensor(p, p, 1.0, z, ALU.add, ALU.mult))
            link(dve.tensor_scalar(e, lam, -1.0, 0.0, ALU.mult, ALU.max))
            link(dve.scalar_tensor_tensor(e, p, 2.0, e, ALU.mult, ALU.add))
            link(dve.tensor_scalar(coef[:, 4, :], e, -8.0, None, ALU.mult))
            dve.tensor_scalar(coef[:, 5, :], e, 8.0, None, ALU.mult).then_inc(coef_done, 1)

            def convolve(h):
                dve.wait_ge(u_out, h + 1)
                if h >= 2:
                    dve.wait_ge(banks.done, banks.number(("i", h - 2, 1, 2)))
                    dve.wait_ge(iu_done, 2 * (h - 2) + 2)
                out = uc[:, h % 2, :]
                tap = lambda k: m.cols[:, C_ODW + K * k + h:C_ODW + K * k + h + 1]
                link(dve.tensor_scalar(out, up[:, 0:UC], tap(0), m.cols[:, C_ODB + h:C_ODB + h + 1], ALU.mult, ALU.add))
                for k in (1, 2):
                    link(dve.scalar_tensor_tensor(out, up[:, k:k + UC], tap(k), out, ALU.mult, ALU.add))
                dve.scalar_tensor_tensor(out, up[:, 3:3 + UC], tap(3), out, ALU.mult, ALU.add).then_inc(conv_done, 1)

            def recur(x):
                h, dr = x // 2, x % 2
                dve.wait_ge(a2_done, x + 1)
                dve.wait_ge(tanh_done, x + 1)
                dve.scalar_tensor_tensor(mu, mu, 1.0, r, ALU.add, ALU.mult).then_inc(m2_done, 1)
                dve.wait_ge(mu_done, x + 1)
                dve.wait_ge(iu_done, x + 1)
                link(dve.tensor_tensor(ig, ig, mu, ALU.mult))
                if dr == 0:
                    link(dve.tensor_tensor_scan(h0[:, SEQ:TOK], a[:, SEQ:TOK], ig[:, SEQ:TOK], 0.0, ALU.mult, ALU.add))
                    dve.tensor_tensor_scan(h0[:, 0:SEQ], a[:, 0:SEQ], ig[:, 0:SEQ], h0[:, TOK - 1:TOK],
                                           ALU.mult, ALU.add).then_inc(scan_done, 1)
                else:
                    dve.tensor_tensor_scan(h1[:, ::-1], a[:, ::-1], ig[:, ::-1], 0.0, ALU.mult, ALU.add).then_inc(scan_done, 1)
                    dve.wait_ge(scan_done, x + 1)
                    link(dve.tensor_tensor(h0[:, 0:SEQ], h0[:, 0:SEQ], h1[:, 0:SEQ], ALU.add))
                    dve.wait_ge(gelu_done, h + 1)
                    link(dve.tensor_tensor(yT[:, h, :], yT[:, h, :], h0[:, 0:SEQ], ALU.mult))

            convolve(0)
            for h in range(K):
                recur(2 * h)
                if h + 1 < K:
                    convolve(h + 1)
                recur(2 * h + 1)


def final_stage(nc, m, d):
    with stage_of(nc) as ctx:
        sq, ms_done, sd_done, rs_done, xn_done, out_done, g_in = semaphores(
            nc, ctx, " ".join(f"f_{x}" for x in "sq ms sd rs xn out g".split()))
        x_in = semaphores(nc, ctx, "f_x0 f_x1")
        stored = semaphores(nc, ctx, "f_o0 f_o1")
        xt = m.A[:, 0:2 * D].rearrange("p (b n) -> p b n", b=2)
        yt = m.A[:, 2 * D:4 * D].rearrange("p (b n) -> p b n", b=2)
        junk, gain = m.A[:, 4 * D:5 * D], m.A[:, 5 * D:6 * D]
        st = m.A[:, 6 * D:6 * D + 8]
        block = ctx.enter_context(nc.Block())

        @block.sync
        def _(sp):
            def load(t, b):
                sp.dma_start(xt[:, b, :], d["x_res"][bass.ds(t * P, P), :]).then_inc(x_in[b], 16)

            def store(t, b):
                sp.wait_ge(out_done, t + 1)
                sp.dma_start(d["out"][bass.ds(t * P, P), :], yt[:, b, :]).then_inc(stored[b], 16)

            load(0, 0)
            load(1, 1)
            sp.dma_start(gain, d["final_g"].to_broadcast((P, D))).then_inc(g_in, 16)
            with sp.Fori(0, LT // 2 - 1) as i:
                for b in range(2):
                    sp.wait_ge(xn_done, i * 2 + (b + 1))
                    load(i * 2 + (b + 2), b)
                    store(i * 2 + b, b)
            for b in range(2):
                store(LT - 2 + b, b)
            for b in range(2):
                sp.wait_ge(stored[b], 16 * LT // 2)

        @block.scalar
        def _(act):
            with act.Fori(0, LT // 2) as i:
                for b in range(2):
                    t = i * 2 + b
                    act.wait_ge(x_in[b], i * 16 + 16)
                    act.activation(junk, xt[:, b, :], ACT.Square, accum_out=st[:, b:b + 1]).then_inc(sq, 1)
                    act.wait_ge(ms_done, t + 1)
                    act.activation(st[:, 4 + b:5 + b], st[:, 2 + b:3 + b], ACT.Sqrt).then_inc(sd_done, 1)

        @block.vector
        def _(dve):
            dve.wait_ge(g_in, 16)

            def tile(i, b):
                t = i * 2 + b
                dve.wait_ge(sq, t + 1)
                dve.tensor_scalar(st[:, 2 + b:3 + b], st[:, b:b + 1], 1.0 / D, EPS, ALU.mult, ALU.add).then_inc(ms_done, 1)
                dve.wait_ge(sd_done, t + 1)
                dve.reciprocal(st[:, 6 + b:7 + b], st[:, 4 + b:5 + b]).then_inc(rs_done, 1)
                dve.wait_ge(rs_done, t + 1)
                if not isinstance(i, int):
                    dve.wait_ge(stored[b], i * 16)
                dve.tensor_scalar(yt[:, b, :], xt[:, b, :], st[:, 6 + b:7 + b], None, ALU.mult).then_inc(xn_done, 1)
                dve.wait_ge(xn_done, t + 1)
                dve.tensor_tensor(yt[:, b, :], yt[:, b, :], gain, ALU.mult).then_inc(out_done, 1)

            for b in range(2):
                tile(0, b)
            with dve.Fori(1, LT // 2) as i:
                for b in range(2):
                    tile(i, b)


def build(nc, d):
    with ExitStack() as ctx:
        m = Memory(nc, ctx)
        affT = m.rope[0:NE, :, :].rearrange("p a n -> p (a n)")[:, 0:TOK]
        chunked = lambda region: region.rearrange("p (k t) -> p k t", k=K)
        stages = [
            (m.plain, lambda: ada_stage(nc, m, d)),
            (m.split, lambda: norm_stage(nc, m, "n0", 0, [(d["x"], 0, LT, 0), (d["ctx"], 0, NT - LT, 1)])),
            (m.split, lambda: even_in_stage(nc, m, d)),
            (m.plain, lambda: attention_stage(nc, m, d)),
            (m.plain, lambda: out_stage(nc, m, d, "o0", 0, chunked(m.B), None,
                                        [(d["x"], LT, 0), (d["ctx"], NT - LT, 1)], affT)),
            (m.plain, lambda: choose_stage(nc, m, "c0", affT, True,
                                           lambda nc, ctx: AdaUnits(nc, ctx, m, d, 1, 4))),
            (m.plain, lambda: expert_stage(nc, m, d, "e0", 0, True)),
            (m.split, lambda: norm_stage(nc, m, "n1", 1, [(d["x_res"], 0, LT, 0), (d["x_res"], SEQ, NT - LT, 1)])),
            (m.split, lambda: odd_mixer_stage(nc, m, d)),
            (m.plain, lambda: out_stage(nc, m, d, "o1", 1, chunked(m.C), d["od_out"],
                                        [(d["x_res"][0:SEQ, :], LT, 0)], affT)),
        ]
        last_stages = [
            (m.for_rows, lambda: choose_stage(nc, m, "c1", affT, False, lambda nc, ctx: FirstPieces(nc, ctx, m, d))),
            (m.for_rows, lambda: expert_rows_stage(nc, m, d, "e1", 1)),
            (m.plain, lambda: final_stage(nc, m, d)),
        ]

        def run(stages, name):
            while stages:
                memory = stages[0][0]
                with memory(nc, f"{name}{len(stages)}"):
                    while stages and stages[0][0] == memory:
                        stages.pop(0)[1]()

        with m.regions(nc, "first"):
            run(stages, "r")
        run(last_stages, "s")


def column_tiles(w):
    n = w.shape[-1] // P
    return w.reshape(K, P, n, P).transpose(2, 1, 0, 3)


def constants():
    f = np.arange(P) % 16
    inv = (10000.0 ** (-np.arange(16, dtype=np.float32) / 16)).astype(np.float32)[f]
    t = np.arange(SEQ)
    pos = np.where(((np.arange(P) % DH) < DH // 2)[:, None], (t // GRID_W)[None, :], (t % GRID_W)[None, :])
    ang = (pos.astype(np.float32) * inv[:, None]).astype(np.float32)
    rope = np.stack([np.cos(ang), np.sin(ang)], axis=1).astype(np.float32)
    rot = np.zeros((P, P), np.float32)
    for i in range(P):
        if i % 32 < 16:
            rot[i + 16, i] = -1.0
        else:
            rot[i - 16, i] = 1.0
    i, j = np.arange(P)[:, None], np.arange(P)[None, :]
    mask = np.zeros((P, 5 * P), np.float32)
    mask[:, 0:P] = np.where(j >= i, 0.0, NEG / DH ** -0.5)
    mask[:, 4 * P:5 * P] = np.where(j <= i, 0.0, NEG / DH ** -0.5)
    return {"rope": rope, "rot": rot, "mask": mask, "ident": np.eye(P, dtype=np.float32)}


def lay_out(x, c, ctx, c_ctx, ada_w, ada_b, norm_mix_g, norm_ffn_g, ev_w_in, ev_w_out, ev_sink, ev_conv_w,
            ev_conv_b, od_w_in, od_w_out, od_conv_w, od_conv_b, od_wa, od_ba, od_wx, od_bx, od_lambda,
            router_w, w_gate, w_up, w_down, final_g):
    col = lambda v: v.reshape(-1, P)
    cond = np.stack([c.reshape(K, P), c_ctx.reshape(K, P)], axis=1)
    cols = np.concatenate([col(v) for v in (cond, norm_mix_g, norm_ffn_g, ev_conv_w, ev_conv_b, od_conv_w,
                                            od_conv_b, od_ba, od_bx, od_lambda)]).T
    pair = lambda w: w.reshape(w.shape[0], NKV, QPK, DH).transpose(0, 2, 1, 3).reshape(w.shape[0], -1)
    w = ev_w_in[0]
    t = column_tiles(np.concatenate([pair(w[:, 0:512]), w[:, 512:]], axis=1))
    order = [0, 1, 2, 3, 4, 5] + [b + c for c in range(CB) for b in (10, 14, 6)]
    ev_in = t[order].reshape(18, P, D)
    wo = ev_w_out[0]
    wo = np.concatenate([pair(wo[0:512].T).T, wo[512:]])
    t = column_tiles(od_w_in[0])
    order = [x for h in range(K) for x in (K + h, h)]
    od_in = t[order].reshape(16, P, D)
    rows = lambda w: w.reshape(K, P, D).transpose(1, 0, 2)
    gates = np.stack([od_wa[0, 0], od_wx[0, 0], od_wa[0, 1], od_wx[0, 1]], axis=2)
    up = lambda w: w.reshape(NE, K, P, FJ, P).transpose(0, 3, 2, 1, 4).reshape(NE * FJ, P, D)
    moe = np.concatenate([up(w_gate[0]), up(w_up[0]), w_down[0].reshape(NE * FJ, P, D)], axis=2)
    U = FF // 4
    up = lambda w: w.reshape(NE, K, P, 4, U).transpose(0, 3, 2, 1, 4).reshape(NE, 4, 1, P, K * U)
    down = w_down[1].reshape(NE, FJ, P, 4, D // 4).transpose(0, 3, 2, 1, 4).reshape(NE, 4, P, K * U)
    moe_rows = np.concatenate([np.concatenate([up(w_gate[1]), up(w_up[1])], axis=2).reshape(NE, 8, P, K * U), down],
                              axis=1).reshape(NE * 12, P, K * U)
    ada = ada_w.reshape(2, K, P, 12, BANK).transpose(0, 3, 2, 1, 4).reshape(24, P, K, BANK)
    router = router_w.reshape(2, K, P, NE).transpose(0, 2, 1, 3)
    return {"x": x[0], "ctx": ctx[0], "cols": cols, "ada_w": ada, "ada_b": ada_b, "ev_in": ev_in,
            "ev_out": rows(wo), "ev_sink": ev_sink, "od_in": od_in, "od_out": rows(od_w_out[0]),
            "od_gates": gates, "router_w": router, "moe": moe, "moe_rows": moe_rows, "final_g": final_g.reshape(1, D), **constants()}


def kernel(**inputs):
    import concourse.bacc as bacc
    from concourse.bass_utils import run_bass_kernel_spmd

    nc = bacc.Bacc("TRN2", target_bir_lowering=False, num_devices=1)
    arrays = {f"in_{k}": np.ascontiguousarray(a) for k, a in lay_out(**{k: np.asarray(v) for k, v in inputs.items()}).items()}
    d = {k[3:]: nc.dram_tensor(k, a.shape, F32, kind="ExternalInput").ap() for k, a in arrays.items()}
    d["out"] = nc.dram_tensor("out", (SEQ, D), F32, kind="ExternalOutput").ap()
    d["x_res"] = nc.dram_tensor("x_res", (TOK, D), F32, kind="Internal").ap()
    d["x_norm"] = nc.dram_tensor("x_norm", (TOK, D), F32, kind="Internal").ap()
    d["mrow"] = nc.dram_tensor("mrow", (2, 12 * D), F32, kind="Internal").ap()
    build(nc, d)
    result = run_bass_kernel_spmd(nc, [arrays], core_ids=[0])
    return result.results[0]["out"].reshape(1, SEQ, D)
```
